# Optimizing a Trainium2 kernel written in Bass

```python
import jax, jax.numpy as jnp
from jax import lax
import numpy as np

D_MODEL = 1024
BATCH = 1
SEQ = 256
DEPTH = 1

HEAD_DIM = 64
ROT_FRACTION = 4
ROPE_THETA = 500000.0
DSA_HEADS = D_MODEL // 2 // HEAD_DIM
DSA_KV_RANK = 128
IDX_HEADS = 8
IDX_DIM = 32
DSA_TOPK_MAX = 256
NSA_HEADS = D_MODEL // 2 // HEAD_DIM
NSA_KV_GROUPS = 2
CMP_LEN = 32
CMP_STRIDE = 16
CMP_HIDDEN = 256
SEL_BLOCK = 64
SEL_COUNT = 16
WINDOW = 512
N_GROUPS = 4
EXPERTS_PER_GROUP = 8
N_EXPERTS = N_GROUPS * EXPERTS_PER_GROUP
EXPERT_TOPK = 2
D_EXPERT = 256
Q_BLOCK = 128
NORM_EPS = 1e-6
NEG_INF = -1e30
TINY = 1e-30
IN_PROJ_COLS = (DSA_HEADS * HEAD_DIM + DSA_KV_RANK + IDX_HEADS * IDX_DIM + IDX_HEADS + IDX_DIM
                + NSA_HEADS * HEAD_DIM + 6 * NSA_KV_GROUPS * HEAD_DIM + 3 * NSA_HEADS + 2 * D_MODEL)

kernel_name = 'hybrid_dsa_nsa_hmoe_block'

def _split_points():
    kvb = NSA_KV_GROUPS * HEAD_DIM
    sizes = [DSA_HEADS * HEAD_DIM, DSA_KV_RANK, IDX_HEADS * IDX_DIM, IDX_HEADS, IDX_DIM,
             NSA_HEADS * HEAD_DIM, kvb, kvb, kvb, kvb, kvb, kvb, 3 * NSA_HEADS, 2 * D_MODEL]
    return [int(v) for v in np.cumsum(sizes)[:-1]]

def rms_norm(x, g):
    xf = x.astype(jnp.float32)
    y = xf * lax.rsqrt(jnp.mean(xf * xf, axis=-1, keepdims=True) + NORM_EPS)
    return (y * g.astype(jnp.float32)).astype(x.dtype)

def partial_rotary(x, positions):
    rot = x.shape[-1] // ROT_FRACTION
    half = rot // 2
    inv_freq = ROPE_THETA ** (-jnp.arange(half, dtype=jnp.float32) / half)
    ang = positions.astype(jnp.float32)[..., None] * inv_freq
    ang = ang.reshape(ang.shape[:2] + (1,) * (x.ndim - 3) + (half,))
    cos = jnp.cos(ang).astype(x.dtype)
    sin = jnp.sin(ang).astype(x.dtype)
    x1, x2, rest = x[..., :half], x[..., half:rot], x[..., rot:]
    return jnp.concatenate([x1 * cos - x2 * sin, x2 * cos + x1 * sin, rest], axis=-1)

def masked_softmax(s, mask):
    s = jnp.where(mask, s.astype(jnp.float32), NEG_INF)
    p = jnp.exp(s - jnp.max(s, axis=-1, keepdims=True))
    p = jnp.where(mask, p, 0.0)
    return p / jnp.maximum(jnp.sum(p, axis=-1, keepdims=True), TINY)

def compress_blocks(k, pe, w1, w2):
    B, S, G, HD = k.shape
    r = CMP_LEN // CMP_STRIDE
    n_chunks = S // CMP_STRIDE
    chunks = k.reshape(B, n_chunks, CMP_STRIDE, G, HD)
    blocks = jnp.concatenate([chunks[:, i:n_chunks - r + 1 + i] for i in range(r)], axis=2)
    blocks = blocks + pe[:, None, :]
    flat = blocks.transpose(0, 1, 3, 2, 4).reshape(B, n_chunks - r + 1, G, CMP_LEN * HD)
    return jax.nn.silu(flat @ w1) @ w2

def token_mixer(h, positions, w_in, g_kv_latent, w_kv_up, pe_cmp_k, pe_cmp_v,
                w_cmp1_k, w_cmp2_k, w_cmp1_v, w_cmp2_v, w_up_a, w_up_b, w_out):
    B, S, _ = h.shape
    G, J, HD = NSA_KV_GROUPS, NSA_HEADS // NSA_KV_GROUPS, HEAD_DIM
    scale = HEAD_DIM ** -0.5
    topk_a = min(DSA_TOPK_MAX, S // 4)
    n_sel = min(SEL_COUNT, S // SEL_BLOCK)

    (q_a, kv_lat, iq, iw, ik, q_b, kc, vc, ks, vs, kw, vw, br_gate, mg) = jnp.split(
        h @ w_in, _split_points(), axis=-1)

    q_a = partial_rotary(q_a.reshape(B, S, DSA_HEADS, HD), positions)
    kv = rms_norm(kv_lat, g_kv_latent) @ w_kv_up
    k_a = partial_rotary(kv[..., :DSA_HEADS * HD].reshape(B, S, DSA_HEADS, HD), positions)
    v_a = kv[..., DSA_HEADS * HD:].reshape(B, S, DSA_HEADS, HD)
    iq = partial_rotary(iq.reshape(B, S, IDX_HEADS, IDX_DIM), positions)
    ik = partial_rotary(ik.reshape(B, S, 1, IDX_DIM), positions)[:, :, 0]

    q_b = partial_rotary(q_b.reshape(B, S, G, J, HD), positions)
    to_g = lambda t: t.reshape(B, S, G, HD)
    kc = compress_blocks(partial_rotary(to_g(kc), positions), pe_cmp_k, w_cmp1_k, w_cmp2_k)
    vc = compress_blocks(to_g(vc), pe_cmp_v, w_cmp1_v, w_cmp2_v)
    n_cmp = kc.shape[1]
    n_blk = S // SEL_BLOCK
    to_blocks = lambda t: t.reshape(B, n_blk, SEL_BLOCK, G, HD).transpose(0, 3, 1, 2, 4)
    ks_blocks = to_blocks(partial_rotary(to_g(ks), positions))
    vs_blocks = to_blocks(to_g(vs))
    pad = ((0, 0), (WINDOW, 0), (0, 0), (0, 0))
    kw_pad = jnp.pad(partial_rotary(to_g(kw), positions), pad)
    vw_pad = jnp.pad(to_g(vw), pad)
    br_gate = jax.nn.sigmoid(br_gate).reshape(B, S, G, J, 3)
    g_a, g_b = jnp.split(jax.nn.sigmoid(mg), 2, axis=-1)

    cmp_end = jnp.arange(n_cmp) * CMP_STRIDE + CMP_LEN - 1
    cmp_start = jnp.arange(n_cmp)[:, None] * CMP_STRIDE
    blk_start = jnp.arange(n_blk)[None, :] * SEL_BLOCK
    overlap = ((cmp_start <= blk_start + SEL_BLOCK - 1)
               & (cmp_start + CMP_LEN - 1 >= blk_start)).astype(jnp.float32)
    key_idx = jnp.arange(S)
    blk_ids = jnp.arange(n_blk)
    gather_rows = jax.vmap(lambda arr, idx: arr[idx])
    gather_blocks = jax.vmap(jax.vmap(lambda arr, idx: arr[idx]))

    def attend_block(q0):
        t = q0 + jnp.arange(Q_BLOCK)
        sl = lambda a: lax.dynamic_slice_in_dim(a, q0, Q_BLOCK, axis=1)
        logits = jnp.einsum('bqhd,bsd->bqhs', sl(iq), ik)
        idx_score = jnp.einsum('bqhs,bqh->bqs', jax.nn.relu(logits), sl(iw)).astype(jnp.float32)
        idx_score = jnp.where(key_idx[None, None, :] <= t[None, :, None], idx_score, NEG_INF)
        _, sel = lax.top_k(idx_score, topk_a)
        kg = gather_rows(k_a, sel)
        vg = gather_rows(v_a, sel)
        s_a = jnp.einsum('bqhd,bqkhd->bhqk', sl(q_a), kg) * scale
        p_a = masked_softmax(s_a, (sel <= t[None, :, None])[:, None])
        o_a = jnp.einsum('bhqk,bqkhd->bqhd', p_a.astype(vg.dtype), vg)

        qb = sl(q_b)
        s_c = jnp.einsum('bqgjd,bcgd->bgjqc', qb, kc) * scale
        p_c = masked_softmax(s_c, cmp_end[None, :] <= t[:, None])
        o_c = jnp.einsum('bgjqc,bcgd->bqgjd', p_c.astype(vc.dtype), vc)
        imp = jnp.einsum('bgjqc,cn->bgqn', p_c, overlap)
        cur = (t // SEL_BLOCK)[:, None]
        admissible = blk_ids[None, :] * SEL_BLOCK <= t[:, None]
        forced = (blk_ids[None, :] == 0) | (blk_ids[None, :] == cur) | (blk_ids[None, :] == cur - 1)
        sel_score = jnp.where(admissible & forced, -NEG_INF, jnp.where(admissible, imp, NEG_INF))
        _, bsel = lax.top_k(sel_score, n_sel)
        flat = bsel.reshape(B, G, Q_BLOCK * n_sel)
        ksg = gather_blocks(ks_blocks, flat).reshape(B, G, Q_BLOCK, n_sel * SEL_BLOCK, HD)
        vsg = gather_blocks(vs_blocks, flat).reshape(B, G, Q_BLOCK, n_sel * SEL_BLOCK, HD)
        tok = bsel[..., None] * SEL_BLOCK + jnp.arange(SEL_BLOCK)
        smask = (tok <= t[None, None, :, None, None]).reshape(B, G, 1, Q_BLOCK, n_sel * SEL_BLOCK)
        s_s = jnp.einsum('bqgjd,bgqmd->bgjqm', qb, ksg) * scale
        p_s = masked_softmax(s_s, smask)
        o_s = jnp.einsum('bgjqm,bgqmd->bqgjd', p_s.astype(vsg.dtype), vsg)
        kwb = lax.dynamic_slice_in_dim(kw_pad, q0, WINDOW + Q_BLOCK, axis=1)
        vwb = lax.dynamic_slice_in_dim(vw_pad, q0, WINDOW + Q_BLOCK, axis=1)
        spos = q0 - WINDOW + jnp.arange(WINDOW + Q_BLOCK)
        wmask = ((spos[None, :] <= t[:, None]) & (spos[None, :] > t[:, None] - WINDOW)
                 & (spos[None, :] >= 0))
        s_w = jnp.einsum('bqgjd,bkgd->bgjqk', qb, kwb) * scale
        p_w = masked_softmax(s_w, wmask)
        o_w = jnp.einsum('bgjqk,bkgd->bqgjd', p_w.astype(vwb.dtype), vwb)
        gb = sl(br_gate)
        o_b = gb[..., 0:1] * o_c + gb[..., 1:2] * o_s + gb[..., 2:3] * o_w
        return o_a, o_b

    o_a, o_b = lax.map(attend_block, jnp.arange(S // Q_BLOCK, dtype=jnp.int32) * Q_BLOCK)
    o_a = jnp.moveaxis(o_a, 0, 1).reshape(B, S, DSA_HEADS * HD)
    o_b = jnp.moveaxis(o_b, 0, 1).reshape(B, S, NSA_HEADS * HD)
    merged = g_a * (o_a @ w_up_a) + g_b * (o_b @ w_up_b)
    return merged @ w_out

def hier_moe(h, w_router_group, b_router_group, w_router_expert, b_router_expert,
             w_expert_gate, w_expert_up, w_expert_down):
    B, S, D = h.shape
    hf = h.reshape(B * S, D)
    lg = (hf @ w_router_group + b_router_group).astype(jnp.float32)
    pg = jax.nn.softmax(lg, axis=-1)
    gsel = jnp.argmax(lg, axis=-1)
    le = (hf @ w_router_expert + b_router_expert).astype(jnp.float32)
    le = le.reshape(B * S, N_GROUPS, EXPERTS_PER_GROUP)
    le_g = jnp.take_along_axis(le, gsel[:, None, None], axis=1)[:, 0]
    top_p, top_i = lax.top_k(jax.nn.softmax(le_g, axis=-1), EXPERT_TOPK)
    pg_sel = jnp.take_along_axis(pg, gsel[:, None], axis=1)
    wts = top_p / jnp.sum(top_p, axis=-1, keepdims=True) * pg_sel
    eidx = gsel[:, None] * EXPERTS_PER_GROUP + top_i
    comb = jnp.sum(jax.nn.one_hot(eidx, N_EXPERTS, dtype=jnp.float32) * wts[..., None], axis=1)
    comb = comb.astype(hf.dtype)
    out = jnp.zeros_like(hf)
    for e in range(N_EXPERTS):
        ye = (jax.nn.silu(hf @ w_expert_gate[e]) * (hf @ w_expert_up[e])) @ w_expert_down[e]
        out = out + comb[:, e:e + 1] * ye
    return out.reshape(B, S, D)

def setup_inputs(seed: int = 0) -> dict:
    key = jax.random.key(seed)
    k = jax.random.split(key, 28)
    f32 = jnp.float32
    L = DEPTH
    HD = HEAD_DIM

    def dense(kk, shape, fan_in, gain=1.0):
        return jax.random.normal(kk, shape, f32) * (gain * fan_in ** -0.5)

    def norm_gain(kk, shape):
        return 1.0 + 0.02 * jax.random.normal(kk, shape, f32)

    def small(kk, shape, s):
        return s * jax.random.normal(kk, shape, f32)

    return {
        'x': jax.random.normal(k[0], (BATCH, SEQ, D_MODEL), f32),
        'c': jax.random.normal(k[1], (BATCH, D_MODEL), f32),
        'positions': jnp.broadcast_to(jnp.arange(SEQ, dtype=jnp.int32)[None, :], (BATCH, SEQ)),
        'w_ada': dense(k[2], (L, D_MODEL, 6 * D_MODEL), D_MODEL, 0.5),
        'b_ada': small(k[3], (L, 6 * D_MODEL), 0.02),
        'g_norm1': norm_gain(k[4], (L, D_MODEL)),
        'w_in': dense(k[5], (L, D_MODEL, IN_PROJ_COLS), D_MODEL),
        'g_kv_latent': norm_gain(k[6], (L, DSA_KV_RANK)),
        'w_kv_up': dense(k[7], (L, DSA_KV_RANK, 2 * DSA_HEADS * HD), DSA_KV_RANK),
        'pe_cmp_k': small(k[8], (L, CMP_LEN, HD), 0.02),
        'pe_cmp_v': small(k[9], (L, CMP_LEN, HD), 0.02),
        'w_cmp1_k': dense(k[10], (L, CMP_LEN * HD, CMP_HIDDEN), CMP_LEN * HD),
        'w_cmp2_k': dense(k[11], (L, CMP_HIDDEN, HD), CMP_HIDDEN),
        'w_cmp1_v': dense(k[12], (L, CMP_LEN * HD, CMP_HIDDEN), CMP_LEN * HD),
        'w_cmp2_v': dense(k[13], (L, CMP_HIDDEN, HD), CMP_HIDDEN),
        'w_up_a': dense(k[14], (L, DSA_HEADS * HD, D_MODEL), DSA_HEADS * HD),
        'w_up_b': dense(k[15], (L, NSA_HEADS * HD, D_MODEL), NSA_HEADS * HD),
        'w_out': dense(k[16], (L, D_MODEL, D_MODEL), D_MODEL),
        'g_norm2': norm_gain(k[17], (L, D_MODEL)),
        'w_router_group': dense(k[18], (L, D_MODEL, N_GROUPS), D_MODEL),
        'b_router_group': small(k[19], (L, N_GROUPS), 0.01),
        'w_router_expert': dense(k[20], (L, D_MODEL, N_EXPERTS), D_MODEL),
        'b_router_expert': small(k[21], (L, N_EXPERTS), 0.01),
        'w_expert_gate': dense(k[22], (L, N_EXPERTS, D_MODEL, D_EXPERT), D_MODEL),
        'w_expert_up': dense(k[23], (L, N_EXPERTS, D_MODEL, D_EXPERT), D_MODEL),
        'w_expert_down': dense(k[24], (L, N_EXPERTS, D_EXPERT, D_MODEL), D_EXPERT),
        'g_final': norm_gain(k[25], (D_MODEL,)),
    }

def reference(x, c, positions, w_ada, b_ada, g_norm1, w_in, g_kv_latent, w_kv_up,
              pe_cmp_k, pe_cmp_v, w_cmp1_k, w_cmp2_k, w_cmp1_v, w_cmp2_v,
              w_up_a, w_up_b, w_out, g_norm2, w_router_group, b_router_group,
              w_router_expert, b_router_expert, w_expert_gate, w_expert_up,
              w_expert_down, g_final):
    cond = jax.nn.silu(c)
    for l in range(DEPTH):
        mod = cond @ w_ada[l] + b_ada[l]
        sh1, sc1, gt1, sh2, sc2, gt2 = jnp.split(mod[:, None, :], 6, axis=-1)
        h = rms_norm(x, g_norm1[l]) * (1.0 + sc1) + sh1
        x = x + gt1 * token_mixer(h, positions, w_in[l], g_kv_latent[l], w_kv_up[l],
                                  pe_cmp_k[l], pe_cmp_v[l], w_cmp1_k[l], w_cmp2_k[l],
                                  w_cmp1_v[l], w_cmp2_v[l], w_up_a[l], w_up_b[l], w_out[l])
        h = rms_norm(x, g_norm2[l]) * (1.0 + sc2) + sh2
        x = x + gt2 * hier_moe(h, w_router_group[l], b_router_group[l], w_router_expert[l],
                               b_router_expert[l], w_expert_gate[l], w_expert_up[l],
                               w_expert_down[l])
    return rms_norm(x, g_final)


_drawn_inputs = setup_inputs


def setup_inputs(seed=0):
    import zlib

    import numpy as np

    out = dict(_drawn_inputs(seed))
    spreads = {}
    factors = {'b_ada': 3.457,
     'g_norm1': 8.0,
     'g_kv_latent': 8.0,
     'pe_cmp_k': 8.0,
     'pe_cmp_v': 33.027,
     'w_cmp1_k': 3.811,
     'w_cmp2_k': 3.646,
     'g_norm2': 5.728,
     'b_router_group': 8.0,
     'b_router_expert': 27.465,
     'g_final': 21.96}
    for name, (base, spread) in spreads.items():
        noise = np.random.default_rng([zlib.crc32(name.encode()), seed]).standard_normal(out[name].shape)
        drawn = base * np.exp(spread * noise) if base else spread * noise
        out[name] = __import__('jax').numpy.asarray(drawn.astype(out[name].dtype))
    for name, factor in factors.items():
        out[name] = (out[name] * factor).astype(out[name].dtype)
    return out
```

```python
from contextlib import ExitStack

import numpy as np

import concourse.bass as bass
from concourse import mybir

F32 = mybir.dt.float32
F32R = mybir.dt.float32r
I32 = mybir.dt.int32
ALU = mybir.AluOpType
ACT = mybir.ActivationFunctionType
AX = mybir.AxisListType.X

P = 128
D = 1024
S = 256
KD = D // P
M = S // P
HD = 64
HEADS = 8
PAIRS = HEADS // 2
ROT = HD // 4
RANK = 128
IDX_HEADS, IDX_DIM = 8, 32
IDX_ROT = IDX_DIM // 4
TOPK = S // 4
GROUPS = 2
CMP_LEN, CMP_STRIDE, CMP_HIDDEN = 32, 16, 256
NCMP = S // CMP_STRIDE - CMP_LEN // CMP_STRIDE + 1
CMP_TILES = CMP_LEN * HD // P
EXPERTS, EXPERT_GROUPS = 32, 4
PER_GROUP = EXPERTS // EXPERT_GROUPS
FF = 256
THETA = 500000.0
EPS = 1e-6
NEG = -1e30
TINY = 1e-30
SCALE = HD ** -0.5

QA = 0
KV = QA + HEADS * HD
IQ = KV + RANK
IW = IQ + IDX_HEADS * IDX_DIM
IK = IW + IDX_HEADS
QB = IK + IDX_DIM
KC = QB + HEADS * HD
VC, KS, VS, KW, VW = (KC + n * GROUPS * HD for n in range(1, 6))
BR = VW + GROUPS * HD
MG = BR + 3 * HEADS
WIN_COLS = MG + 2 * D

CH = 256
WINC = [(c, min(c + CH, MG)) for c in range(0, MG, CH)]
RING = 9
SLOTS = 64
ROUNDS = S // SLOTS
MRING = 12
PIECES = 3

R_C, R_BADA, R_G1, R_G2, R_GKV, R_PEK, R_PEV, R_END = 0, 8, 56, 64, 72, 73, 89, 105

UNITS = [("sel", 0), ("win", 0), ("sel", 1), ("win", 1), ("dsa", 0), ("dsa", 1)]


def product_order():
    act, dve = "act", "dve"

    def score(kind, m):
        return [(f"S{kind}{m}_{n}", dve) for n in range(2 * (m + 1))]

    def turn(kind, m):
        return [(f"T{kind}{m}_{n}", act) for n in range(2 * (m + 1))]

    def mg(n):
        return [(f"mg{n}", act)]

    o = [("rows", dve), ("ada0", dve), ("ada1", dve)]
    o += [(f"xT{n}", dve) for n in range(4)]
    o += [(f"win{n}", act) for n in range(len(WINC))]
    o += mg(0) + [("kvT", dve)] + mg(1) + [(f"kvp{n}", act) for n in range(4)]
    o += [("iqT", act), ("ikT", act), ("cmpx", act), ("qbT0", act), ("qbT1", act), ("ksT", act), ("kwT", act)]
    o += mg(2) + [(f"il{n}", act) for n in range(8)]
    o += [("cmp1k", dve), ("cmp1v", dve)] + mg(3) + [("cmp2", dve), ("sc0", dve), ("sc1", dve)]
    o += score("sel", 0) + score("win", 0) + mg(4)
    o += [(f"pcT{n}", act) for n in range(4)]
    o += [("qaT0", act), ("qaT1", act), ("kaT0", act), ("kaT1", act)]
    o += turn("sel", 0) + score("sel", 1) + mg(5) + turn("win", 0) + score("win", 1) + mg(6)
    o += [("PVb0", act)] + turn("sel", 1) + score("dsa", 0) + mg(7) + turn("win", 1) + [("PVb1", act)]
    o += score("dsa", 1) + [("ada2", dve)] + turn("dsa", 0) + [("PVa0", act), ("ada3", dve)]
    o += turn("dsa", 1) + [("PVa1", act), ("ada4", dve), ("ada5", dve), ("gb0", act), ("gb1", act)]
    o += [(f"up{n}", dve) for n in range(KD)] + [(f"out{n}", dve) for n in range(4)]
    o += [("gb2", act), ("gb3", act)] + [(f"x1T{n}", dve) for n in range(4)] + [("rt", dve), ("pos", dve)]
    return o


ORDER = product_order()
INDEX = {name: n for n, (name, _) in enumerate(ORDER)}


def chunk_order():
    o = []
    for name, _ in ORDER:
        if name[:3] == "ada":
            o += [(name, "ada", 4 * int(name[3:]) + j) for j in range(4)]
        elif name[:3] == "win":
            o.append((name, "win", int(name[3:])))
        elif name[:2] == "mg":
            o.append((name, "mg", int(name[2:])))
        elif name in ("cmp1k", "cmp1v"):
            o += [(name, name, j) for j in range(2)]
        elif name in ("up0", "up4"):
            n = int(name[2:])
            o += [(f"up{n + 3}", "upa", n // 4), (f"up{n + 3}", "upb", n // 4)]
        elif name[:3] == "out":
            o.append((name, "out", int(name[3:])))
    return o


CHUNKS = chunk_order()
CHUNK_AT = {(kind, n): at for at, (_, kind, n) in enumerate(CHUNKS)}


def layer_kernel(nc, x, c, positions, w_ada, b_ada, g_norm1, w_in, g_kv_latent, w_kv_up, pe_cmp_k,
                 pe_cmp_v, w_cmp1_k, w_cmp2_k, w_cmp1_v, w_cmp2_v, w_up_a, w_up_b, w_out, g_norm2,
                 w_router_group, b_router_group, w_router_expert, b_router_expert, w_expert_gate,
                 w_expert_up, w_expert_down, g_final, out):
    base = (nc.sbuf_base + 63) // 64 * 64
    top = nc.sbuf_usable_end

    class Map:

        def __init__(self, at):
            self.at = at

        def __call__(self, name, shape, dt=F32):
            size = int(np.prod(shape[1:])) * 4
            t = place(name, shape, dt, self.at)
            self.at += (size + 31) // 32 * 32
            assert self.at <= top, (name, self.at, top)
            return t

    def place(name, shape, dt, at):
        return nc.alloc_sbuf_tensor_at(name, shape, dt, offset=at)

    keep = Map(base)
    ring = keep("ring", [P, RING, KD * CH])
    ident = keep("ident", [P, P])
    ones = keep("ones", [P, P])
    tri = keep("tri", [P, P])
    iota_slot = keep("iota_slot", [P, SLOTS])
    iota8 = keep("iota8", [P, 8])
    cols = keep("cols", [P, R_END])
    modT = keep("modT", [P, 48])
    A1 = keep("A1", [P, KD])
    A2 = keep("A2", [P, KD])
    condT = keep("condT", [P, KD])
    tiny = keep("tiny", [P, 64])
    wr = keep("wr", [P, KD, 36])
    brow = keep("brow", [P, 36])
    x1_at = keep.at
    x1 = keep("x1", [P, M, D])

    a = Map(keep.at)
    hT = place("hT", [P, KD, S], F32, x1_at)
    xs = a("xs", [P, M, D])
    kvx = place("kvx", [P, M, D], F32, a.at - 8192)
    xp = a("xp", [P, M, MG])
    gT = a("gT", [P, 2 * KD, S])
    qaT = a("qaT", [P, PAIRS, S])
    kaT = a("kaT", [P, PAIRS, S])
    qbT = a("qbT", [P, PAIRS, S])
    ksT = a("ksT", [P, GROUPS, S])
    kwT = a("kwT", [P, GROUPS, S])
    iqT = a("iqT", [P, 2, S])
    ikT = a("ikT", [P, S])
    probs_at = [a.at, a.at + 8192]
    probs = [a("probs0", [P, HEADS, S]), a("probs1", [P, HEADS, S])]
    pT_at = [a.at, a.at + 8192]
    pT = [a("pT0", [P, 2 * HEADS, P]), a("pT1", [P, 2 * HEADS, P])]
    oaT = a("oaT", [P, PAIRS, S])
    obT = a("obT", [P, PAIRS, S])
    cbias = a("cbias", [P, M, S])
    abias = a("abias", [P, M, S])
    pcT = a("pcT", [P, M * HEADS, P])
    smc = a("smc", [P, M, HEADS, NCMP])
    kcT = a("kcT", [P, GROUPS * NCMP])
    vcs = a("vcs", [P, GROUPS, HD])
    w2 = a("w2", [P, 2, 2, HD])
    cbc = a("cbc", [P, M, NCMP])
    cmk = a("cmk", [P, M, NCMP])
    trig = a("trig", [P, 12, M * 8])
    c16 = a("c16", [P, 2, M, ROT])
    c8 = a("c8", [P, 2, M, IDX_ROT])
    posi = a("posi", [P, M], I32)
    gates = a("gates", [P, M, 3 * HEADS])
    stats = a("stats", [P, 12, HEADS])
    w_kv = place("w_kv", [P, 2 * HEADS * HD], F32, probs_at[1])
    junk = place("junk", [P, D], F32, probs_at[0])
    rows = place("rows", [P, P], F32, pT_at[0] + 4096)
    relu = [place(f"relu{m}", [P, HEADS, S], F32, probs_at[m]) for m in range(M)]
    cx = place("cx", [P, 2, GROUPS, P], F32, pT_at[0])
    flat = place("flat", [P, 2, CMP_TILES, GROUPS * NCMP], F32, pT_at[0] + 4096)
    kdup = place("kdup", [P, M, 5, P], F32, pT_at[1])
    hid = place("hid", [P, 2, 2, GROUPS * NCMP], F32, pT_at[1] + 5120)
    hth = place("hth", [P, 2, 2, GROUPS * NCMP], F32, pT_at[1] + 5120 + 1024)
    iscore = place("iscore", [P, M, S], F32, pT_at[0])
    iwork = place("iwork", [P, M, S], F32, pT_at[0] + 2048)
    ropeA = a("ropeA", [P, M, 10, ROT])
    ropeB = a("ropeB", [P, M, 10, ROT])
    kvn = place("kvn", [P, M, RANK], F32, pT_at[1] + 7168)
    kvnT = place("kvnT", [P, S], F32, probs_at[0] + 4096)
    xr = place("xr", [P, M, D], F32, probs_at[0])
    mT = place("mT", [P, KD, S], F32, probs_at[1])
    gt1bc = place("gt1bc", [P, D], F32, pT_at[0])
    diag = place("diag", [P, D], F32, pT_at[0] + 4096)
    tmp_up = place("tmp_up", [P, 2, S], F32, pT_at[1])

    e = Map(keep.at)
    extra = e("extra", [P, MRING - RING, KD * CH])
    h2T = e("h2T", [P, KD, S])
    x1n = e("x1n", [P, M, D])
    x1hi = e("x1hi", [P, M, D], F32R)
    x1lo = e("x1lo", [P, M, D], F32R)
    acc = e("acc", [P, M, D])
    gt2bc = e("gt2bc", [P, D])
    gfbc = e("gfbc", [P, D])
    diag2 = e("diag2", [P, D])
    xgT = [e(f"xgT{n}", [P, KD, 2 * SLOTS]) for n in range(2)]
    pick = [e(f"pick{n}", [P, M, 2 * SLOTS], F32R) for n in range(2)]
    pickw = [e(f"pickw{n}", [P, M, 2 * SLOTS]) for n in range(2)]
    putT = e("putT", [P, M * P], F32R)
    yw = e("yw", [P, 1])
    thg = [e(f"thg{n}", [P, 2 * SLOTS]) for n in range(2)]
    sig = [e(f"sig{n}", [P, 2 * SLOTS]) for n in range(2)]
    aT = [e(f"aT{n}", [P, 2, SLOTS]) for n in range(2)]
    yhi = e("yhi", [P, D], F32R)
    ylo = e("ylo", [P, D], F32R)
    route = e("route", [P, M, 36])
    r4 = e("r4", [P, 6, M, EXPERT_GROUPS])
    r8 = e("r8", [P, 12, M, PER_GROUP])
    r32 = e("r32", [P, M, EXPERT_GROUPS, PER_GROUP])
    r1 = e("r1", [P, 20, M])
    NCOL = EXPERTS + 2
    comb = e("comb", [P, M, NCOL])
    sel = e("sel", [P, M, NCOL])
    slot = e("slot", [P, M, NCOL])
    most = e("most", [P, 1])
    mosti = e("mosti", [P, 1], I32)

    with ExitStack() as ctx:
        bank = [ctx.enter_context(nc.psum_tensor(f"bank{n}", [P, 512], F32)) for n in range(8)]

        def sem(name):
            return ctx.enter_context(nc.semaphore(name))

        x_in = sem("x_in")
        rows_in = sem("rows_in")
        pos_in = sem("pos_in")
        kv_w_in = sem("kv_w_in")
        cmp_w_in = sem("cmp_w_in")
        router_in = sem("router_in")
        x_again = sem("x_again")
        gf_in = sem("gf_in")
        landed = [sem(f"landed{n}") for n in range(RING)]
        consts = sem("consts")
        product_done = sem("product_done")
        act_drained = sem("act_drained")
        dve_drained = sem("dve_drained")
        act_step = sem("act_step")
        dve_step = sem("dve_step")
        tanh_c = sem("tanh_c")
        cond_ready = sem("cond_ready")
        squares = sem("squares")
        recip_ms = sem("recip_ms")
        rms_ready = sem("rms_ready")
        xn_ready = sem("xn_ready")
        angles = sem("angles")
        trig_ready = sem("trig_ready")
        tanh_br = sem("tanh_br")
        kvn_ready = sem("kvn_ready")
        roped = sem("roped")
        flat_ready = sem("flat_ready")
        tanh_hid = sem("tanh_hid")
        hid_ready = sem("hid_ready")
        cmp_shift = sem("cmp_shift")
        cmp_exp = sem("cmp_exp")
        cmp_probs = sem("cmp_probs")
        unit_max = sem("unit_max")
        unit_exp = sem("unit_exp")
        unit_probs = sem("unit_probs")
        diag_ready = sem("diag_ready")
        gates_ready = sem("gates_ready")
        x1n_ready = sem("x1n_ready")
        hi_ready = sem("hi_ready")
        lo_ready = sem("lo_ready")
        rt_shift = sem("rt_shift")
        rt_exp = sem("rt_exp")
        sel_ready = sem("sel_ready")
        most_ready = sem("most_ready")
        mlanded = [sem(f"mlanded{n}") for n in range(MRING)]
        pick_ready = sem("pick_ready")
        xg_done = sem("xg_done")
        xgT_act = sem("xgT_act")
        xgT_dve = sem("xgT_dve")
        gu_done = sem("gu_done")
        tanh_g = sem("tanh_g")
        aT_ready = sem("aT_ready")
        put_done = sem("put_done")
        put_ready = sem("put_ready")
        down_done = sem("down_done")
        yhi_ready = sem("yhi_ready")
        ylo_ready = sem("ylo_ready")
        sc_done = sem("sc_done")
        sc_drained = sem("sc_drained")
        silu_step = sem("silu_step")
        mo_step = sem("mo_step")
        result = sem("result")
        stored = sem("stored")

        NCONST = 9

        def drains_until(name, engine):
            return sum(1 for _, who in ORDER[:INDEX[name] + 1] if who == engine)

        def made(eng, name):
            eng.wait_ge(product_done, INDEX[name] + 1)

        def drained(eng, name):
            who = ORDER[INDEX[name]][1]
            eng.wait_ge(act_drained if who == "act" else dve_drained, drains_until(name, who))

        def bank_of(name):
            return bank[INDEX[name] % 8]

        class Steps:

            def __init__(self, eng, s):
                self.eng, self.s, self.n = eng, s, 0

            def do(self, ins):
                ins.then_inc(self.s, 1)
                self.n += 1

            def settle(self):
                self.eng.wait_ge(self.s, self.n)

        def chunk(kind, n):
            return ring[:, CHUNK_AT[kind, n] % RING, :]

        def arrived(eng, kind, n):
            at = CHUNK_AT[kind, n]
            eng.wait_ge(landed[at % RING], 16 * (at // RING + 1))

        def chunk_source(kind, n):
            if kind == "ada":
                return w_ada[:, n * CH:(n + 1) * CH].rearrange("(k p) n -> p k n", p=P)
            if kind == "win":
                lo, hi = WINC[n]
                return w_in[:, lo:hi].rearrange("(k p) n -> p k n", p=P)
            if kind == "mg":
                return w_in[:, MG + n * CH:MG + (n + 1) * CH].rearrange("(k p) n -> p k n", p=P)
            if kind in ("cmp1k", "cmp1v"):
                w = w_cmp1_k if kind == "cmp1k" else w_cmp1_v
                return w[n * D:(n + 1) * D, :].rearrange("(k p) n -> p k n", p=P)
            if kind in ("upa", "upb"):
                w = w_up_a if kind == "upa" else w_up_b
                return w[:, n * 512:(n + 1) * 512].rearrange("(k p) n -> p k n", p=P)
            return w_out[:, n * CH:(n + 1) * CH].rearrange("(k p) n -> p k n", p=P)

        def head_slot(h):
            return (h % 2) * PAIRS + h // 2

        def mslot(n):
            return ring[:, (len(CHUNKS) + n) % RING, :] if n < RING else extra[:, n - RING, :]

        with nc.Block() as block:

            @block.sync
            def _(sp):
                sp.dma_start(xs[:, :, :], x[0].rearrange("(m p) d -> p m d", p=P)).then_inc(x_in, 16)
                for at, (_, kind, n) in enumerate(CHUNKS):
                    if kind == "upa" and n == 0:
                        made(sp, "Tdsa0_1")
                        sp.dma_start(xr[:, :, :], x[0].rearrange("(m p) d -> p m d", p=P)).then_inc(x_again, 16)
                    if at >= RING:
                        made(sp, CHUNKS[at - RING][0])
                    src = chunk_source(kind, n)
                    dst = chunk(kind, n)[:, 0:src.shape[1] * src.shape[2]]
                    sp.dma_start(dst.rearrange("p (k n) -> p k n", k=src.shape[1]), src).then_inc(landed[at % RING], 16)

                def expert(i, j, pieces_free):
                    for q in range(PIECES):
                        n = PIECES * j + q
                        pieces_free(q, n)
                        if q < 2:
                            w = w_expert_gate if q == 0 else w_expert_up
                            src = w[bass.ds(i, 1)].rearrange("o (k p) n -> p (o k) n", p=P)
                            dst = mslot(n).rearrange("p (k n) -> p k n", k=KD)
                        else:
                            src = w_expert_down[bass.ds(i, 1)].rearrange("o (k p) n -> p (o k) n", p=P)
                            dst = mslot(n).rearrange("p (k n) -> p k n", k=2)
                        sp.dma_start(dst, src).then_inc(mlanded[n], 16)

                def first_free(q, n):
                    if n < RING:
                        made(sp, CHUNKS[len(CHUNKS) - RING + n][0])
                    elif n == RING:
                        drained(sp, "out3")

                for j in range(4):
                    expert(j, j, first_free)

                def stream(r, first):
                    with sp.Fori(first, EXPERTS // 4) as it:
                        for j in range(4):
                            done = (r * EXPERTS + it * 4 + j) - 3

                            def free(q, n):
                                if q == 0:
                                    sp.wait_ge(gu_done, done)
                                elif q == 2:
                                    sp.wait_ge(down_done, done)
                            expert(it * 4 + j, j, free)

                stream(0, 1)
                sp.wait_ge(most_ready, 1)
                count = sp.value_load(mosti[0:1, 0:1], min_val=0, max_val=S)
                with sp.Fori(1, ROUNDS) as r:
                    with sp.If(count > r * SLOTS):
                        stream(r, 0)

            @block.gpsimd
            def _(g):
                g.memset(ident[:, :], 0.0).then_inc(consts, 1)
                g.memset(ones[:, :], 1.0).then_inc(consts, 1)
                g.memset(tri[:, :], 1.0).then_inc(consts, 1)
                g.memset(cbias[:, :, :], 0.0).then_inc(consts, 1)
                g.memset(cbc[:, :, :], 0.0).then_inc(consts, 1)
                g.memset(cmk[:, :, :], 1.0).then_inc(consts, 1)
                g.iota(iota_slot[:, :], [[1, SLOTS]], base=0, channel_multiplier=0,
                       allow_small_or_imprecise_dtypes=True).then_inc(consts, 1)
                g.iota(iota8[:, :], [[1, 8]], base=0, channel_multiplier=0,
                       allow_small_or_imprecise_dtypes=True).then_inc(consts, 1)
                g.wait_ge(consts, 8)
                g.affine_select(out=ident[:, :], in_=ident[:, :], compare_op=ALU.not_equal, fill=1.0, base=0,
                                pattern=[[-1, P]], channel_multiplier=1).then_inc(consts, 1)
                g.affine_select(out=tri[:, :], in_=tri[:, :], compare_op=ALU.is_gt, fill=0.0, base=0,
                                pattern=[[1, P]], channel_multiplier=-1).then_inc(consts, 1)
                g.affine_select(out=cbias[:, :, :], in_=cbias[:, :, :], compare_op=ALU.is_ge, fill=NEG, base=0,
                                pattern=[[P, M], [-1, S]], channel_multiplier=1).then_inc(consts, 1)
                for t, fill in ((cbc, NEG), (cmk, 0.0)):
                    g.affine_select(out=t[:, :, :], in_=t[:, :, :], compare_op=ALU.is_ge, fill=fill,
                                    base=-(CMP_LEN - 1), pattern=[[P, M], [-CMP_STRIDE, NCMP]],
                                    channel_multiplier=1).then_inc(consts, 1)

            ALL_CONSTS = 8 + 5

            @block.scalar
            def _(act):
                step = Steps(act, act_step)
                for lo, src in ((R_C, c.rearrange("a (k p) -> (a k) p", p=P)),
                                (R_BADA, b_ada.rearrange("a (k p) -> (a k) p", p=P)),
                                (R_G1, g_norm1.rearrange("a (k p) -> (a k) p", p=P)),
                                (R_G2, g_norm2.rearrange("a (k p) -> (a k) p", p=P)),
                                (R_GKV, g_kv_latent),
                                (R_PEK, pe_cmp_k[0].rearrange("(j e) d -> j (e d)", e=2)),
                                (R_PEV, pe_cmp_v[0].rearrange("(j e) d -> j (e d)", e=2))):
                    act.dma_start(rows[lo:lo + src.shape[0], :], src).then_inc(rows_in, 16)
                act.dma_start(posi[:, :], positions[0].rearrange("(m p) -> p m", p=P), allow_slow_non_contiguous=True).then_inc(pos_in, 16)
                act.dma_start(w_kv[:, :], w_kv_up[0]).then_inc(kv_w_in, 16)
                for n, w in enumerate((w_cmp2_k, w_cmp2_v)):
                    act.dma_start(w2[:, n, :, :], w[0].rearrange("(t p) d -> p t d", p=P)).then_inc(cmp_w_in, 16)
                act.dma_start(wr[:, :, 0:EXPERT_GROUPS], w_router_group[0].rearrange("(k p) n -> p k n", p=P)).then_inc(router_in, 16)
                act.dma_start(wr[:, :, EXPERT_GROUPS:], w_router_expert[0].rearrange("(k p) n -> p k n", p=P)).then_inc(router_in, 16)
                act.dma_start(brow[:, 0:EXPERT_GROUPS], b_router_group[0].partition_broadcast(P)).then_inc(router_in, 16)
                act.dma_start(brow[:, EXPERT_GROUPS:], b_router_expert[0].partition_broadcast(P)).then_inc(router_in, 16)

                def root(n, t):
                    act.wait_ge(recip_ms, n)
                    act.activation(t, t, ACT.Sqrt).then_inc(rms_ready, 1)

                drained(act, "rows")
                act.activation(condT[:, :], cols[:, R_C:R_C + KD], ACT.Tanh, scale=0.5).then_inc(tanh_c, 1)
                act.wait_ge(x_in, 16)
                for m in range(M):
                    if m:
                        step.settle()
                    ins = act.activation(junk[:, :], xs[:, m, :], ACT.Square, accum_out=tiny[:, m:m + 1])
                    if m == M - 1:
                        ins.then_inc(squares, 1)
                    else:
                        step.do(ins)
                root(1, tiny[:, 0:M])
                act.wait_ge(angles, 1)
                act.activation(trig[:, 10:12, :], trig[:, 8:10, :], ACT.Sin).then_inc(trig_ready, 1)

                def copy_out(name, dst, src):
                    made(act, name)
                    act.activation(dst, src, ACT.Copy).then_inc(act_drained, 1)

                def win(n):
                    lo, hi = WINC[n]
                    w = hi - lo
                    copy_out(f"win{n}", xp[:, :, lo:hi], bank_of(f"win{n}")[:, 0:M * w].rearrange("p (m n) -> p m n", m=M))

                def mg(n):
                    made(act, f"mg{n}")
                    act.activation(gT[:, 2 * n:2 * n + 2, :], bank_of(f"mg{n}")[:, :].rearrange("p (t n) -> p t n", t=2),
                                   ACT.Tanh, scale=0.5).then_inc(act_drained, 1)

                for n in range(3):
                    win(n)
                drained(act, "win2")
                for m in range(M):
                    if m:
                        step.settle()
                    ins = act.activation(junk[:, 0:RANK], xp[:, m, KV:KV + RANK], ACT.Square, accum_out=tiny[:, 2 + m:3 + m])
                    if m == M - 1:
                        ins.then_inc(squares, 1)
                    else:
                        step.do(ins)
                for n in range(3, len(WINC)):
                    win(n)
                root(2, tiny[:, 2:2 + M])
                drained(act, f"win{len(WINC) - 1}")
                act.activation(gates[:, :, :], xp[:, :, BR:BR + 3 * HEADS], ACT.Tanh, scale=0.5).then_inc(tanh_br, 1)
                mg(0)
                mg(1)
                for n in range(4):
                    m, half = n // 2, n % 2
                    copy_out(f"kvp{n}", kvx[:, m, half * 512:half * 512 + 512], bank_of(f"kvp{n}")[:, :])
                copy_out("iqT", iqT[:, :, :], bank_of("iqT")[:, :].rearrange("p (t n) -> p t n", t=2))
                copy_out("ikT", ikT[:, :], bank_of("ikT")[:, 0:S])
                copy_out("cmpx", cx[:, :, :, :], bank_of("cmpx")[:, :].rearrange("p (a g n) -> p a g n", a=2, g=2))
                for n in range(2):
                    copy_out(f"qbT{n}", qbT[:, 2 * n:2 * n + 2, :], bank_of(f"qbT{n}")[:, :].rearrange("p (t n) -> p t n", t=2))
                copy_out("ksT", ksT[:, :, :], bank_of("ksT")[:, :].rearrange("p (t n) -> p t n", t=2))
                copy_out("kwT", kwT[:, :, :], bank_of("kwT")[:, :].rearrange("p (t n) -> p t n", t=2))
                mg(2)
                for n in range(8):
                    m, r = n // 4, n % 4
                    nk = P * (m + 1)
                    made(act, f"il{n}")
                    act.activation(relu[m][:, r:HEADS:4, 0:nk], bank_of(f"il{n}")[:, 0:2 * nk].rearrange("p (t n) -> p t n", t=2),
                                   ACT.Relu).then_inc(act_drained, 1)
                for n, name in enumerate(("cmp1k", "cmp1v")):
                    made(act, name)
                    act.activation(hth[:, n, :, :], bank_of(name)[:, 0:2 * GROUPS * NCMP].rearrange("p (t n) -> p t n", t=2),
                                   ACT.Tanh, scale=0.5).then_inc(tanh_hid, 1)
                mg(3)
                act.wait_ge(cmp_shift, 1)
                act.activation(smc[:, :, :, :], smc[:, :, :, :], ACT.Exp, scale=SCALE).then_inc(cmp_exp, 1)

                def exps(u):
                    kind, m = UNITS[u]
                    nk = P * (m + 1)
                    act.wait_ge(unit_max, u + 1)
                    p = probs[u % 2]
                    so = 4 * (u % 2)
                    for h in range(HEADS):
                        ins = act.activation(p[:, h, 0:nk], p[:, h, 0:nk], ACT.Exp, bias=stats[:, so + 1, h:h + 1],
                                             accum_out=stats[:, so + 2, h:h + 1])
                    ins.then_inc(unit_exp, 1)

                def turns(u):
                    kind, m = UNITS[u]
                    for n in range(2 * (m + 1)):
                        name = f"T{kind}{m}_{n}"
                        copy_out(name, pT[u % 2][:, 4 * n:4 * n + 4, :], bank_of(name)[:, :].rearrange("p (t n) -> p t n", t=4))

                def pv(name, dst, m):
                    copy_out(name, dst[:, :, m * P:m * P + P], bank_of(name)[:, :].rearrange("p (t n) -> p t n", t=PAIRS))

                exps(0)
                exps(1)
                mg(4)
                for n in range(4):
                    name = f"pcT{n}"
                    made(act, name)
                    act.activation(pcT[0:NCMP, 4 * n:4 * n + 4, :], bank_of(name)[0:NCMP, :].rearrange("p (t n) -> p t n", t=4),
                                   ACT.Copy).then_inc(act_drained, 1)
                for t, name in ((qaT, "qaT"), (kaT, "kaT")):
                    for n in range(2):
                        copy_out(f"{name}{n}", t[:, 2 * n:2 * n + 2, :], bank_of(f"{name}{n}")[:, :].rearrange("p (t n) -> p t n", t=2))
                turns(0)
                exps(2)
                mg(5)
                turns(1)
                exps(3)
                mg(6)
                pv("PVb0", obT, 0)
                turns(2)
                exps(4)
                mg(7)
                turns(3)
                pv("PVb1", obT, 1)
                exps(5)
                turns(4)
                pv("PVa0", oaT, 0)
                turns(5)
                pv("PVa1", oaT, 1)
                for n in range(2):
                    copy_out(f"gb{n}", gt1bc[:, n * 512:n * 512 + 512], bank_of(f"gb{n}")[:, :])
                drained(act, "out3")
                act.dma_start(gfbc[:, :], g_final.partition_broadcast(P)).then_inc(gf_in, 16)
                for n in range(2):
                    copy_out(f"gb{n + 2}", gt2bc[:, n * 512:n * 512 + 512], bank_of(f"gb{n + 2}")[:, :])
                for m in range(M):
                    if m:
                        step.settle()
                    ins = act.activation(h2T[:, 0:4, :].rearrange("p a b -> p (a b)"), x1[:, m, :], ACT.Square, accum_out=tiny[:, 4 + m:5 + m])
                    if m == M - 1:
                        ins.then_inc(squares, 1)
                    else:
                        step.do(ins)
                root(3, tiny[:, 4:4 + M])
                act.wait_ge(x1n_ready, 1)
                act.activation(x1hi[:, :, :], x1n[:, :, :], ACT.Copy).then_inc(hi_ready, 1)
                act.wait_ge(rt_shift, 1)
                act.activation(r4[:, 1, :, :], r4[:, 0, :, :], ACT.Exp).then_inc(rt_exp, 1)
                act.wait_ge(rt_shift, 2)
                act.activation(r1[:, 6, :], r1[:, 5, :], ACT.Exp).then_inc(rt_exp, 1)

                def xg_out(count, buf):
                    act.wait_ge(xg_done, 2 * count + 1)
                    for k in range(4):
                        ins = act.activation(xgT[buf][:, k, :], bank[0][:, k * P:k * P + P], ACT.Identity,
                                             scale=A2[:, k:k + 1], bias=modT[:, 24 + k:25 + k])
                    ins.then_inc(xgT_act, 1)

                def rounds(r, late=False):
                    if late:
                        act.wait_ge(gu_done, r * EXPERTS)
                    xg_out(r * (EXPERTS // 2 + 1), 0)
                    with act.Fori(0, EXPERTS // 4) as it:
                        for b in range(2):
                            pair = r * (EXPERTS // 2) + it * 2 + b
                            for j in range(2):
                                ex = pair * 2 + j
                                act.wait_ge(gu_done, ex + 1)
                                act.wait_ge(aT_ready, ex + 1)
                                act.activation(thg[j][:, :], bank[2 + j][:, 0:2 * SLOTS], ACT.Tanh, scale=0.5).then_inc(tanh_g, 1)
                            act.wait_ge(down_done, 2 * pair + 2)
                            act.wait_ge(put_ready, pair + 1)
                            act.wait_ge(sc_drained, 4 * pair + 4)
                            for n in range(2):
                                ins = act.activation(yhi[:, n * 512:n * 512 + 512], bank[4 + n][:, :], ACT.Copy, scale=yw[:, 0:1])
                            ins.then_inc(yhi_ready, 1)
                            xg_out(pair + r + 1, 1 - b)

                act.wait_ge(most_ready, 1)
                count = act.value_load(mosti[0:1, 0:1], min_val=0, max_val=S)
                rounds(0)
                with act.Fori(1, ROUNDS) as r:
                    with act.If(count > r * SLOTS):
                        rounds(r, late=True)

                for m in range(M):
                    act.wait_ge(result, m + 1)
                    ins = act.activation(x1n[:, m, :], acc[:, m, :], ACT.Square, accum_out=tiny[:, 6 + m:7 + m])
                    ins.then_inc(squares, 1)
                root(4, tiny[:, 6:6 + M])
                for m in range(M):
                    act.wait_ge(result, M + m + 1)
                    act.dma_start(out[0, m * P:(m + 1) * P, :], x1[:, m, :]).then_inc(stored, 16)
                act.wait_ge(stored, 16 * M)

            @block.vector
            def _(dve):
                step = Steps(dve, dve_step)
                do, settle = step.do, step.settle

                def drain_done(ins):
                    ins.then_inc(dve_drained, 1)

                def mean_square(n, t, width):
                    dve.wait_ge(squares, n)
                    do(dve.tensor_scalar(t, t, 1.0 / width, EPS, ALU.mult, ALU.add))
                    settle()
                    dve.reciprocal(t, t).then_inc(recip_ms, 1)

                made(dve, "rows")
                drain_done(dve.tensor_copy(cols[:, :], bank_of("rows")[:, 0:R_END]))
                mean_square(1, tiny[:, 0:M], D)
                dve.wait_ge(tanh_c, 1)
                do(dve.scalar_tensor_tensor(condT[:, :], condT[:, :], 1.0, cols[:, R_C:R_C + KD], ALU.add, ALU.mult))
                settle()
                dve.tensor_scalar(condT[:, :], condT[:, :], 0.5, None, ALU.mult).then_inc(cond_ready, 1)
                dve.wait_ge(rms_ready, 1)
                for m in range(M):
                    dve.tensor_scalar(xs[:, m, :], xs[:, m, :], tiny[:, m:m + 1], None, ALU.mult).then_inc(xn_ready, 1)

                freq = (THETA ** (-np.arange(8, dtype=np.float32) / 8)).astype(np.float32)
                for n in range(8):
                    do(dve.memset(trig[:, 0, n:M * 8:8], float(freq[n])))
                dve.wait_ge(pos_in, 16)
                do(dve.tensor_copy(stats[:, 0, 0:M], posi[:, :]))
                settle()
                for m in range(M):
                    do(dve.tensor_scalar(trig[:, 1, m * 8:m * 8 + 8], trig[:, 0, m * 8:m * 8 + 8], stats[:, 0, m:m + 1], None, ALU.mult))
                settle()
                magic = 1.5 * 2.0 ** 23
                do(dve.tensor_scalar(trig[:, 2, :], trig[:, 1, :], float(1 / (2 * np.pi)), magic, ALU.mult, ALU.add))
                settle()
                do(dve.tensor_scalar(trig[:, 3, :], trig[:, 2, :], -magic, None, ALU.add))
                settle()
                two_pi = 2 * np.pi
                part1 = 6.28125
                part2 = float(np.float32(np.round((two_pi - part1) * 2 ** 22) / 2 ** 22))
                part3 = float(two_pi - part1 - part2)
                for n, part in enumerate((part1, part2, part3)):
                    do(dve.scalar_tensor_tensor(trig[:, 4 + n, :], trig[:, 3, :], -part, trig[:, 1 if n == 0 else 3 + n, :], ALU.mult, ALU.add))
                    settle()
                lim = float(np.nextafter(np.float32(np.pi), np.float32(0)))
                do(dve.tensor_scalar(trig[:, 8, :], trig[:, 6, :], lim, -lim, ALU.min, ALU.max))
                settle()
                do(dve.scalar_tensor_tensor(trig[:, 7, :], trig[:, 8, :], -1.0, trig[:, 8, :], ALU.mult, ALU.max))
                settle()
                dve.tensor_scalar(trig[:, 9, :], trig[:, 7, :], -1.0, float(np.float32(np.pi / 2)), ALU.mult, ALU.add).then_inc(angles, 1)
                dve.wait_ge(trig_ready, 1)
                for n, row in enumerate((11, 10)):
                    src = trig[:, row, :].rearrange("p (m f) -> p m f", m=M)
                    for half in range(2):
                        do(dve.tensor_copy(c16[:, n, :, half * 8:half * 8 + 8], src))
                        do(dve.tensor_copy(c8[:, n, :, half * 4:half * 4 + 4], src[:, :, 0:8:2]))
                settle()

                for n in range(2):
                    made(dve, f"ada{n}")
                    drain_done(dve.tensor_tensor(modT[:, 8 * n:8 * n + 8], bank_of(f"ada{n}")[:, 0:KD],
                                                 cols[:, R_BADA + 8 * n:R_BADA + 8 * n + 8], ALU.add))
                drained(dve, "ada1")
                do(dve.scalar_tensor_tensor(A1[:, :], modT[:, 8:16], 1.0, cols[:, R_G1:R_G1 + KD], ALU.add, ALU.mult))
                settle()
                for n in range(4):
                    name = f"xT{n}"
                    made(dve, name)
                    for kk in range(2):
                        k = 2 * n + kk
                        ins = dve.tensor_scalar(hT[:, k, :], bank_of(name)[:, kk * S:kk * S + S], A1[:, k:k + 1],
                                                modT[:, k:k + 1], ALU.mult, ALU.add)
                    drain_done(ins)

                def rotate(xv, heads, table, rot, final=None):
                    half = rot // 2
                    av, bv = ropeA[:, :, 0:heads, 0:rot], ropeB[:, :, 0:heads, 0:rot]
                    cosv = table[:, 0].unsqueeze(2).to_broadcast([P, M, heads, rot])
                    sinv = table[:, 1].unsqueeze(2).to_broadcast([P, M, heads, rot])
                    do(dve.tensor_tensor(av, xv[:, :, :, 0:rot], cosv, ALU.mult))
                    do(dve.tensor_tensor(bv, xv[:, :, :, 0:rot], sinv, ALU.mult))
                    settle()
                    do(dve.tensor_tensor(xv[:, :, :, 0:half], av[:, :, :, 0:half], bv[:, :, :, half:rot], ALU.subtract))
                    ins = dve.tensor_tensor(xv[:, :, :, half:rot], av[:, :, :, half:rot], bv[:, :, :, 0:half], ALU.add)
                    do(ins)
                    settle()

                def heads_of(col, heads, width):
                    return xp[:, :, col:col + heads * width].rearrange("p m (h w) -> p m h w", w=width)

                mean_square(2, tiny[:, 2:2 + M], RANK)
                drained(dve, "win3")
                rotate(heads_of(IQ, IDX_HEADS, IDX_DIM), IDX_HEADS, c8, IDX_ROT)
                rotate(heads_of(IK, 1, IDX_DIM), 1, c8, IDX_ROT)
                for n in range(4):
                    do(dve.tensor_copy(kdup[:, :, 4, n * IDX_DIM:(n + 1) * IDX_DIM], xp[:, :, IK:IK + IDX_DIM]))
                settle()
                dve.wait_ge(rms_ready, 2)
                for m in range(M):
                    dve.tensor_scalar(kvn[:, m, :], xp[:, m, KV:KV + RANK], tiny[:, 2 + m:3 + m], None, ALU.mult).then_inc(kvn_ready, 1)
                drained(dve, f"win{len(WINC) - 1}")
                rotate(heads_of(QB, HEADS + GROUPS, HD), HEADS + GROUPS, c16, ROT)
                for n, col in enumerate((KS, KW)):
                    rotate(heads_of(col, GROUPS, HD), GROUPS, c16, ROT)
                    for twice in range(2):
                        do(dve.tensor_copy(kdup[:, :, 2 * n:2 * n + 2, twice * HD:(twice + 1) * HD], heads_of(col, GROUPS, HD)))
                settle()
                do(dve.memset(tiny[:, 60:61], 0.0))
                settle()
                dve.memset(tiny[:, 61:62], 0.0).then_inc(roped, 1)
                made(dve, "kvT")
                drain_done(dve.tensor_scalar(kvnT[:, :], bank_of("kvT")[:, 0:S], cols[:, R_GKV:R_GKV + 1], None, ALU.mult))
                rotate(heads_of(QA, HEADS, HD), HEADS, c16, ROT)
                dve.wait_ge(tanh_br, 1)
                do(dve.tensor_scalar(gates[:, :, :], gates[:, :, :], 0.5, 0.5, ALU.mult, ALU.add))
                settle()

                drained(dve, "cmpx")
                for n in range(2):
                    pe = cols[:, (R_PEK, R_PEV)[n]:(R_PEK, R_PEV)[n] + CMP_TILES]
                    for gi in range(GROUPS):
                        src = cx[:, n, gi, :]
                        win_ap = overlap(src)
                        ins = dve.tensor_tensor(flat[:, n, :, gi * NCMP:(gi + 1) * NCMP], win_ap,
                                                pe.unsqueeze(2).to_broadcast([P, CMP_TILES, NCMP]), ALU.add)
                        do(ins)
                settle()
                dve.memset(tiny[:, 62:63], 0.0).then_inc(flat_ready, 1)
                drained(dve, "kvp3")
                rotate(kvx[:, :, 0:HEADS * HD].rearrange("p m (h w) -> p m h w", w=HD), HEADS, c16, ROT)
                dve.memset(tiny[:, 61:62], 0.0).then_inc(roped, 1)

                for n, name in enumerate(("cmp1k", "cmp1v")):
                    made(dve, name)
                    dve.wait_ge(tanh_hid, n + 1)
                    drain_done(dve.scalar_tensor_tensor(hid[:, n, :, :], hth[:, n, :, :], 1.0,
                                                        bank_of(name)[:, 0:2 * GROUPS * NCMP].rearrange("p (t n) -> p t n", t=2),
                                                        ALU.add, ALU.mult))
                made(dve, "cmp2")
                do(dve.tensor_scalar(kcT[:, :], bank_of("cmp2")[:, 0:GROUPS * NCMP], 0.5, None, ALU.mult))
                drain_done(dve.tensor_scalar(vcs[0:NCMP, :, :], bank_of("cmp2")[0:NCMP, 64:64 + GROUPS * HD].rearrange("p (g d) -> p g d", g=GROUPS),
                                             0.5, None, ALU.mult))
                for par in range(2):
                    made(dve, f"sc{par}")
                    drain_done(dve.tensor_tensor(smc[:, :, par * PAIRS:(par + 1) * PAIRS, :],
                                                 bank_of(f"sc{par}")[:, 0:M * PAIRS * NCMP].rearrange("p (m i c) -> p m i c", m=M, i=PAIRS),
                                                 cbc[:, :, :].unsqueeze(2).to_broadcast([P, M, PAIRS, NCMP]), ALU.add))
                drained(dve, "sc1")
                cmax = stats[:, 8:10, :]
                do(dve.tensor_reduce(cmax, smc[:, :, :, :], AX, ALU.max))
                settle()
                dve.tensor_tensor(smc[:, :, :, :], smc[:, :, :, :], cmax.unsqueeze(3).to_broadcast([P, M, HEADS, NCMP]),
                                  ALU.subtract).then_inc(cmp_shift, 1)
                dve.wait_ge(cmp_exp, 1)
                do(dve.tensor_tensor(smc[:, :, :, :], smc[:, :, :, :], cmk[:, :, :].unsqueeze(2).to_broadcast([P, M, HEADS, NCMP]), ALU.mult))
                settle()
                do(dve.tensor_reduce(cmax, smc[:, :, :, :], AX, ALU.add))
                settle()
                do(dve.tensor_scalar_max(cmax, cmax, TINY))
                settle()
                do(dve.reciprocal(cmax, cmax))
                settle()
                for par in range(2):
                    do(dve.tensor_tensor(cmax[:, :, par * PAIRS:(par + 1) * PAIRS], cmax[:, :, par * PAIRS:(par + 1) * PAIRS],
                                         gates[:, :, 3 * par:3 * HEADS:6], ALU.mult))
                settle()
                dve.tensor_tensor(smc[:, :, :, :], smc[:, :, :, :], cmax.unsqueeze(3).to_broadcast([P, M, HEADS, NCMP]),
                                  ALU.mult).then_inc(cmp_probs, 1)

                def index_select():
                    for m in range(M):
                        nk = P * (m + 1)
                        drained(dve, f"il{4 * m + 3}")
                        for h in range(IDX_HEADS):
                            prev = cbias[:, m, 0:nk] if h == 0 else iscore[:, m, 0:nk]
                            do(dve.scalar_tensor_tensor(iscore[:, m, 0:nk], relu[m][:, h, 0:nk], xp[:, m, IW + h:IW + h + 1],
                                                        prev, ALU.mult, ALU.add))
                            settle()
                        for n in range(TOPK // 8):
                            src = iscore if n == 0 else iwork
                            do(dve.max(stats[:, 11, :], src[:, m, 0:nk]))
                            settle()
                            do(dve.match_replace(iwork[:, m, 0:nk], stats[:, 11, :], src[:, m, 0:nk], -3e38))
                            settle()
                        do(dve.tensor_scalar(iwork[:, m, 0:nk], iwork[:, m, 0:nk], -2e38, NEG, ALU.is_gt, ALU.mult))
                        settle()
                        do(dve.tensor_tensor(abias[:, m, 0:nk], iwork[:, m, 0:nk], cbias[:, m, 0:nk], ALU.min))
                        settle()

                def scores(u):
                    kind, m = UNITS[u]
                    nk = P * (m + 1)
                    per = PAIRS // (m + 1)
                    p, so = probs[u % 2], 4 * (u % 2)
                    mask = (abias if kind == "dsa" else cbias)[:, m, 0:nk]
                    if u >= 2:
                        made(dve, f"T{UNITS[u - 2][0]}{UNITS[u - 2][1]}_{2 * UNITS[u - 2][1] + 1}")
                    for n in range(2 * (m + 1)):
                        name = f"S{kind}{m}_{n}"
                        made(dve, name)
                        for j in range(per):
                            hs = n * per + j
                            ins = dve.tensor_tensor_reduce(p[:, hs, 0:nk], bank_of(name)[:, j * nk:(j + 1) * nk], mask,
                                                           SCALE, -3e38, ALU.add, ALU.max, stats[:, so, hs:hs + 1])
                        drain_done(ins)
                    drained(dve, f"S{kind}{m}_{2 * m + 1}")
                    dve.tensor_scalar(stats[:, so + 1, :], stats[:, so, :], -1.0, None, ALU.mult).then_inc(unit_max, 1)

                def normalise(u):
                    kind, m = UNITS[u]
                    nk = P * (m + 1)
                    p, so = probs[u % 2], 4 * (u % 2)
                    dve.wait_ge(unit_exp, u + 1)
                    do(dve.reciprocal(stats[:, so + 3, :], stats[:, so + 2, :]))
                    settle()
                    if kind != "dsa":
                        branch = 1 if kind == "sel" else 2
                        for par in range(2):
                            s = stats[:, so + 3, par * PAIRS:(par + 1) * PAIRS]
                            do(dve.tensor_tensor(s, s, gates[:, m, 3 * par + branch:3 * HEADS:6], ALU.mult))
                        settle()
                    dve.tensor_tensor(p[:, :, 0:nk], p[:, :, 0:nk], stats[:, so + 3, :].unsqueeze(2).to_broadcast([P, HEADS, nk]),
                                      ALU.mult).then_inc(unit_probs, 1)

                index_select()
                scores(0)
                scores(1)
                normalise(0)
                normalise(1)
                scores(2)
                scores(3)
                normalise(2)
                scores(4)
                normalise(3)
                scores(5)

                def ada(n):
                    made(dve, f"ada{n}")
                    drain_done(dve.tensor_tensor(modT[:, 8 * n:8 * n + 8], bank_of(f"ada{n}")[:, 0:KD],
                                                 cols[:, R_BADA + 8 * n:R_BADA + 8 * n + 8], ALU.add))

                normalise(4)
                ada(2)
                ada(3)
                normalise(5)
                ada(4)
                drained(dve, "ada4")
                do(dve.scalar_tensor_tensor(A2[:, :], modT[:, 32:40], 1.0, cols[:, R_G2:R_G2 + KD], ALU.add, ALU.mult))
                ada(5)
                made(dve, "PVa0")
                for k in range(KD):
                    ins = dve.tensor_scalar(diag[:, k * P:(k + 1) * P], ident[:, :], modT[:, 16 + k:17 + k], 0.5, ALU.mult, ALU.mult)
                ins.then_inc(diag_ready, 1)
                drained(dve, "mg7")
                for t in range(KD):
                    name = f"up{t}"
                    made(dve, name)
                    b = bank_of(name)
                    do(dve.scalar_tensor_tensor(mT[:, t, :], gT[:, t, :], 1.0, b[:, 0:S], ALU.add, ALU.mult))
                    drain_done(dve.scalar_tensor_tensor(tmp_up[:, t % 2, :], gT[:, KD + t, :], 1.0, b[:, S:2 * S], ALU.add, ALU.mult))
                    drained(dve, name)
                    settle()
                    dve.tensor_tensor(mT[:, t, :], mT[:, t, :], tmp_up[:, t % 2, :], ALU.add).then_inc(gates_ready, 1)
                drained(dve, "gb1")
                dve.wait_ge(x_again, 16)
                for n in range(4):
                    name = f"out{n}"
                    made(dve, name)
                    xv = x1[:, :, n * CH:(n + 1) * CH]
                    do(dve.tensor_tensor(xv, bank_of(name)[:, :].rearrange("p (m n) -> p m n", m=M),
                                         gt1bc[:, n * CH:(n + 1) * CH].unsqueeze(1).to_broadcast([P, M, CH]), ALU.mult))
                    settle()
                    drain_done(dve.tensor_tensor(xv, xv, xr[:, :, n * CH:(n + 1) * CH], ALU.add))
                drained(dve, "out3")
                for k in range(KD):
                    ins = dve.tensor_scalar(diag2[:, k * P:(k + 1) * P], ident[:, :], modT[:, 40 + k:41 + k], None, ALU.mult)
                ins.then_inc(diag_ready, 1)
                do(dve.memset(acc[:, :, :], 0.0))
                mean_square(3, tiny[:, 4:4 + M], D)
                dve.wait_ge(rms_ready, 3)
                do(dve.tensor_scalar(x1n[:, 0, :], x1[:, 0, :], tiny[:, 4:5], None, ALU.mult))
                dve.tensor_scalar(x1n[:, 1, :], x1[:, 1, :], tiny[:, 5:6], None, ALU.mult).then_inc(x1n_ready, 1)
                for n in range(4):
                    name = f"x1T{n}"
                    made(dve, name)
                    for kk in range(2):
                        k = 2 * n + kk
                        ins = dve.tensor_scalar(h2T[:, k, :], bank_of(name)[:, kk * S:kk * S + S], A2[:, k:k + 1],
                                                modT[:, 24 + k:25 + k], ALU.mult, ALU.add)
                    drain_done(ins)

                made(dve, "rt")
                dve.wait_ge(router_in, 64)
                drain_done(dve.tensor_tensor(route[:, :, :], bank_of("rt")[:, 0:M * 36].rearrange("p (m n) -> p m n", m=M),
                                             brow[:, :].unsqueeze(1).to_broadcast([P, M, 36]), ALU.add))
                drained(dve, "rt")
                dve.wait_ge(hi_ready, 1)
                dve.tensor_tensor(x1lo[:, :, :], x1n[:, :, :], x1hi[:, :, :].bitcast(F32), ALU.subtract).then_inc(lo_ready, 1)

                def bc(v, n):
                    return v.unsqueeze(2).to_broadcast([P, M, n])

                def first_greatest(values, greatest, cand, n):
                    do(dve.tensor_reduce(greatest, values, AX, ALU.max))
                    settle()
                    do(dve.tensor_tensor(cand, values, bc(greatest, n), ALU.is_ge))
                    settle()
                    do(dve.scalar_tensor_tensor(cand, cand, -1000.0, iota8[:, 0:n].unsqueeze(1).to_broadcast([P, M, n]), ALU.mult, ALU.add))
                    settle()
                    do(dve.tensor_reduce(r1[:, 10, :], cand, AX, ALU.min))
                    settle()
                    do(dve.tensor_tensor(cand, cand, bc(r1[:, 10, :], n), ALU.is_equal))
                    settle()

                lg = route[:, :, 0:EXPERT_GROUPS]
                oh4 = r4[:, 2]
                first_greatest(lg, r1[:, 0, :], oh4, EXPERT_GROUPS)
                dve.tensor_tensor(r4[:, 0], lg, bc(r1[:, 0, :], EXPERT_GROUPS), ALU.subtract).then_inc(rt_shift, 1)
                do(dve.tensor_tensor(r32[:, :, :, :], route[:, :, EXPERT_GROUPS:].rearrange("p m (g n) -> p m g n", g=EXPERT_GROUPS),
                                     oh4.unsqueeze(3).to_broadcast([P, M, EXPERT_GROUPS, PER_GROUP]), ALU.mult))
                settle()
                le = r8[:, 0]
                do(dve.tensor_reduce(le, r32[:, :, :, :].rearrange("p m g n -> p m n g"), AX, ALU.add))
                settle()
                first_greatest(le, r1[:, 1, :], r8[:, 1], PER_GROUP)
                do(dve.scalar_tensor_tensor(r8[:, 2], r8[:, 1], -3e38, le, ALU.mult, ALU.add))
                settle()
                first_greatest(r8[:, 2], r1[:, 2, :], r8[:, 3], PER_GROUP)
                dve.tensor_tensor(r1[:, 5, :], r1[:, 2, :], r1[:, 1, :], ALU.subtract).then_inc(rt_shift, 1)
                dve.wait_ge(rt_exp, 2)
                do(dve.tensor_reduce(r1[:, 3, :], r4[:, 1], AX, ALU.add))
                do(dve.tensor_scalar(r1[:, 7, :], r1[:, 6, :], 1.0, 2.0, ALU.add, ALU.mult))
                settle()
                do(dve.tensor_tensor(r1[:, 8, :], r1[:, 3, :], r1[:, 7, :], ALU.mult))
                settle()
                do(dve.reciprocal(r1[:, 8, :], r1[:, 8, :]))
                settle()
                do(dve.tensor_tensor(r1[:, 9, :], r1[:, 8, :], r1[:, 6, :], ALU.mult))
                settle()
                do(dve.tensor_tensor(r8[:, 4], r8[:, 1], bc(r1[:, 8, :], PER_GROUP), ALU.mult))
                do(dve.tensor_tensor(r8[:, 5], r8[:, 3], bc(r1[:, 9, :], PER_GROUP), ALU.mult))
                do(dve.tensor_tensor(r8[:, 6], r8[:, 1], r8[:, 3], ALU.add))
                settle()
                do(dve.tensor_tensor(r8[:, 4], r8[:, 4], r8[:, 5], ALU.add))
                do(dve.memset(comb[:, :, EXPERTS:], 0.0))
                do(dve.memset(slot[:, :, EXPERTS:], -1.0))
                settle()
                four = oh4.unsqueeze(3).to_broadcast([P, M, EXPERT_GROUPS, PER_GROUP])
                do(dve.tensor_tensor(comb[:, :, 0:EXPERTS].rearrange("p m (g n) -> p m g n", g=EXPERT_GROUPS), four,
                                     r8[:, 4].unsqueeze(2).to_broadcast([P, M, EXPERT_GROUPS, PER_GROUP]), ALU.mult))
                dve.tensor_tensor(sel[:, :, 0:EXPERTS].rearrange("p m (g n) -> p m g n", g=EXPERT_GROUPS), four,
                                  r8[:, 6].unsqueeze(2).to_broadcast([P, M, EXPERT_GROUPS, PER_GROUP]), ALU.mult).then_inc(sel_ready, 1)
                made(dve, "pos")
                dve.wait_ge(sel_ready, 1)
                do(dve.tensor_reduce(most[:, :], bank_of("pos")[:, 2 * EXPERTS:3 * EXPERTS], AX, ALU.max))
                settle()
                drain_done(dve.scalar_tensor_tensor(slot[:, :, 0:EXPERTS], bank_of("pos")[:, 0:2 * EXPERTS].rearrange("p (m n) -> p m n", m=M),
                                                    1.0, sel[:, :, 0:EXPERTS], ALU.add, ALU.mult))
                dve.tensor_copy(mosti[:, :], most[:, :]).then_inc(most_ready, 1)
                drained(dve, "pos")
                do(dve.tensor_scalar_add(slot[:, :, 0:EXPERTS], slot[:, :, 0:EXPERTS], -1.0))
                settle()

                def picks(first, buf):
                    for m in range(M):
                        for j in range(2):
                            s = slice(j * SLOTS, (j + 1) * SLOTS)
                            sc = slot[:, m, bass.ds(first + j, 1)]
                            w = comb[:, m, bass.ds(first + j, 1)]
                            dve.tensor_scalar(pick[buf][:, m, s], iota_slot[:, :], sc, None, ALU.is_equal)
                            ins = dve.tensor_scalar(pickw[buf][:, m, s], iota_slot[:, :], sc, w, ALU.is_equal, ALU.mult)
                    ins.then_inc(pick_ready, 1)

                def xg_out(count, buf):
                    dve.wait_ge(xg_done, 2 * count + 2)
                    for k in range(4, KD):
                        ins = dve.tensor_scalar(xgT[buf][:, k, :], bank[1][:, (k - 4) * P:(k - 3) * P], A2[:, k:k + 1],
                                                modT[:, 24 + k:25 + k], ALU.mult, ALU.add)
                    ins.then_inc(xgT_dve, 1)

                def rounds(r, late=False):
                    if late:
                        dve.wait_ge(pick_ready, r * (EXPERTS // 2 + 1))
                        dve.tensor_scalar_add(slot[:, :, :], slot[:, :, :], float(-SLOTS)).then_inc(mo_step, 1)
                        dve.wait_ge(mo_step, r)
                        dve.wait_ge(xg_done, r * (EXPERTS + 2))
                        dve.wait_ge(put_done, r * (EXPERTS // 2))
                    picks(0, 0)
                    xg_out(r * (EXPERTS // 2 + 1), 0)
                    with dve.Fori(0, EXPERTS // 4) as it:
                        for b in range(2):
                            pair = r * (EXPERTS // 2) + it * 2 + b
                            picks(it * 4 + 2 * b + 2, 1 - b)
                            for j in range(2):
                                ex = pair * 2 + j
                                dve.wait_ge(tanh_g, ex + 1)
                                dve.scalar_tensor_tensor(sig[j][:, :], thg[j][:, :], 1.0, bank[2 + j][:, 0:2 * SLOTS],
                                                         ALU.add, ALU.mult).then_inc(silu_step, 1)
                                dve.wait_ge(silu_step, ex + 1)
                                dve.tensor_tensor(aT[j][:, :, :], bank[2 + j][:, 2 * SLOTS:4 * SLOTS].rearrange("p (t n) -> p t n", t=2),
                                                  sig[j][:, :].rearrange("p (t n) -> p t n", t=2), ALU.mult).then_inc(aT_ready, 1)
                            dve.wait_ge(put_done, pair + 1)
                            pb = bank[6 + (5 * b) % 2]
                            dve.tensor_copy(putT[:, :], pb[:, 0:M * P])
                            dve.tensor_copy(yw[:, :], pb[:, M * P:M * P + 1]).then_inc(put_ready, 1)
                            dve.wait_ge(put_ready, pair + 1)
                            dve.wait_ge(yhi_ready, pair + 1)
                            for n in range(2):
                                s = slice(n * 512, n * 512 + 512)
                                ins = dve.scalar_tensor_tensor(ylo[:, s], bank[4 + n][:, :], yw[:, 0:1], yhi[:, s].bitcast(F32),
                                                               ALU.mult, ALU.subtract)
                            ins.then_inc(ylo_ready, 1)
                            xg_out(pair + r + 1, 1 - b)
                            dve.wait_ge(sc_drained, 4 * pair + 4)
                            for n in range(4):
                                dve.wait_ge(sc_done, 4 * pair + n + 1)
                                av = acc[:, n // 2, (n % 2) * 512:(n % 2) * 512 + 512]
                                dve.tensor_tensor(av, bank[6 + (5 * b + 1 + n) % 2][:, :], av, ALU.add).then_inc(sc_drained, 1)

                dve.memset(aT[0][:, :, :], 0.0).then_inc(aT_ready, 2)
                dve.memset(aT[1][:, :, :], 0.0).then_inc(sc_drained, 4)
                dve.wait_ge(sc_drained, 4)
                dve.wait_ge(aT_ready, 2)
                dve.wait_ge(most_ready, 1)
                count = dve.value_load(mosti[0:1, 0:1], min_val=0, max_val=S)
                rounds(0)
                with dve.Fori(1, ROUNDS) as r:
                    with dve.If(count > r * SLOTS):
                        rounds(r, late=True)

                dve.drain()
                drained(dve, "gb3")
                dve.wait_ge(gf_in, 16)
                for m in range(M):
                    do(dve.tensor_tensor(acc[:, m, :], acc[:, m, :], gt2bc[:, :], ALU.mult))
                    settle()
                    dve.tensor_tensor(acc[:, m, :], acc[:, m, :], x1[:, m, :], ALU.add).then_inc(result, 1)
                dve.wait_ge(result, M)
                mean_square(3 + M, tiny[:, 6:6 + M], D)
                dve.wait_ge(rms_ready, 4)
                for m in range(M):
                    dve.scalar_tensor_tensor(x1[:, m, :], acc[:, m, :], tiny[:, 6 + m:7 + m], gfbc[:, :], ALU.mult, ALU.mult).then_inc(result, 1)

            @block.tensor
            def _(pe):
                def begin(name):
                    n = INDEX[name]
                    if n >= 8:
                        drained(pe, ORDER[n - 8][0])
                    return bank_of(name)

                def done(ins):
                    ins.then_inc(product_done, 1)

                pe.wait_ge(rows_in, 16 * 7)
                pe.wait_ge(consts, ALL_CONSTS)
                b = begin("rows")
                done(pe.transpose(b[:, 0:R_END], rows[0:R_END, :], ident[0:R_END, 0:R_END]))

                def ada(n):
                    b = begin(f"ada{n}")
                    for t in range(KD):
                        arrived(pe, "ada", 4 * n + t // 2)
                        w = chunk("ada", 4 * n + t // 2).rearrange("p (k n) -> p k n", k=KD)
                        for k in range(KD):
                            ins = pe.matmul(b[:, t:t + 1], w[:, k, (t % 2) * P:(t % 2) * P + P], condT[:, k:k + 1],
                                            start=(k == 0), stop=(k == KD - 1))
                    done(ins)

                def turn_x(name, n, src):
                    b = begin(name)
                    for kk in range(2):
                        for m in range(M):
                            k = 2 * n + kk
                            ins = pe.transpose(b[:, kk * S + m * P:kk * S + m * P + P], src[:, m, k * P:(k + 1) * P], ident[:, :])
                    done(ins)

                def win(n):
                    lo, hi = WINC[n]
                    wd = hi - lo
                    b = begin(f"win{n}")
                    arrived(pe, "win", n)
                    w = chunk("win", n)[:, 0:KD * wd].rearrange("p (k n) -> p k n", k=KD)
                    for m in range(M):
                        for k in range(KD):
                            ins = pe.matmul(b[:, m * wd:(m + 1) * wd], hT[:, k, m * P:(m + 1) * P], w[:, k, :],
                                            start=(k == 0), stop=(k == KD - 1))
                    done(ins)

                def mg(n):
                    b = begin(f"mg{n}")
                    arrived(pe, "mg", n)
                    w = chunk("mg", n).rearrange("p (k n) -> p k n", k=KD)
                    for t in range(2):
                        for k in range(KD):
                            ins = pe.matmul(b[:, t * S:(t + 1) * S], w[:, k, t * P:(t + 1) * P], hT[:, k, :],
                                            start=(k == 0), stop=(k == KD - 1))
                    done(ins)

                def turn_cols(name, tiles):
                    b = begin(name)
                    for t, tile in enumerate(tiles):
                        for m in range(M):
                            ins = pe.transpose(b[:, t * S + m * P:t * S + m * P + P], tile(m), ident[:, :])
                    done(ins)

                pe.wait_ge(cond_ready, 1)
                ada(0)
                ada(1)
                pe.wait_ge(xn_ready, 2)
                for n in range(4):
                    turn_x(f"xT{n}", n, xs)
                drained(pe, "xT3")
                for n in range(len(WINC)):
                    win(n)
                mg(0)
                pe.wait_ge(kvn_ready, 2)
                b = begin("kvT")
                for m in range(M):
                    ins = pe.transpose(b[:, m * P:(m + 1) * P], kvn[:, m, :], ident[:, :])
                done(ins)
                mg(1)
                drained(pe, "kvT")
                pe.wait_ge(kv_w_in, 16)
                for n in range(4):
                    m, half = n // 2, n % 2
                    b = begin(f"kvp{n}")
                    done(pe.matmul(b[:, :], kvnT[:, m * P:(m + 1) * P], w_kv[:, half * 512:half * 512 + 512], start=True, stop=True))
                pe.wait_ge(roped, 1)
                turn_cols("iqT", [lambda m, t=t: xp[:, m, IQ + t * P:IQ + (t + 1) * P] for t in range(2)])
                turn_cols("ikT", [lambda m: kdup[:, m, 4, :]])
                b = begin("cmpx")
                for n, col in enumerate((KC, VC)):
                    for gi in range(GROUPS):
                        for par in range(2):
                            for m in range(M):
                                at = (n * GROUPS + gi) * P + m * HD
                                ins = pe.matmul(b[par * HD:(par + 1) * HD, at:at + HD], xp[:, m, col + gi * HD:col + (gi + 1) * HD],
                                                ident[:, par:P:2], start=True, stop=True)
                done(ins)
                for n in range(2):
                    turn_cols(f"qbT{n}", [lambda m, t=t: xp[:, m, QB + t * P:QB + (t + 1) * P] for t in (2 * n, 2 * n + 1)])
                turn_cols("ksT", [lambda m, gi=gi: kdup[:, m, gi, :] for gi in range(2)])
                turn_cols("kwT", [lambda m, gi=gi: kdup[:, m, 2 + gi, :] for gi in range(2)])
                mg(2)
                drained(pe, "ikT")
                for n in range(8):
                    m, r = n // 4, n % 4
                    nk = P * (m + 1)
                    rows_ = slice(r * IDX_DIM, (r + 1) * IDX_DIM)
                    b = begin(f"il{n}")
                    for t in range(2):
                        ins = pe.matmul(b[:, t * nk:(t + 1) * nk], iqT[rows_, t, m * P:(m + 1) * P], ikT[rows_, 0:nk], start=True, stop=True,
                                        tile_position=(r * IDX_DIM, 0))
                    done(ins)
                pe.wait_ge(flat_ready, 1)
                for n, name in enumerate(("cmp1k", "cmp1v")):
                    b = begin(name)
                    arrived(pe, name, 0)
                    arrived(pe, name, 1)
                    for t in range(2):
                        for j in range(CMP_TILES):
                            w = chunk(name, j // KD).rearrange("p (k n) -> p k n", k=KD)
                            ins = pe.matmul(b[:, t * GROUPS * NCMP:(t + 1) * GROUPS * NCMP], w[:, j % KD, t * P:(t + 1) * P],
                                            flat[:, n, j, :], start=(j == 0), stop=(j == CMP_TILES - 1))
                    done(ins)
                mg(3)
                b = begin("cmp2")
                drained(pe, "cmp1v")
                pe.wait_ge(cmp_w_in, 32)
                for par in range(2):
                    for t in range(2):
                        pe.matmul(b[par * HD:(par + 1) * HD, 0:GROUPS * NCMP], w2[:, 0, t, :], hid[:, 0, t, :], start=(t == 0), stop=(t == 1))
                for gi in range(GROUPS):
                    for t in range(2):
                        ins = pe.matmul(b[0:NCMP, 64 + gi * HD:64 + (gi + 1) * HD], hid[:, 1, t, gi * NCMP:(gi + 1) * NCMP],
                                        w2[:, 1, t, :], start=(t == 0), stop=(t == 1))
                done(ins)
                drained(pe, "cmp2")
                for par in range(2):
                    b = begin(f"sc{par}")
                    r = slice(par * HD, (par + 1) * HD)
                    for m in range(M):
                        for i in range(PAIRS):
                            g = (2 * i + par) // (HEADS // GROUPS)
                            at = (m * PAIRS + i) * NCMP
                            ins = pe.matmul(b[:, at:at + NCMP], qbT[r, i, m * P:(m + 1) * P], kcT[r, g * NCMP:(g + 1) * NCMP], start=True, stop=True,
                                            tile_position=(par * HD, 0))
                    done(ins)

                def scores(u):
                    kind, m = UNITS[u]
                    nk = P * (m + 1)
                    per = PAIRS // (m + 1)
                    for n in range(2 * (m + 1)):
                        b = begin(f"S{kind}{m}_{n}")
                        for j in range(per):
                            hs = n * per + j
                            par, i = hs // PAIRS, hs % PAIRS
                            g = (2 * i + par) // (HEADS // GROUPS)
                            r = slice(par * HD, (par + 1) * HD)
                            q = (qaT if kind == "dsa" else qbT)[r, i, m * P:(m + 1) * P]
                            k = kaT[r, i, 0:nk] if kind == "dsa" else (ksT if kind == "sel" else kwT)[r, g, 0:nk]
                            ins = pe.matmul(b[:, j * nk:(j + 1) * nk], q, k, start=True, stop=True, tile_position=(par * HD, 0))
                        done(ins)

                def turns(u):
                    kind, m = UNITS[u]
                    pe.wait_ge(unit_probs, u + 1)
                    if u >= 2:
                        pass
                    for n in range(2 * (m + 1)):
                        b = begin(f"T{kind}{m}_{n}")
                        for j in range(4):
                            at = 4 * n + j
                            hs, kb = at // (m + 1), at % (m + 1)
                            ins = pe.transpose(b[:, j * P:(j + 1) * P], probs[u % 2][:, hs, kb * P:(kb + 1) * P], ident[:, :])
                        done(ins)

                def last_turn(u):
                    return f"T{UNITS[u][0]}{UNITS[u][1]}_{2 * UNITS[u][1] + 1}"

                def pv_b(m):
                    drained(pe, last_turn(2 * m + 1))
                    drained(pe, "pcT3")
                    b = begin(f"PVb{m}")
                    for hs in range(HEADS):
                        par, i = hs // PAIRS, hs % PAIRS
                        g = (2 * i + par) // (HEADS // GROUPS)
                        o = b[par * HD:(par + 1) * HD, i * P:(i + 1) * P]
                        pe.matmul(o, vcs[0:NCMP, g, :], pcT[0:NCMP, m * HEADS + hs, :], start=True, stop=False)
                        for buf, col in ((0, VS), (1, VW)):
                            for kb in range(m + 1):
                                ins = pe.matmul(o, xp[:, kb, col + g * HD:col + (g + 1) * HD], pT[buf][:, hs * (m + 1) + kb, :],
                                                start=False, stop=(buf == 1 and kb == m))
                    done(ins)

                def pv_a(m):
                    drained(pe, last_turn(4 + m))
                    b = begin(f"PVa{m}")
                    for hs in range(HEADS):
                        par, i = hs // PAIRS, hs % PAIRS
                        h = 2 * i + par
                        o = b[par * HD:(par + 1) * HD, i * P:(i + 1) * P]
                        for kb in range(m + 1):
                            v = kvx[:, kb, HEADS * HD + h * HD:HEADS * HD + (h + 1) * HD]
                            ins = pe.matmul(o, v, pT[m][:, hs * (m + 1) + kb, :], start=(kb == 0), stop=(kb == m))
                    done(ins)

                drained(pe, "kwT")
                scores(0)
                scores(1)
                mg(4)
                pe.wait_ge(cmp_probs, 1)
                for n in range(4):
                    b = begin(f"pcT{n}")
                    for j in range(4):
                        at = 4 * n + j
                        ins = pe.transpose(b[0:NCMP, j * P:(j + 1) * P], smc[:, at // HEADS, at % HEADS, :], ident[:, :])
                    done(ins)
                pe.wait_ge(roped, 2)
                for n in range(2):
                    turn_cols(f"qaT{n}", [lambda m, t=t: xp[:, m, QA + t * P:QA + (t + 1) * P] for t in (2 * n, 2 * n + 1)])
                for n in range(2):
                    turn_cols(f"kaT{n}", [lambda m, t=t: kvx[:, m, t * P:(t + 1) * P] for t in (2 * n, 2 * n + 1)])
                turns(0)
                scores(2)
                mg(5)
                turns(1)
                scores(3)
                mg(6)
                pv_b(0)
                turns(2)
                drained(pe, "kaT1")
                scores(4)
                mg(7)
                turns(3)
                pv_b(1)
                scores(5)
                ada(2)
                turns(4)
                pv_a(0)
                ada(3)
                turns(5)
                pv_a(1)
                ada(4)
                ada(5)
                pe.wait_ge(diag_ready, 1)
                for n in range(2):
                    b = begin(f"gb{n}")
                    done(pe.matmul(b[:, :], ones[:, :], diag[:, n * 512:n * 512 + 512], start=True, stop=True))
                drained(pe, "PVa1")
                for t in range(KD):
                    b = begin(f"up{t}")
                    for n, (kind, o) in enumerate((("upa", oaT), ("upb", obT))):
                        if t % 4 == 0:
                            arrived(pe, kind, t // 4)
                        w = chunk(kind, t // 4).rearrange("p (k n) -> p k n", k=PAIRS)
                        for i in range(PAIRS):
                            ins = pe.matmul(b[:, n * S:(n + 1) * S], w[:, i, (t % 4) * P:(t % 4) * P + P], o[:, i, :],
                                            start=(i == 0), stop=(i == PAIRS - 1))
                    done(ins)
                pe.wait_ge(gates_ready, KD)
                for n in range(4):
                    b = begin(f"out{n}")
                    arrived(pe, "out", n)
                    w = chunk("out", n).rearrange("p (k n) -> p k n", k=KD)
                    for m in range(M):
                        for k in range(KD):
                            ins = pe.matmul(b[:, m * CH:(m + 1) * CH], mT[:, k, m * P:(m + 1) * P], w[:, k, :],
                                            start=(k == 0), stop=(k == KD - 1))
                    done(ins)
                pe.wait_ge(diag_ready, 2)
                for n in range(2):
                    b = begin(f"gb{n + 2}")
                    done(pe.matmul(b[:, :], ones[:, :], diag2[:, n * 512:n * 512 + 512], start=True, stop=True))
                pe.wait_ge(x1n_ready, 1)
                for n in range(4):
                    turn_x(f"x1T{n}", n, x1n)
                drained(pe, "x1T3")
                pe.wait_ge(router_in, 64)
                b = begin("rt")
                for m in range(M):
                    for k in range(KD):
                        ins = pe.matmul(b[:, m * 36:(m + 1) * 36], h2T[:, k, m * P:(m + 1) * P], wr[:, k, :],
                                        start=(k == 0), stop=(k == KD - 1))
                done(ins)
                pe.wait_ge(sel_ready, 1)
                b = begin("pos")
                E = EXPERTS
                pe.matmul(b[:, 0:E], tri[:, :], sel[:, 0, 0:E], start=True, stop=True)
                pe.matmul(b[:, E:2 * E], tri[:, :], sel[:, 1, 0:E], start=True, stop=False)
                pe.matmul(b[:, E:2 * E], ones[:, :], sel[:, 0, 0:E], start=False, stop=True)
                pe.matmul(b[:, 2 * E:3 * E], ones[:, :], sel[:, 0, 0:E], start=True, stop=False)
                done(pe.matmul(b[:, 2 * E:3 * E], ones[:, :], sel[:, 1, 0:E], start=False, stop=True))

                def gather(count, buf, first=False):
                    pe.wait_ge(pick_ready, count + 1)
                    if not first:
                        pe.wait_ge(xgT_act, count)
                        pe.wait_ge(xgT_dve, count)
                    for half in range(2):
                        for k in range(4):
                            kk = 4 * half + k
                            for n, (src, m) in enumerate(((s, m) for s in (x1hi, x1lo) for m in range(M))):
                                ins = pe.matmul(bank[half][:, k * P:(k + 1) * P], src[:, m, kk * P:(kk + 1) * P],
                                                pick[buf][:, m, :], start=(n == 0), stop=(n == 3))
                        ins.then_inc(xg_done, 1)

                def gate_up(ex, it_count, j4, j, buf):
                    for q in range(2):
                        pe.wait_ge(mlanded[PIECES * j4 + q], 16 * (it_count + 1))
                    pe.wait_ge(aT_ready, ex + 1)
                    for q in range(2):
                        w = mslot(PIECES * j4 + q).rearrange("p (k n) -> p k n", k=KD)
                        for t in range(2):
                            for k in range(KD):
                                ins = pe.matmul(bank[2 + j][:, (2 * q + t) * SLOTS:(2 * q + t + 1) * SLOTS], w[:, k, t * P:(t + 1) * P],
                                                xgT[buf][:, k, j * SLOTS:(j + 1) * SLOTS], start=(k == 0), stop=(k == KD - 1))
                    ins.then_inc(gu_done, 1)

                def down(ex, it_count, j4, j):
                    pe.wait_ge(mlanded[PIECES * j4 + 2], 16 * (it_count + 1))
                    pe.wait_ge(aT_ready, ex + 3)
                    w = mslot(PIECES * j4 + 2).rearrange("p (k n) -> p k n", k=2)
                    for n in range(2):
                        for t in range(2):
                            ins = pe.matmul(bank[4 + n][j * SLOTS:(j + 1) * SLOTS, :], aT[j][:, t, :], w[:, t, n * 512:n * 512 + 512],
                                            start=(t == 0), stop=(t == 1))
                    ins.then_inc(down_done, 1)

                def rounds(r, late=False):
                    gather(r * (EXPERTS // 2 + 1), 0, first=not late)
                    with pe.Fori(0, EXPERTS // 4) as it:
                        its = r * (EXPERTS // 4) + it
                        for b in range(2):
                            pair = r * (EXPERTS // 2) + it * 2 + b
                            pe.wait_ge(xgT_act, pair + r + 1)
                            pe.wait_ge(xgT_dve, pair + r + 1)
                            for j in range(2):
                                gate_up(pair * 2 + j, its, 2 * b + j, j, b)
                            pe.wait_ge(sc_drained, 4 * pair + 3)
                            pb = bank[6 + (5 * b) % 2]
                            for m in range(M):
                                pe.transpose(pb[:, m * P:(m + 1) * P], pick[b][:, m, :].bitcast(F32), ident[:, :])
                            for m in range(M):
                                ins = pe.matmul(pb[:, M * P:M * P + 1], pickw[b][:, m, :], ones[:, 0:1], start=(m == 0), stop=(m == M - 1))
                            ins.then_inc(put_done, 1)
                            for j in range(2):
                                down(pair * 2 + j, its, 2 * b + j, j)
                            gather(pair + r + 1, 1 - b)
                            pe.wait_ge(ylo_ready, pair + 1)
                            pe.wait_ge(put_ready, pair + 1)
                            for n in range(4):
                                m, half = n // 2, n % 2
                                pe.wait_ge(sc_drained, 4 * pair + 3 + n if n > 1 else 4 * pair + 4)
                                for q, y in enumerate((yhi, ylo)):
                                    ins = pe.matmul(bank[6 + (5 * b + 1 + n) % 2][:, :], putT[:, m * P:(m + 1) * P],
                                                    y[:, half * 512:half * 512 + 512], start=(q == 0), stop=(q == 1))
                                ins.then_inc(sc_done, 1)

                drained(pe, "pos")
                pe.wait_ge(hi_ready, 1)
                pe.wait_ge(lo_ready, 1)
                pe.wait_ge(most_ready, 1)
                count = pe.value_load(mosti[0:1, 0:1], min_val=0, max_val=S)
                rounds(0)
                with pe.Fori(1, ROUNDS) as r:
                    with pe.If(count > r * SLOTS):
                        rounds(r, late=True)


def overlap(src):
    v = src[:, 0:CMP_TILES].unsqueeze(2).to_broadcast([P, CMP_TILES, NCMP]).copy()
    ap = [list(d) for d in v.ap]
    ap[-1][0] = CMP_STRIDE // 2
    return bass.AP(tensor=v.tensor, offset=v.offset, ap=ap)


_INS = ["x", "c", "positions", "w_ada", "b_ada", "g_norm1", "w_in", "g_kv_latent", "w_kv_up", "pe_cmp_k", "pe_cmp_v",
        "w_cmp1_k", "w_cmp2_k", "w_cmp1_v", "w_cmp2_v", "w_up_a", "w_up_b", "w_out", "g_norm2", "w_router_group",
        "b_router_group", "w_router_expert", "b_router_expert", "w_expert_gate", "w_expert_up", "w_expert_down", "g_final"]
_STRIP = {"w_ada", "w_in", "w_cmp1_k", "w_cmp1_v", "w_up_a", "w_up_b", "w_out", "w_expert_gate", "w_expert_up", "w_expert_down"}


def kernel(**inputs):
    import concourse.bacc as bacc
    from concourse.bass_utils import run_bass_kernel_spmd

    nc = bacc.Bacc("TRN2", target_bir_lowering=False, num_devices=1)
    arrays, args = {}, {}
    for name in _INS:
        v = np.ascontiguousarray(inputs[name])
        arrays[f"in_{name}_dram"] = v
        ap = nc.dram_tensor(f"in_{name}_dram", v.shape, mybir.dt.from_np(v.dtype), kind="ExternalInput").ap()
        args[name] = ap[0] if name in _STRIP else ap
    out = nc.dram_tensor("out_0_dram", (1, S, D), F32, kind="ExternalOutput").ap()
    layer_kernel(nc, **args, out=out)
    r = run_bass_kernel_spmd(nc, [arrays], core_ids=[0])
    return r.results[0]["out_0_dram"]
```

```python
from contextlib import ExitStack

import numpy as np

import concourse.bass as bass
from concourse import mybir

F32 = mybir.dt.float32
F32R = mybir.dt.float32r
I32 = mybir.dt.int32
ALU = mybir.AluOpType
ACT = mybir.ActivationFunctionType
AX = mybir.AxisListType.X

P = 128
D = 1024
S = 256
KD = D // P
M = S // P
HD = 64
HEADS = 8
PAIRS = HEADS // 2
ROT = HD // 4
RANK = 128
IDX_HEADS, IDX_DIM = 8, 32
IDX_ROT = IDX_DIM // 4
TOPK = S // 4
GROUPS = 2
CMP_LEN, CMP_STRIDE, CMP_HIDDEN = 32, 16, 256
NCMP = S // CMP_STRIDE - CMP_LEN // CMP_STRIDE + 1
CMP_TILES = CMP_LEN * HD // P
EXPERTS, EXPERT_GROUPS = 32, 4
PER_GROUP = EXPERTS // EXPERT_GROUPS
FF = 256
THETA = 500000.0
EPS = 1e-6
NEG = -1e30
TINY = 1e-30
SCALE = HD ** -0.5

QA = 0
KV = QA + HEADS * HD
IQ = KV + RANK
IW = IQ + IDX_HEADS * IDX_DIM
IK = IW + IDX_HEADS
QB = IK + IDX_DIM
KC = QB + HEADS * HD
VC, KS, VS, KW, VW = (KC + n * GROUPS * HD for n in range(1, 6))
BR = VW + GROUPS * HD
MG = BR + 3 * HEADS
WIN_COLS = MG + 2 * D

CH = 256
WINC = [(c, min(c + CH, MG)) for c in range(0, MG, CH)]
RING = 9
SLOTS = 64
ROUNDS = S // SLOTS
MRING = 12
PIECES = 3

R_C, R_BADA, R_G1, R_G2, R_GKV, R_PEK, R_PEV, R_END = 0, 8, 56, 64, 72, 73, 89, 105

UNITS = [("sel", 0), ("win", 0), ("sel", 1), ("win", 1), ("dsa", 0), ("dsa", 1)]


def product_order():
    act, dve = "act", "dve"

    def score(kind, m):
        return [(f"S{kind}{m}_{n}", dve) for n in range(2 * (m + 1))]

    def turn(kind, m):
        return [(f"T{kind}{m}_{n}", act) for n in range(2 * (m + 1))]

    def mg(n):
        return [(f"mg{n}", act)]

    o = [("rows", dve), ("ada0", dve), ("ada1", dve), ("adt0", dve), ("adt1", dve)]
    o += [(f"xT{n}", dve) for n in range(4)]
    o += [(f"win{n}", act) for n in range(len(WINC))]
    o += mg(0) + [("kvT", dve)] + mg(1) + [(f"kvp{n}", act) for n in range(4)]
    o += [("iqT", act), ("ikT", act), ("cmpx", act), ("qbT0", act), ("qbT1", act), ("ksT", act), ("kwT", act)]
    o += mg(2) + [(f"il{n}", act) for n in range(8)]
    o += [("cmp1", dve)] + mg(3) + [("cmpT", dve), ("cmp2", dve), ("sc0", dve), ("sc1", dve)]
    o += score("sel", 0) + score("win", 0) + mg(4)
    o += [(f"pcT{n}", act) for n in range(4)]
    o += [("qaT0", act), ("qaT1", act), ("kaT0", act), ("kaT1", act)]
    o += turn("sel", 0) + score("sel", 1) + mg(5) + turn("win", 0) + score("win", 1) + mg(6)
    o += [("PVb0", act)] + turn("sel", 1) + score("dsa", 0) + mg(7) + turn("win", 1) + [("PVb1", act)]
    o += score("dsa", 1) + [("ada2", dve)] + turn("dsa", 0) + [("adt2", dve), ("PVa0", act), ("ada3", dve)]
    o += turn("dsa", 1) + [("adt3", dve), ("PVa1", act), ("ada4", dve), ("gb0", act), ("gb1", act), ("adt4", dve)]
    o += [("ada5", dve)]
    o += [("up0", dve), ("adt5", dve)] + [(f"up{n}", dve) for n in range(1, KD)] + [(f"out{n}", dve) for n in range(4)]
    o += [("gb2", act), ("gb3", act)] + [(f"x1T{n}", dve) for n in range(4)] + [("rt", dve), ("pos", dve)]
    return o


ORDER = product_order()
INDEX = {name: n for n, (name, _) in enumerate(ORDER)}


def chunk_order():
    o = []
    for name, _ in ORDER:
        if name[:3] == "ada":
            o += [(name, "ada", 4 * int(name[3:]) + j) for j in range(4)]
        elif name[:3] == "win":
            o.append((name, "win", int(name[3:])))
        elif name[:2] == "mg":
            o.append((name, "mg", int(name[2:])))
        elif name == "cmp1":
            o += [(name, kind, j) for j in range(2) for kind in ("cmp1k", "cmp1v")]
        elif name in ("up0", "up4"):
            n = int(name[2:])
            o += [(f"up{n + 3}", "upa", n // 4), (f"up{n + 3}", "upb", n // 4)]
        elif name[:3] == "out":
            o.append((name, "out", int(name[3:])))
    return o


CHUNKS = chunk_order()
CHUNK_AT = {(kind, n): at for at, (_, kind, n) in enumerate(CHUNKS)}


def layer_kernel(nc, x, c, positions, w_ada, b_ada, g_norm1, w_in, g_kv_latent, w_kv_up, pe_cmp_k,
                 pe_cmp_v, w_cmp1_k, w_cmp2_k, w_cmp1_v, w_cmp2_v, w_up_a, w_up_b, w_out, g_norm2,
                 w_router_group, b_router_group, w_router_expert, b_router_expert, w_expert_gate,
                 w_expert_up, w_expert_down, g_final, out):
    base = (nc.sbuf_base + 63) // 64 * 64
    top = nc.sbuf_usable_end

    class Map:

        def __init__(self, at):
            self.at = at

        def __call__(self, name, shape, dt=F32):
            size = int(np.prod(shape[1:])) * 4
            t = place(name, shape, dt, self.at)
            self.at += (size + 31) // 32 * 32
            assert self.at <= top, (name, self.at, top)
            return t

    def place(name, shape, dt, at):
        return nc.alloc_sbuf_tensor_at(name, shape, dt, offset=at)

    keep = Map(base)
    ring = keep("ring", [P, RING, KD * CH])
    ident = keep("ident", [P, P])
    ones = keep("ones", [P, P])
    tri = keep("tri", [P, P])
    iota_slot = keep("iota_slot", [P, SLOTS])
    iota8 = keep("iota8", [P, 8])
    cols = keep("cols", [P, R_END])
    modT = keep("modT", [P, 48])
    A1 = keep("A1", [P, KD])
    A2 = keep("A2", [P, KD])
    condT = keep("condT", [P, KD])
    condB = keep("condB", [P, KD, 32])
    adaR = [keep(f"adaR{n}", [P, CH]) for n in range(2)]
    tiny = keep("tiny", [P, 64])
    wr = keep("wr", [P, KD, 36])
    brow = keep("brow", [P, 36])
    x1_at = keep.at
    x1 = keep("x1", [P, M, D])

    a = Map(keep.at)
    hT = place("hT", [P, KD, S], F32, x1_at)
    xs = a("xs", [P, M, D])
    kvx = place("kvx", [P, M, D], F32, a.at - 8192)
    xp = a("xp", [P, M, MG])
    gT = a("gT", [P, 2 * KD, S])
    qaT = a("qaT", [P, PAIRS, S])
    kaT = a("kaT", [P, PAIRS, S])
    qbT = a("qbT", [P, PAIRS, S])
    ksT = a("ksT", [P, GROUPS, S])
    kwT = a("kwT", [P, GROUPS, S])
    iqT = a("iqT", [P, 2, S])
    ikT = a("ikT", [P, S])
    probs_at = [a.at, a.at + 8192]
    probs = [a("probs0", [P, HEADS, S]), a("probs1", [P, HEADS, S])]
    pT_at = [a.at, a.at + 8192]
    pT = [a("pT0", [P, 2 * HEADS, P]), a("pT1", [P, 2 * HEADS, P])]
    oaT = a("oaT", [P, PAIRS, S])
    obT = a("obT", [P, PAIRS, S])
    cbias = a("cbias", [P, M, S])
    abias = a("abias", [P, M, S])
    pcT = a("pcT", [P, M * HEADS, P])
    smc = a("smc", [P, M, HEADS, NCMP])
    kcT = a("kcT", [P, GROUPS * NCMP])
    vcs = a("vcs", [P, GROUPS, HD])
    w2 = a("w2", [P, 2, 2, HD])
    cbc = a("cbc", [P, M, NCMP])
    cmk = a("cmk", [P, M, NCMP])
    trig = a("trig", [P, 12, M * 8])
    c16 = a("c16", [P, 2, M, ROT])
    c8 = a("c8", [P, 2, M, IDX_ROT])
    posi = a("posi", [P, M], I32)
    gates = a("gates", [P, M, 3 * HEADS])
    stats = a("stats", [P, 12, HEADS])
    w_kv = place("w_kv", [P, 2 * HEADS * HD], F32, probs_at[1])
    junk = place("junk", [P, D], F32, probs_at[0])
    rows = place("rows", [P, P], F32, pT_at[0] + 4096)
    relu = [place(f"relu{m}", [P, HEADS, S], F32, probs_at[m]) for m in range(M)]
    cx = place("cx", [P, 2, GROUPS, P], F32, pT_at[0])
    flat = place("flat", [P, 2, CMP_TILES, GROUPS * NCMP], F32, pT_at[0] + 4096)
    kdup = place("kdup", [P, M, 5, P], F32, pT_at[1])
    hid = place("hid", [P, CMP_HIDDEN], F32, pT_at[1])
    hth = place("hth", [P, CMP_HIDDEN], F32, pT_at[1] + 1024)
    hidT = place("hidT", [P, 2, 96], F32, pT_at[1] + 2048)
    iscore = place("iscore", [P, M, S], F32, pT_at[0])
    iwork = place("iwork", [P, M, S], F32, pT_at[0] + 2048)
    ropeA = a("ropeA", [P, M, 10, ROT])
    ropeB = a("ropeB", [P, M, 10, ROT])
    kvn = place("kvn", [P, M, RANK], F32, pT_at[1] + 7168)
    kvnT = place("kvnT", [P, S], F32, probs_at[0] + 4096)
    xr = place("xr", [P, M, D], F32, probs_at[0])
    mT = place("mT", [P, KD, S], F32, probs_at[1])
    gt1bc = place("gt1bc", [P, D], F32, pT_at[0])
    diag = place("diag", [P, D], F32, pT_at[0] + 4096)
    tmp_up = place("tmp_up", [P, 2, S], F32, pT_at[1])

    e = Map(keep.at)
    extra = e("extra", [P, MRING - RING, KD * CH])
    h2T = e("h2T", [P, KD, S])
    x1n = e("x1n", [P, M, D])
    x1hi = e("x1hi", [P, M, D], F32R)
    x1lo = e("x1lo", [P, M, D], F32R)
    acc = e("acc", [P, M, D])
    gt2bc = e("gt2bc", [P, D])
    gfbc = e("gfbc", [P, D])
    diag2 = e("diag2", [P, D])
    xgT = [e(f"xgT{n}", [P, KD, 2 * SLOTS]) for n in range(2)]
    pick = [e(f"pick{n}", [P, M, 2 * SLOTS], F32R) for n in range(2)]
    pickw = [e(f"pickw{n}", [P, M, 2 * SLOTS]) for n in range(2)]
    putT = [e(f"putT{n}", [P, M * P], F32R) for n in range(2)]
    yw = [e(f"yw{n}", [P, 1]) for n in range(2)]
    thg = e("thg", [P, FF])
    sig = e("sig", [P, FF])
    act_rows = e("act_rows", [P, FF])
    aT = e("aT", [P, 2, 2 * SLOTS])
    yhi = e("yhi", [P, D], F32R)
    ylo = e("ylo", [P, D], F32R)
    route = e("route", [P, M, 36])
    r4 = e("r4", [P, 6, M, EXPERT_GROUPS])
    r8 = e("r8", [P, 12, M, PER_GROUP])
    r32 = e("r32", [P, M, EXPERT_GROUPS, PER_GROUP])
    r1 = e("r1", [P, 20, M])
    NCOL = EXPERTS + 2
    comb = e("comb", [P, M, NCOL])
    sel = e("sel", [P, M, NCOL])
    slot = e("slot", [P, M, NCOL])
    most = e("most", [P, 1])
    mosti = e("mosti", [P, 1], I32)

    with ExitStack() as ctx:
        bank = [ctx.enter_context(nc.psum_tensor(f"bank{n}", [P, 512], F32)) for n in range(8)]

        def sem(name):
            return ctx.enter_context(nc.semaphore(name))

        x_in = sem("x_in")
        rows_in = sem("rows_in")
        pos_in = sem("pos_in")
        kv_w_in = sem("kv_w_in")
        cmp_w_in = sem("cmp_w_in")
        router_in = sem("router_in")
        x_again = sem("x_again")
        gf_in = sem("gf_in")
        landed = [sem(f"landed{n}") for n in range(RING)]
        consts = sem("consts")
        product_done = sem("product_done")
        act_drained = sem("act_drained")
        dve_drained = sem("dve_drained")
        act_step = sem("act_step")
        dve_step = sem("dve_step")
        tanh_c = sem("tanh_c")
        cond_ready = sem("cond_ready")
        squares = sem("squares")
        recip_ms = sem("recip_ms")
        rms_ready = sem("rms_ready")
        xn_ready = sem("xn_ready")
        angles = sem("angles")
        trig_ready = sem("trig_ready")
        tanh_br = sem("tanh_br")
        kvn_ready = sem("kvn_ready")
        roped = sem("roped")
        flat_ready = sem("flat_ready")
        tanh_hid = sem("tanh_hid")
        hid_ready = sem("hid_ready")
        cmp_shift = sem("cmp_shift")
        cmp_exp = sem("cmp_exp")
        cmp_probs = sem("cmp_probs")
        unit_max = sem("unit_max")
        unit_exp = sem("unit_exp")
        unit_probs = sem("unit_probs")
        diag_ready = sem("diag_ready")
        gates_ready = sem("gates_ready")
        x1n_ready = sem("x1n_ready")
        hi_ready = sem("hi_ready")
        lo_ready = sem("lo_ready")
        rt_shift = sem("rt_shift")
        rt_exp = sem("rt_exp")
        sel_ready = sem("sel_ready")
        most_ready = sem("most_ready")
        mlanded = [sem(f"mlanded{n}") for n in range(MRING)]
        pick_ready = sem("pick_ready")
        xg_done = sem("xg_done")
        xgT_act = sem("xgT_act")
        xgT_dve = sem("xgT_dve")
        gu_done = sem("gu_done")
        tanh_g = sem("tanh_g")
        a_ready = sem("a_ready")
        turned = sem("turned")
        aT_ready = sem("aT_ready")
        put_done = sem("put_done")
        put_ready = sem("put_ready")
        down_done = sem("down_done")
        yhi_ready = sem("yhi_ready")
        ylo_ready = sem("ylo_ready")
        sc_done = sem("sc_done")
        sc_drained = sem("sc_drained")
        silu_step = sem("silu_step")
        mo_step = sem("mo_step")
        result = sem("result")
        stored = sem("stored")

        NCONST = 9

        def drains_until(name, engine):
            return sum(1 for _, who in ORDER[:INDEX[name] + 1] if who == engine)

        def made(eng, name):
            eng.wait_ge(product_done, INDEX[name] + 1)

        def drained(eng, name):
            who = ORDER[INDEX[name]][1]
            eng.wait_ge(act_drained if who == "act" else dve_drained, drains_until(name, who))

        def bank_of(name):
            return bank[INDEX[name] % 8]

        class Steps:

            def __init__(self, eng, s):
                self.eng, self.s, self.n = eng, s, 0

            def do(self, ins):
                ins.then_inc(self.s, 1)
                self.n += 1

            def settle(self):
                self.eng.wait_ge(self.s, self.n)

        def chunk(kind, n):
            return ring[:, CHUNK_AT[kind, n] % RING, :]

        def arrived(eng, kind, n):
            at = CHUNK_AT[kind, n]
            eng.wait_ge(landed[at % RING], 16 * (at // RING + 1))

        def chunk_source(kind, n):
            if kind == "ada":
                return w_ada[:, n * CH:(n + 1) * CH].rearrange("(k p) n -> p k n", p=P)
            if kind == "win":
                lo, hi = WINC[n]
                return w_in[:, lo:hi].rearrange("(k p) n -> p k n", p=P)
            if kind == "mg":
                return w_in[:, MG + n * CH:MG + (n + 1) * CH].rearrange("(k p) n -> p k n", p=P)
            if kind in ("cmp1k", "cmp1v"):
                w = w_cmp1_k if kind == "cmp1k" else w_cmp1_v
                return w[n * D:(n + 1) * D, :].rearrange("(k p) n -> p k n", p=P)
            if kind in ("upa", "upb"):
                w = w_up_a if kind == "upa" else w_up_b
                return w[:, n * 512:(n + 1) * 512].rearrange("(k p) n -> p k n", p=P)
            return w_out[:, n * CH:(n + 1) * CH].rearrange("(k p) n -> p k n", p=P)

        def head_slot(h):
            return (h % 2) * PAIRS + h // 2

        first = len(CHUNKS) % RING
        assert first == RING - 1
        MSLOTS = [0, 1, RING - 1, 2, 3, 4, 5, 6, 7]

        def mslot(n):
            return ring[:, MSLOTS[n], :] if n < RING else extra[:, n - RING, :]

        def gate_up_weights(j4, k):
            t, at = (ring, MSLOTS[PIECES * j4]) if j4 < 3 else (extra, 0)
            return t[:, at:at + 2, k * CH:(k + 1) * CH]

        with nc.Block() as block:

            @block.sync
            def _(sp):
                sp.dma_start(xs[:, :, :], x[0].rearrange("(m p) d -> p m d", p=P)).then_inc(x_in, 16)
                for at, (_, kind, n) in enumerate(CHUNKS):
                    if kind == "upa" and n == 0:
                        made(sp, "Tdsa0_1")
                        sp.dma_start(xr[:, :, :], x[0].rearrange("(m p) d -> p m d", p=P)).then_inc(x_again, 16)
                    if at >= RING:
                        made(sp, CHUNKS[at - RING][0])
                    src = chunk_source(kind, n)
                    dst = chunk(kind, n)[:, 0:src.shape[1] * src.shape[2]]
                    sp.dma_start(dst.rearrange("p (k n) -> p k n", k=src.shape[1]), src).then_inc(landed[at % RING], 16)

                def expert(i, j, pieces_free):
                    for q in (2, 0, 1):
                        n = PIECES * j + q
                        pieces_free(q, n)
                        if q < 2:
                            w = w_expert_gate if q == 0 else w_expert_up
                            src = w[bass.ds(i, 1)].rearrange("o (k p) n -> p (o k) n", p=P)
                            dst = mslot(n).rearrange("p (k n) -> p k n", k=KD)
                        else:
                            src = w_expert_down[bass.ds(i, 1)].rearrange("o (k p) n -> p (o k) n", p=P)
                            dst = mslot(n).rearrange("p (k n) -> p k n", k=2)
                        sp.dma_start(dst, src).then_inc(mlanded[n], 16)

                def first_free(q, n):
                    if n < RING:
                        at = MSLOTS[n]
                        made(sp, CHUNKS[max(c for c in range(len(CHUNKS)) if c % RING == at)][0])
                    elif n == RING + 2:
                        drained(sp, "out3")

                for j in range(4):
                    expert(j, j, first_free)

                def stream(r, first):
                    with sp.Fori(first, EXPERTS // 4) as it:
                        for j in range(4):
                            done = r * (EXPERTS // 2) + it * 2 + (j // 2 - 1)

                            def free(q, n):
                                if q == 0:
                                    sp.wait_ge(gu_done, done)
                                elif q == 2:
                                    sp.wait_ge(down_done, done)
                            expert(it * 4 + j, j, free)

                stream(0, 1)
                sp.wait_ge(most_ready, 1)
                count = sp.value_load(mosti[0:1, 0:1], min_val=0, max_val=S)
                with sp.Fori(1, ROUNDS) as r:
                    with sp.If(count > r * SLOTS):
                        stream(r, 0)

            @block.gpsimd
            def _(g):
                g.memset(ident[:, :], 0.0).then_inc(consts, 1)
                g.memset(ones[:, :], 1.0).then_inc(consts, 1)
                g.memset(tri[:, :], 1.0).then_inc(consts, 1)
                g.memset(cbias[:, :, :], 0.0).then_inc(consts, 1)
                g.memset(cbc[:, :, :], 0.0).then_inc(consts, 1)
                g.memset(cmk[:, :, :], 1.0).then_inc(consts, 1)
                g.iota(iota_slot[:, :], [[1, SLOTS]], base=0, channel_multiplier=0,
                       allow_small_or_imprecise_dtypes=True).then_inc(consts, 1)
                g.iota(iota8[:, :], [[1, 8]], base=0, channel_multiplier=0,
                       allow_small_or_imprecise_dtypes=True).then_inc(consts, 1)
                g.wait_ge(consts, 8)
                g.affine_select(out=ident[:, :], in_=ident[:, :], compare_op=ALU.not_equal, fill=1.0, base=0,
                                pattern=[[-1, P]], channel_multiplier=1).then_inc(consts, 1)
                g.affine_select(out=tri[:, :], in_=tri[:, :], compare_op=ALU.is_gt, fill=0.0, base=0,
                                pattern=[[1, P]], channel_multiplier=-1).then_inc(consts, 1)
                g.affine_select(out=cbias[:, :, :], in_=cbias[:, :, :], compare_op=ALU.is_ge, fill=NEG, base=0,
                                pattern=[[P, M], [-1, S]], channel_multiplier=1).then_inc(consts, 1)
                for t, fill in ((cbc, NEG), (cmk, 0.0)):
                    g.affine_select(out=t[:, :, :], in_=t[:, :, :], compare_op=ALU.is_ge, fill=fill,
                                    base=-(CMP_LEN - 1), pattern=[[P, M], [-CMP_STRIDE, NCMP]],
                                    channel_multiplier=1).then_inc(consts, 1)

            ALL_CONSTS = 8 + 5

            @block.scalar
            def _(act):
                step = Steps(act, act_step)
                for lo, src in ((R_C, c.rearrange("a (k p) -> (a k) p", p=P)),
                                (R_BADA, b_ada.rearrange("a (k p) -> (a k) p", p=P)),
                                (R_G1, g_norm1.rearrange("a (k p) -> (a k) p", p=P)),
                                (R_G2, g_norm2.rearrange("a (k p) -> (a k) p", p=P)),
                                (R_GKV, g_kv_latent),
                                (R_PEK, pe_cmp_k[0].rearrange("(j e) d -> j (e d)", e=2)),
                                (R_PEV, pe_cmp_v[0].rearrange("(j e) d -> j (e d)", e=2))):
                    act.dma_start(rows[lo:lo + src.shape[0], :], src).then_inc(rows_in, 16)
                act.dma_start(posi[:, :], positions[0].rearrange("(m p) -> p m", p=P), allow_slow_non_contiguous=True).then_inc(pos_in, 16)
                act.dma_start(w_kv[:, :], w_kv_up[0]).then_inc(kv_w_in, 16)
                for n, w in enumerate((w_cmp2_k, w_cmp2_v)):
                    act.dma_start(w2[:, n, :, :], w[0].rearrange("(t p) d -> p t d", p=P)).then_inc(cmp_w_in, 16)
                act.dma_start(wr[:, :, 0:EXPERT_GROUPS], w_router_group[0].rearrange("(k p) n -> p k n", p=P)).then_inc(router_in, 16)
                act.dma_start(wr[:, :, EXPERT_GROUPS:], w_router_expert[0].rearrange("(k p) n -> p k n", p=P)).then_inc(router_in, 16)
                act.dma_start(brow[:, 0:EXPERT_GROUPS], b_router_group[0].partition_broadcast(P)).then_inc(router_in, 16)
                act.dma_start(brow[:, EXPERT_GROUPS:], b_router_expert[0].partition_broadcast(P)).then_inc(router_in, 16)

                def root(n, t):
                    act.wait_ge(recip_ms, n)
                    act.activation(t, t, ACT.Sqrt).then_inc(rms_ready, 1)

                drained(act, "rows")
                act.activation(condT[:, :], cols[:, R_C:R_C + KD], ACT.Tanh, scale=0.5).then_inc(tanh_c, 1)
                act.wait_ge(x_in, 16)
                for m in range(M):
                    if m:
                        step.settle()
                    ins = act.activation(junk[:, :], xs[:, m, :], ACT.Square, accum_out=tiny[:, m:m + 1])
                    if m == M - 1:
                        ins.then_inc(squares, 1)
                    else:
                        step.do(ins)
                root(1, tiny[:, 0:M])
                act.wait_ge(angles, 1)
                act.activation(trig[:, 10:12, :], trig[:, 8:10, :], ACT.Sin).then_inc(trig_ready, 1)

                def copy_out(name, dst, src):
                    made(act, name)
                    act.activation(dst, src, ACT.Copy).then_inc(act_drained, 1)

                def win(n):
                    lo, hi = WINC[n]
                    w = hi - lo
                    copy_out(f"win{n}", xp[:, :, lo:hi], bank_of(f"win{n}")[:, 0:M * w].rearrange("p (m n) -> p m n", m=M))

                def mg(n):
                    made(act, f"mg{n}")
                    act.activation(gT[:, 2 * n:2 * n + 2, :], bank_of(f"mg{n}")[:, :].rearrange("p (t n) -> p t n", t=2),
                                   ACT.Tanh, scale=0.5).then_inc(act_drained, 1)

                for n in range(3):
                    win(n)
                drained(act, "win2")
                for m in range(M):
                    if m:
                        step.settle()
                    ins = act.activation(junk[:, 0:RANK], xp[:, m, KV:KV + RANK], ACT.Square, accum_out=tiny[:, 2 + m:3 + m])
                    if m == M - 1:
                        ins.then_inc(squares, 1)
                    else:
                        step.do(ins)
                for n in range(3, len(WINC)):
                    win(n)
                root(2, tiny[:, 2:2 + M])
                drained(act, f"win{len(WINC) - 1}")
                act.activation(gates[:, :, :], xp[:, :, BR:BR + 3 * HEADS], ACT.Tanh, scale=0.5).then_inc(tanh_br, 1)
                mg(0)
                mg(1)
                for n in range(4):
                    m, half = n // 2, n % 2
                    copy_out(f"kvp{n}", kvx[:, m, half * 512:half * 512 + 512], bank_of(f"kvp{n}")[:, :])
                copy_out("iqT", iqT[:, :, :], bank_of("iqT")[:, :].rearrange("p (t n) -> p t n", t=2))
                copy_out("ikT", ikT[:, :], bank_of("ikT")[:, 0:S])
                copy_out("cmpx", cx[:, :, :, :], bank_of("cmpx")[:, :].rearrange("p (a g n) -> p a g n", a=2, g=2))
                for n in range(2):
                    copy_out(f"qbT{n}", qbT[:, 2 * n:2 * n + 2, :], bank_of(f"qbT{n}")[:, :].rearrange("p (t n) -> p t n", t=2))
                copy_out("ksT", ksT[:, :, :], bank_of("ksT")[:, :].rearrange("p (t n) -> p t n", t=2))
                copy_out("kwT", kwT[:, :, :], bank_of("kwT")[:, :].rearrange("p (t n) -> p t n", t=2))
                mg(2)
                for n in range(8):
                    m, r = n // 4, n % 4
                    nk = P * (m + 1)
                    made(act, f"il{n}")
                    act.activation(relu[m][:, r:HEADS:4, 0:nk], bank_of(f"il{n}")[:, 0:2 * nk].rearrange("p (t n) -> p t n", t=2),
                                   ACT.Relu).then_inc(act_drained, 1)
                made(act, "cmp1")
                for lo in (0, HD):
                    act.activation(hth[lo:lo + GROUPS * NCMP, :], bank_of("cmp1")[lo:lo + GROUPS * NCMP, 0:CMP_HIDDEN],
                                   ACT.Tanh, scale=0.5).then_inc(tanh_hid, 1)
                mg(3)
                act.wait_ge(cmp_shift, 1)
                act.activation(smc[:, :, :, :], smc[:, :, :, :], ACT.Exp, scale=SCALE).then_inc(cmp_exp, 1)

                def exps(u):
                    kind, m = UNITS[u]
                    nk = P * (m + 1)
                    act.wait_ge(unit_max, u + 1)
                    p = probs[u % 2]
                    so = 4 * (u % 2)
                    for h in range(HEADS):
                        ins = act.activation(p[:, h, 0:nk], p[:, h, 0:nk], ACT.Exp, bias=stats[:, so + 1, h:h + 1],
                                             accum_out=stats[:, so + 2, h:h + 1])
                    ins.then_inc(unit_exp, 1)

                def turns(u):
                    kind, m = UNITS[u]
                    for n in range(2 * (m + 1)):
                        name = f"T{kind}{m}_{n}"
                        copy_out(name, pT[u % 2][:, 4 * n:4 * n + 4, :], bank_of(name)[:, :].rearrange("p (t n) -> p t n", t=4))

                def pv(name, dst, m):
                    copy_out(name, dst[:, :, m * P:m * P + P], bank_of(name)[:, :].rearrange("p (t n) -> p t n", t=PAIRS))

                exps(0)
                exps(1)
                mg(4)
                for n in range(4):
                    name = f"pcT{n}"
                    made(act, name)
                    act.activation(pcT[0:NCMP, 4 * n:4 * n + 4, :], bank_of(name)[0:NCMP, :].rearrange("p (t n) -> p t n", t=4),
                                   ACT.Copy).then_inc(act_drained, 1)
                for t, name in ((qaT, "qaT"), (kaT, "kaT")):
                    for n in range(2):
                        copy_out(f"{name}{n}", t[:, 2 * n:2 * n + 2, :], bank_of(f"{name}{n}")[:, :].rearrange("p (t n) -> p t n", t=2))
                turns(0)
                exps(2)
                mg(5)
                turns(1)
                exps(3)
                mg(6)
                pv("PVb0", obT, 0)
                turns(2)
                exps(4)
                mg(7)
                turns(3)
                pv("PVb1", obT, 1)
                exps(5)
                turns(4)
                pv("PVa0", oaT, 0)
                turns(5)
                pv("PVa1", oaT, 1)
                for n in range(2):
                    copy_out(f"gb{n}", gt1bc[:, n * 512:n * 512 + 512], bank_of(f"gb{n}")[:, :])
                drained(act, "out3")
                act.dma_start(gfbc[:, :], g_final.partition_broadcast(P)).then_inc(gf_in, 16)
                for n in range(2):
                    copy_out(f"gb{n + 2}", gt2bc[:, n * 512:n * 512 + 512], bank_of(f"gb{n + 2}")[:, :])
                for m in range(M):
                    if m:
                        step.settle()
                    ins = act.activation(h2T[:, 0:4, :].rearrange("p a b -> p (a b)"), x1[:, m, :], ACT.Square, accum_out=tiny[:, 4 + m:5 + m])
                    if m == M - 1:
                        ins.then_inc(squares, 1)
                    else:
                        step.do(ins)
                root(3, tiny[:, 4:4 + M])
                act.wait_ge(x1n_ready, 1)
                act.activation(x1hi[:, :, :], x1n[:, :, :], ACT.Copy).then_inc(hi_ready, 1)
                act.wait_ge(rt_shift, 1)
                act.activation(r4[:, 1, :, :], r4[:, 0, :, :], ACT.Exp).then_inc(rt_exp, 1)
                act.wait_ge(rt_shift, 2)
                act.activation(r1[:, 6, :], r1[:, 5, :], ACT.Exp).then_inc(rt_exp, 1)

                def xg_out(count, buf):
                    act.wait_ge(xg_done, 2 * count + 1)
                    for k in range(4):
                        ins = act.activation(xgT[buf][:, k, :], bank[0][:, k * P:k * P + P], ACT.Identity,
                                             scale=A2[:, k:k + 1], bias=modT[:, 24 + k:25 + k])
                    ins.then_inc(xgT_act, 1)

                def rounds(r, late=False):
                    if late:
                        act.wait_ge(gu_done, r * (EXPERTS // 2))
                    xg_out(r * (EXPERTS // 2 + 1), 0)
                    with act.Fori(0, EXPERTS // 4) as it:
                        for b in range(2):
                            pair = r * (EXPERTS // 2) + it * 2 + b
                            act.wait_ge(gu_done, pair + 1)
                            act.wait_ge(aT_ready, pair + 1)
                            act.activation(thg[:, :], bank[2 + b][:, 0:FF], ACT.Tanh, scale=0.5).then_inc(tanh_g, 1)
                            xg_out(pair + r + 1, 1 - b)
                            act.wait_ge(down_done, pair + 1)
                            act.wait_ge(put_ready, pair + 2)
                            act.wait_ge(sc_drained, 4 * (pair + r) + 8)
                            for n in range(2):
                                ins = act.activation(yhi[:, n * 512:n * 512 + 512], bank[4 + n][:, :], ACT.Copy, scale=yw[b][:, 0:1])
                            ins.then_inc(yhi_ready, 1)

                act.wait_ge(most_ready, 1)
                count = act.value_load(mosti[0:1, 0:1], min_val=0, max_val=S)
                rounds(0)
                with act.Fori(1, ROUNDS) as r:
                    with act.If(count > r * SLOTS):
                        rounds(r, late=True)

                for m in range(M):
                    act.wait_ge(result, m + 1)
                    ins = act.activation(x1n[:, m, :], acc[:, m, :], ACT.Square, accum_out=tiny[:, 6 + m:7 + m])
                    ins.then_inc(squares, 1)
                root(4, tiny[:, 6:6 + M])
                for m in range(M):
                    act.wait_ge(result, M + m + 1)
                    act.dma_start(out[0, m * P:(m + 1) * P, :], x1[:, m, :]).then_inc(stored, 16)
                act.wait_ge(stored, 16 * M)

            @block.vector
            def _(dve):
                step = Steps(dve, dve_step)
                do, settle = step.do, step.settle

                def drain_done(ins):
                    ins.then_inc(dve_drained, 1)

                def mean_square(n, t, width):
                    dve.wait_ge(squares, n)
                    do(dve.tensor_scalar(t, t, 1.0 / width, EPS, ALU.mult, ALU.add))
                    settle()
                    dve.reciprocal(t, t).then_inc(recip_ms, 1)

                made(dve, "rows")
                drain_done(dve.tensor_copy(cols[:, :], bank_of("rows")[:, 0:R_END]))
                mean_square(1, tiny[:, 0:M], D)
                dve.wait_ge(tanh_c, 1)
                do(dve.scalar_tensor_tensor(condT[:, :], condT[:, :], 1.0, cols[:, R_C:R_C + KD], ALU.add, ALU.mult))
                settle()
                dve.tensor_scalar(condB[:, :, :], condT[:, :].unsqueeze(2).to_broadcast([P, KD, 32]), 0.5, None, ALU.mult).then_inc(cond_ready, 1)
                dve.wait_ge(rms_ready, 1)
                for m in range(M):
                    dve.tensor_scalar(xs[:, m, :], xs[:, m, :], tiny[:, m:m + 1], None, ALU.mult).then_inc(xn_ready, 1)

                freq = (THETA ** (-np.arange(8, dtype=np.float32) / 8)).astype(np.float32)
                for n in range(8):
                    do(dve.memset(trig[:, 0, n:M * 8:8], float(freq[n])))
                dve.wait_ge(pos_in, 16)
                do(dve.tensor_copy(stats[:, 0, 0:M], posi[:, :]))
                settle()
                for m in range(M):
                    do(dve.tensor_scalar(trig[:, 1, m * 8:m * 8 + 8], trig[:, 0, m * 8:m * 8 + 8], stats[:, 0, m:m + 1], None, ALU.mult))
                settle()
                magic = 1.5 * 2.0 ** 23
                do(dve.tensor_scalar(trig[:, 2, :], trig[:, 1, :], float(1 / (2 * np.pi)), magic, ALU.mult, ALU.add))
                settle()
                do(dve.tensor_scalar(trig[:, 3, :], trig[:, 2, :], -magic, None, ALU.add))
                settle()
                two_pi = 2 * np.pi
                part1 = 6.28125
                part2 = float(np.float32(np.round((two_pi - part1) * 2 ** 22) / 2 ** 22))
                part3 = float(two_pi - part1 - part2)
                for n, part in enumerate((part1, part2, part3)):
                    do(dve.scalar_tensor_tensor(trig[:, 4 + n, :], trig[:, 3, :], -part, trig[:, 1 if n == 0 else 3 + n, :], ALU.mult, ALU.add))
                    settle()
                lim = float(np.nextafter(np.float32(np.pi), np.float32(0)))
                do(dve.tensor_scalar(trig[:, 8, :], trig[:, 6, :], lim, -lim, ALU.min, ALU.max))
                settle()
                do(dve.scalar_tensor_tensor(trig[:, 7, :], trig[:, 8, :], -1.0, trig[:, 8, :], ALU.mult, ALU.max))
                settle()
                dve.tensor_scalar(trig[:, 9, :], trig[:, 7, :], -1.0, float(np.float32(np.pi / 2)), ALU.mult, ALU.add).then_inc(angles, 1)
                dve.wait_ge(trig_ready, 1)
                for n, row in enumerate((11, 10)):
                    src = trig[:, row, :].rearrange("p (m f) -> p m f", m=M)
                    for half in range(2):
                        do(dve.tensor_copy(c16[:, n, :, half * 8:half * 8 + 8], src))
                        do(dve.tensor_copy(c8[:, n, :, half * 4:half * 4 + 4], src[:, :, 0:8:2]))
                settle()

                def ada(n):
                    made(dve, f"ada{n}")
                    drain_done(dve.tensor_copy(adaR[n % 2][:, :], bank_of(f"ada{n}")[:, 0:CH]))

                def adt(n):
                    made(dve, f"adt{n}")
                    drain_done(dve.tensor_tensor(modT[:, 8 * n:8 * n + 8].rearrange("p (q c) -> p c q", c=2),
                                                 bank_of(f"adt{n}")[:, 0:2 * P].rearrange("p (c q) -> p c q", c=2)[:, :, 0:P:32],
                                                 cols[:, R_BADA + 8 * n:R_BADA + 8 * n + 8].rearrange("p (q c) -> p c q", c=2), ALU.add))

                ada(0)
                ada(1)
                adt(0)
                adt(1)
                drained(dve, "adt1")
                do(dve.scalar_tensor_tensor(A1[:, :], modT[:, 8:16], 1.0, cols[:, R_G1:R_G1 + KD], ALU.add, ALU.mult))
                settle()
                for n in range(4):
                    name = f"xT{n}"
                    made(dve, name)
                    for kk in range(2):
                        k = 2 * n + kk
                        ins = dve.tensor_scalar(hT[:, k, :], bank_of(name)[:, kk * S:kk * S + S], A1[:, k:k + 1],
                                                modT[:, k:k + 1], ALU.mult, ALU.add)
                    drain_done(ins)

                def rotate(xv, heads, table, rot, final=None):
                    half = rot // 2
                    av, bv = ropeA[:, :, 0:heads, 0:rot], ropeB[:, :, 0:heads, 0:rot]
                    cosv = table[:, 0].unsqueeze(2).to_broadcast([P, M, heads, rot])
                    sinv = table[:, 1].unsqueeze(2).to_broadcast([P, M, heads, rot])
                    do(dve.tensor_tensor(av, xv[:, :, :, 0:rot], cosv, ALU.mult))
                    do(dve.tensor_tensor(bv, xv[:, :, :, 0:rot], sinv, ALU.mult))
                    settle()
                    do(dve.tensor_tensor(xv[:, :, :, 0:half], av[:, :, :, 0:half], bv[:, :, :, half:rot], ALU.subtract))
                    ins = dve.tensor_tensor(xv[:, :, :, half:rot], av[:, :, :, half:rot], bv[:, :, :, 0:half], ALU.add)
                    do(ins)
                    settle()

                def heads_of(col, heads, width):
                    return xp[:, :, col:col + heads * width].rearrange("p m (h w) -> p m h w", w=width)

                mean_square(2, tiny[:, 2:2 + M], RANK)
                drained(dve, "win3")
                rotate(heads_of(IQ, IDX_HEADS, IDX_DIM), IDX_HEADS, c8, IDX_ROT)
                rotate(heads_of(IK, 1, IDX_DIM), 1, c8, IDX_ROT)
                for n in range(4):
                    do(dve.tensor_copy(kdup[:, :, 4, n * IDX_DIM:(n + 1) * IDX_DIM], xp[:, :, IK:IK + IDX_DIM]))
                settle()
                dve.wait_ge(rms_ready, 2)
                for m in range(M):
                    dve.tensor_scalar(kvn[:, m, :], xp[:, m, KV:KV + RANK], tiny[:, 2 + m:3 + m], None, ALU.mult).then_inc(kvn_ready, 1)
                drained(dve, f"win{len(WINC) - 1}")
                rotate(heads_of(QB, HEADS + GROUPS, HD), HEADS + GROUPS, c16, ROT)
                for n, col in enumerate((KS, KW)):
                    rotate(heads_of(col, GROUPS, HD), GROUPS, c16, ROT)
                    for twice in range(2):
                        do(dve.tensor_copy(kdup[:, :, 2 * n:2 * n + 2, twice * HD:(twice + 1) * HD], heads_of(col, GROUPS, HD)))
                settle()
                do(dve.memset(tiny[:, 60:61], 0.0))
                settle()
                dve.memset(tiny[:, 61:62], 0.0).then_inc(roped, 1)
                made(dve, "kvT")
                drain_done(dve.tensor_scalar(kvnT[:, :], bank_of("kvT")[:, 0:S], cols[:, R_GKV:R_GKV + 1], None, ALU.mult))
                rotate(heads_of(QA, HEADS, HD), HEADS, c16, ROT)
                dve.wait_ge(tanh_br, 1)
                do(dve.tensor_scalar(gates[:, :, :], gates[:, :, :], 0.5, 0.5, ALU.mult, ALU.add))
                settle()

                drained(dve, "cmpx")
                for n in range(2):
                    pe = cols[:, (R_PEK, R_PEV)[n]:(R_PEK, R_PEV)[n] + CMP_TILES]
                    for gi in range(GROUPS):
                        src = cx[:, n, gi, :]
                        win_ap = overlap(src)
                        ins = dve.tensor_tensor(flat[:, n, :, gi * NCMP:(gi + 1) * NCMP], win_ap,
                                                pe.unsqueeze(2).to_broadcast([P, CMP_TILES, NCMP]), ALU.add)
                        do(ins)
                settle()
                dve.memset(tiny[:, 62:63], 0.0).then_inc(flat_ready, 1)
                drained(dve, "kvp3")
                rotate(kvx[:, :, 0:HEADS * HD].rearrange("p m (h w) -> p m h w", w=HD), HEADS, c16, ROT)
                dve.memset(tiny[:, 61:62], 0.0).then_inc(roped, 1)

                made(dve, "kwT")
                do(dve.memset(hid[:, :], 0.0))
                settle()
                dve.wait_ge(tanh_hid, 2)
                for lo in (0, HD):
                    r = slice(lo, lo + GROUPS * NCMP)
                    ins = dve.scalar_tensor_tensor(hid[r, :], hth[r, :], 1.0, bank_of("cmp1")[r, 0:CMP_HIDDEN], ALU.add, ALU.mult)
                drain_done(ins)
                made(dve, "cmpT")
                drain_done(dve.tensor_copy(hidT[:, :, :], bank_of("cmpT")[:, 0:2 * 96].rearrange("p (t n) -> p t n", t=2)))
                made(dve, "cmp2")
                do(dve.tensor_scalar(kcT[:, :], bank_of("cmp2")[:, 0:GROUPS * NCMP], 0.5, None, ALU.mult))
                drain_done(dve.tensor_scalar(vcs[0:NCMP, :, :], bank_of("cmp2")[0:NCMP, 64:64 + GROUPS * HD].rearrange("p (g d) -> p g d", g=GROUPS),
                                             0.5, None, ALU.mult))
                for par in range(2):
                    made(dve, f"sc{par}")
                    drain_done(dve.tensor_tensor(smc[:, :, par * PAIRS:(par + 1) * PAIRS, :],
                                                 bank_of(f"sc{par}")[:, 0:M * PAIRS * NCMP].rearrange("p (m i c) -> p m i c", m=M, i=PAIRS),
                                                 cbc[:, :, :].unsqueeze(2).to_broadcast([P, M, PAIRS, NCMP]), ALU.add))
                drained(dve, "sc1")
                cmax = stats[:, 8:10, :]
                do(dve.tensor_reduce(cmax, smc[:, :, :, :], AX, ALU.max))
                settle()
                dve.tensor_tensor(smc[:, :, :, :], smc[:, :, :, :], cmax.unsqueeze(3).to_broadcast([P, M, HEADS, NCMP]),
                                  ALU.subtract).then_inc(cmp_shift, 1)
                dve.wait_ge(cmp_exp, 1)
                do(dve.tensor_tensor(smc[:, :, :, :], smc[:, :, :, :], cmk[:, :, :].unsqueeze(2).to_broadcast([P, M, HEADS, NCMP]), ALU.mult))
                settle()
                do(dve.tensor_reduce(cmax, smc[:, :, :, :], AX, ALU.add))
                settle()
                do(dve.tensor_scalar_max(cmax, cmax, TINY))
                settle()
                do(dve.reciprocal(cmax, cmax))
                settle()
                for par in range(2):
                    do(dve.tensor_tensor(cmax[:, :, par * PAIRS:(par + 1) * PAIRS], cmax[:, :, par * PAIRS:(par + 1) * PAIRS],
                                         gates[:, :, 3 * par:3 * HEADS:6], ALU.mult))
                settle()
                dve.tensor_tensor(smc[:, :, :, :], smc[:, :, :, :], cmax.unsqueeze(3).to_broadcast([P, M, HEADS, NCMP]),
                                  ALU.mult).then_inc(cmp_probs, 1)

                def index_select():
                    for m in range(M):
                        nk = P * (m + 1)
                        drained(dve, f"il{4 * m + 3}")
                        for h in range(IDX_HEADS):
                            prev = cbias[:, m, 0:nk] if h == 0 else iscore[:, m, 0:nk]
                            do(dve.scalar_tensor_tensor(iscore[:, m, 0:nk], relu[m][:, h, 0:nk], xp[:, m, IW + h:IW + h + 1],
                                                        prev, ALU.mult, ALU.add))
                            settle()
                        for n in range(TOPK // 8):
                            src = iscore if n == 0 else iwork
                            do(dve.max(stats[:, 11, :], src[:, m, 0:nk]))
                            settle()
                            do(dve.match_replace(iwork[:, m, 0:nk], stats[:, 11, :], src[:, m, 0:nk], -3e38))
                            settle()
                        do(dve.tensor_scalar(iwork[:, m, 0:nk], iwork[:, m, 0:nk], -2e38, NEG, ALU.is_gt, ALU.mult))
                        settle()
                        do(dve.tensor_tensor(abias[:, m, 0:nk], iwork[:, m, 0:nk], cbias[:, m, 0:nk], ALU.min))
                        settle()

                def scores(u):
                    kind, m = UNITS[u]
                    nk = P * (m + 1)
                    per = PAIRS // (m + 1)
                    p, so = probs[u % 2], 4 * (u % 2)
                    mask = (abias if kind == "dsa" else cbias)[:, m, 0:nk]
                    if u >= 2:
                        made(dve, f"T{UNITS[u - 2][0]}{UNITS[u - 2][1]}_{2 * UNITS[u - 2][1] + 1}")
                    for n in range(2 * (m + 1)):
                        name = f"S{kind}{m}_{n}"
                        made(dve, name)
                        for j in range(per):
                            hs = (n % 2) * PAIRS + (n // 2) * per + j
                            ins = dve.tensor_tensor_reduce(p[:, hs, 0:nk], bank_of(name)[:, j * nk:(j + 1) * nk], mask,
                                                           SCALE, -3e38, ALU.add, ALU.max, stats[:, so, hs:hs + 1])
                        drain_done(ins)
                    drained(dve, f"S{kind}{m}_{2 * m + 1}")
                    dve.tensor_scalar(stats[:, so + 1, :], stats[:, so, :], -1.0, None, ALU.mult).then_inc(unit_max, 1)

                def normalise(u):
                    kind, m = UNITS[u]
                    nk = P * (m + 1)
                    p, so = probs[u % 2], 4 * (u % 2)
                    dve.wait_ge(unit_exp, u + 1)
                    do(dve.reciprocal(stats[:, so + 3, :], stats[:, so + 2, :]))
                    settle()
                    if kind != "dsa":
                        branch = 1 if kind == "sel" else 2
                        for par in range(2):
                            s = stats[:, so + 3, par * PAIRS:(par + 1) * PAIRS]
                            do(dve.tensor_tensor(s, s, gates[:, m, 3 * par + branch:3 * HEADS:6], ALU.mult))
                        settle()
                    dve.tensor_tensor(p[:, :, 0:nk], p[:, :, 0:nk], stats[:, so + 3, :].unsqueeze(2).to_broadcast([P, HEADS, nk]),
                                      ALU.mult).then_inc(unit_probs, 1)

                index_select()
                scores(0)
                scores(1)
                normalise(0)
                normalise(1)
                scores(2)
                scores(3)
                normalise(2)
                scores(4)
                normalise(3)
                scores(5)

                normalise(4)
                ada(2)
                adt(2)
                drained(dve, "adt2")
                ada(3)
                normalise(5)
                adt(3)
                ada(4)
                made(dve, "PVa0")
                for k in range(KD):
                    ins = dve.tensor_scalar(diag[:, k * P:(k + 1) * P], ident[:, :], modT[:, 16 + k:17 + k], 0.5, ALU.mult, ALU.mult)
                ins.then_inc(diag_ready, 1)
                adt(4)
                ada(5)
                drained(dve, "adt4")
                do(dve.scalar_tensor_tensor(A2[:, :], modT[:, 32:40], 1.0, cols[:, R_G2:R_G2 + KD], ALU.add, ALU.mult))
                drained(dve, "mg7")
                for t in range(KD):
                    name = f"up{t}"
                    made(dve, name)
                    b = bank_of(name)
                    do(dve.scalar_tensor_tensor(mT[:, t, :], gT[:, t, :], 1.0, b[:, 0:S], ALU.add, ALU.mult))
                    drain_done(dve.scalar_tensor_tensor(tmp_up[:, t % 2, :], gT[:, KD + t, :], 1.0, b[:, S:2 * S], ALU.add, ALU.mult))
                    drained(dve, name)
                    settle()
                    dve.tensor_tensor(mT[:, t, :], mT[:, t, :], tmp_up[:, t % 2, :], ALU.add).then_inc(gates_ready, 1)
                    if t == 0:
                        adt(5)
                drained(dve, "gb1")
                dve.wait_ge(x_again, 16)
                for n in range(4):
                    name = f"out{n}"
                    made(dve, name)
                    xv = x1[:, :, n * CH:(n + 1) * CH]
                    do(dve.tensor_tensor(xv, bank_of(name)[:, :].rearrange("p (m n) -> p m n", m=M),
                                         gt1bc[:, n * CH:(n + 1) * CH].unsqueeze(1).to_broadcast([P, M, CH]), ALU.mult))
                    settle()
                    drain_done(dve.tensor_tensor(xv, xv, xr[:, :, n * CH:(n + 1) * CH], ALU.add))
                drained(dve, "out3")
                for k in range(KD):
                    ins = dve.tensor_scalar(diag2[:, k * P:(k + 1) * P], ident[:, :], modT[:, 40 + k:41 + k], None, ALU.mult)
                ins.then_inc(diag_ready, 1)
                do(dve.memset(acc[:, :, :], 0.0))
                mean_square(3, tiny[:, 4:4 + M], D)
                dve.wait_ge(rms_ready, 3)
                do(dve.tensor_scalar(x1n[:, 0, :], x1[:, 0, :], tiny[:, 4:5], None, ALU.mult))
                dve.tensor_scalar(x1n[:, 1, :], x1[:, 1, :], tiny[:, 5:6], None, ALU.mult).then_inc(x1n_ready, 1)
                for n in range(4):
                    name = f"x1T{n}"
                    made(dve, name)
                    for kk in range(2):
                        k = 2 * n + kk
                        ins = dve.tensor_scalar(h2T[:, k, :], bank_of(name)[:, kk * S:kk * S + S], A2[:, k:k + 1],
                                                modT[:, 24 + k:25 + k], ALU.mult, ALU.add)
                    drain_done(ins)

                made(dve, "rt")
                dve.wait_ge(router_in, 64)
                drain_done(dve.tensor_tensor(route[:, :, :], bank_of("rt")[:, 0:M * 36].rearrange("p (m n) -> p m n", m=M),
                                             brow[:, :].unsqueeze(1).to_broadcast([P, M, 36]), ALU.add))
                drained(dve, "rt")
                dve.wait_ge(hi_ready, 1)
                dve.tensor_tensor(x1lo[:, :, :], x1n[:, :, :], x1hi[:, :, :].bitcast(F32), ALU.subtract).then_inc(lo_ready, 1)

                def bc(v, n):
                    return v.unsqueeze(2).to_broadcast([P, M, n])

                def first_greatest(values, greatest, cand, n):
                    do(dve.tensor_reduce(greatest, values, AX, ALU.max))
                    settle()
                    do(dve.tensor_tensor(cand, values, bc(greatest, n), ALU.is_ge))
                    settle()
                    do(dve.scalar_tensor_tensor(cand, cand, -1000.0, iota8[:, 0:n].unsqueeze(1).to_broadcast([P, M, n]), ALU.mult, ALU.add))
                    settle()
                    do(dve.tensor_reduce(r1[:, 10, :], cand, AX, ALU.min))
                    settle()
                    do(dve.tensor_tensor(cand, cand, bc(r1[:, 10, :], n), ALU.is_equal))
                    settle()

                lg = route[:, :, 0:EXPERT_GROUPS]
                oh4 = r4[:, 2]
                first_greatest(lg, r1[:, 0, :], oh4, EXPERT_GROUPS)
                dve.tensor_tensor(r4[:, 0], lg, bc(r1[:, 0, :], EXPERT_GROUPS), ALU.subtract).then_inc(rt_shift, 1)
                do(dve.tensor_tensor(r32[:, :, :, :], route[:, :, EXPERT_GROUPS:].rearrange("p m (g n) -> p m g n", g=EXPERT_GROUPS),
                                     oh4.unsqueeze(3).to_broadcast([P, M, EXPERT_GROUPS, PER_GROUP]), ALU.mult))
                settle()
                le = r8[:, 0]
                do(dve.tensor_reduce(le, r32[:, :, :, :].rearrange("p m g n -> p m n g"), AX, ALU.add))
                settle()
                first_greatest(le, r1[:, 1, :], r8[:, 1], PER_GROUP)
                do(dve.scalar_tensor_tensor(r8[:, 2], r8[:, 1], -3e38, le, ALU.mult, ALU.add))
                settle()
                first_greatest(r8[:, 2], r1[:, 2, :], r8[:, 3], PER_GROUP)
                dve.tensor_tensor(r1[:, 5, :], r1[:, 2, :], r1[:, 1, :], ALU.subtract).then_inc(rt_shift, 1)
                dve.wait_ge(rt_exp, 2)
                do(dve.tensor_reduce(r1[:, 3, :], r4[:, 1], AX, ALU.add))
                do(dve.tensor_scalar(r1[:, 7, :], r1[:, 6, :], 1.0, 2.0, ALU.add, ALU.mult))
                settle()
                do(dve.tensor_tensor(r1[:, 8, :], r1[:, 3, :], r1[:, 7, :], ALU.mult))
                settle()
                do(dve.reciprocal(r1[:, 8, :], r1[:, 8, :]))
                settle()
                do(dve.tensor_tensor(r1[:, 9, :], r1[:, 8, :], r1[:, 6, :], ALU.mult))
                settle()
                do(dve.tensor_tensor(r8[:, 4], r8[:, 1], bc(r1[:, 8, :], PER_GROUP), ALU.mult))
                do(dve.tensor_tensor(r8[:, 5], r8[:, 3], bc(r1[:, 9, :], PER_GROUP), ALU.mult))
                do(dve.tensor_tensor(r8[:, 6], r8[:, 1], r8[:, 3], ALU.add))
                settle()
                do(dve.tensor_tensor(r8[:, 4], r8[:, 4], r8[:, 5], ALU.add))
                do(dve.memset(comb[:, :, EXPERTS:], 0.0))
                do(dve.memset(slot[:, :, EXPERTS:], -1.0))
                settle()
                four = oh4.unsqueeze(3).to_broadcast([P, M, EXPERT_GROUPS, PER_GROUP])
                do(dve.tensor_tensor(comb[:, :, 0:EXPERTS].rearrange("p m (g n) -> p m g n", g=EXPERT_GROUPS), four,
                                     r8[:, 4].unsqueeze(2).to_broadcast([P, M, EXPERT_GROUPS, PER_GROUP]), ALU.mult))
                dve.tensor_tensor(sel[:, :, 0:EXPERTS].rearrange("p m (g n) -> p m g n", g=EXPERT_GROUPS), four,
                                  r8[:, 6].unsqueeze(2).to_broadcast([P, M, EXPERT_GROUPS, PER_GROUP]), ALU.mult).then_inc(sel_ready, 1)
                made(dve, "pos")
                dve.wait_ge(sel_ready, 1)
                do(dve.tensor_reduce(most[:, :], bank_of("pos")[:, 2 * EXPERTS:3 * EXPERTS], AX, ALU.max))
                settle()
                drain_done(dve.scalar_tensor_tensor(slot[:, :, 0:EXPERTS], bank_of("pos")[:, 0:2 * EXPERTS].rearrange("p (m n) -> p m n", m=M),
                                                    1.0, sel[:, :, 0:EXPERTS], ALU.add, ALU.mult))
                dve.tensor_copy(mosti[:, :], most[:, :]).then_inc(most_ready, 1)
                drained(dve, "pos")
                do(dve.tensor_scalar_add(slot[:, :, 0:EXPERTS], slot[:, :, 0:EXPERTS], -1.0))
                settle()

                def picks(first, buf):
                    for m in range(M):
                        for j in range(2):
                            s = slice(j * SLOTS, (j + 1) * SLOTS)
                            sc = slot[:, m, bass.ds(first + j, 1)]
                            w = comb[:, m, bass.ds(first + j, 1)]
                            dve.tensor_scalar(pick[buf][:, m, s], iota_slot[:, :], sc, None, ALU.is_equal)
                            ins = dve.tensor_scalar(pickw[buf][:, m, s], iota_slot[:, :], sc, w, ALU.is_equal, ALU.mult)
                    ins.then_inc(pick_ready, 1)

                def xg_out(count, buf):
                    dve.wait_ge(xg_done, 2 * count + 2)
                    for k in range(4, KD):
                        ins = dve.tensor_scalar(xgT[buf][:, k, :], bank[1][:, (k - 4) * P:(k - 3) * P], A2[:, k:k + 1],
                                                modT[:, 24 + k:25 + k], ALU.mult, ALU.add)
                    ins.then_inc(xgT_dve, 1)

                def scatter_out(s):
                    for n in range(4):
                        dve.wait_ge(sc_done, 4 * s + n + 1)
                        av = acc[:, n // 2, (n % 2) * 512:(n % 2) * 512 + 512]
                        dve.tensor_tensor(av, bank[6 + n % 2][:, :], av, ALU.add).then_inc(sc_drained, 1)

                def rounds(r, late=False):
                    if late:
                        dve.wait_ge(pick_ready, r * (EXPERTS // 2 + 1))
                        dve.tensor_scalar_add(slot[:, :, :], slot[:, :, :], float(-SLOTS)).then_inc(mo_step, 1)
                        dve.wait_ge(mo_step, r)
                        dve.wait_ge(xg_done, r * (EXPERTS + 2))
                        dve.wait_ge(put_done, r * (EXPERTS // 2))
                    dve.memset(yhi[:, :].bitcast(F32), 0.0)
                    dve.memset(ylo[:, :].bitcast(F32), 0.0).then_inc(ylo_ready, 1)
                    picks(0, 0)
                    xg_out(r * (EXPERTS // 2 + 1), 0)
                    with dve.Fori(0, EXPERTS // 4) as it:
                        for b in range(2):
                            pair = r * (EXPERTS // 2) + it * 2 + b
                            picks(it * 4 + 2 * b + 2, 1 - b)
                            dve.wait_ge(tanh_g, pair + 1)
                            dve.scalar_tensor_tensor(sig[:, :], thg[:, :], 1.0, bank[2 + b][:, 0:FF], ALU.add, ALU.mult).then_inc(silu_step, 1)
                            dve.wait_ge(silu_step, pair + 1)
                            dve.tensor_tensor(act_rows[:, :], bank[2 + b][:, FF:2 * FF], sig[:, :], ALU.mult).then_inc(a_ready, 1)
                            dve.wait_ge(put_done, pair + 1)
                            pb = bank[3 - b]
                            dve.tensor_copy(putT[b][:, :], pb[:, 0:M * P])
                            dve.tensor_copy(yw[b][:, :], pb[:, M * P:M * P + 1]).then_inc(put_ready, 1)
                            dve.wait_ge(sc_drained, 4 * (pair + r) + 4)
                            scatter_out(pair + r)
                            dve.wait_ge(turned, pair + 1)
                            dve.tensor_copy(aT[:, :, :], bank[2 + b][:, 0:FF].rearrange("p (t n) -> p t n", t=2)).then_inc(aT_ready, 1)
                            xg_out(pair + r + 1, 1 - b)
                            dve.wait_ge(put_ready, pair + 2)
                            dve.wait_ge(yhi_ready, pair + 1)
                            for n in range(2):
                                s = slice(n * 512, n * 512 + 512)
                                ins = dve.scalar_tensor_tensor(ylo[:, s], bank[4 + n][:, :], yw[b][:, 0:1], yhi[:, s].bitcast(F32),
                                                               ALU.mult, ALU.subtract)
                            ins.then_inc(ylo_ready, 1)
                    last = (r + 1) * (EXPERTS // 2) + r
                    dve.wait_ge(sc_drained, 4 * last + 4)
                    scatter_out(last)

                dve.memset(aT[:, :, :], 0.0).then_inc(aT_ready, 1)
                dve.memset(yw[1][:, :], 0.0).then_inc(put_ready, 1)
                dve.memset(putT[1][:, :].bitcast(F32), 0.0).then_inc(sc_drained, 4)
                dve.wait_ge(sc_drained, 4)
                dve.wait_ge(aT_ready, 1)
                dve.wait_ge(put_ready, 1)
                dve.wait_ge(most_ready, 1)
                count = dve.value_load(mosti[0:1, 0:1], min_val=0, max_val=S)
                rounds(0)
                with dve.Fori(1, ROUNDS) as r:
                    with dve.If(count > r * SLOTS):
                        rounds(r, late=True)

                dve.drain()
                drained(dve, "gb3")
                dve.wait_ge(gf_in, 16)
                for m in range(M):
                    do(dve.tensor_tensor(acc[:, m, :], acc[:, m, :], gt2bc[:, :], ALU.mult))
                    settle()
                    dve.tensor_tensor(acc[:, m, :], acc[:, m, :], x1[:, m, :], ALU.add).then_inc(result, 1)
                dve.wait_ge(result, M)
                mean_square(3 + M, tiny[:, 6:6 + M], D)
                dve.wait_ge(rms_ready, 4)
                for m in range(M):
                    dve.scalar_tensor_tensor(x1[:, m, :], acc[:, m, :], tiny[:, 6 + m:7 + m], gfbc[:, :], ALU.mult, ALU.mult).then_inc(result, 1)

            @block.tensor
            def _(pe):
                def begin(name):
                    n = INDEX[name]
                    if n >= 8:
                        drained(pe, ORDER[n - 8][0])
                    return bank_of(name)

                def done(ins):
                    ins.then_inc(product_done, 1)

                pe.wait_ge(rows_in, 16 * 7)
                pe.wait_ge(consts, ALL_CONSTS)
                b = begin("rows")
                done(pe.transpose(b[:, 0:R_END], rows[0:R_END, :], ident[0:R_END, 0:R_END]))

                def ada(n):
                    b = begin(f"ada{n}")
                    for q in range(4):
                        arrived(pe, "ada", 4 * n + q)
                    for k in range(KD):
                        for q in range(4):
                            w = chunk("ada", 4 * n + q).rearrange("p (k n) -> p k n", k=KD)
                            ins = pe.matmul(b[32 * q:32 * q + 32, 0:CH], condB[:, k, :], w[:, k, :], start=(k == 0),
                                            stop=(k == KD - 1), tile_position=(0, 32 * q))
                    done(ins)

                def adt(n):
                    b = begin(f"adt{n}")
                    drained(pe, f"ada{n}")
                    for t in range(2):
                        ins = pe.transpose(b[:, t * P:(t + 1) * P], adaR[n % 2][:, t * P:(t + 1) * P], ident[:, :])
                    done(ins)

                def turn_x(name, n, src):
                    b = begin(name)
                    for kk in range(2):
                        for m in range(M):
                            k = 2 * n + kk
                            ins = pe.transpose(b[:, kk * S + m * P:kk * S + m * P + P], src[:, m, k * P:(k + 1) * P], ident[:, :])
                    done(ins)

                def win(n):
                    lo, hi = WINC[n]
                    wd = hi - lo
                    b = begin(f"win{n}")
                    arrived(pe, "win", n)
                    w = chunk("win", n)[:, 0:KD * wd].rearrange("p (k n) -> p k n", k=KD)
                    for m in range(M):
                        for k in range(KD):
                            ins = pe.matmul(b[:, m * wd:(m + 1) * wd], hT[:, k, m * P:(m + 1) * P], w[:, k, :],
                                            start=(k == 0), stop=(k == KD - 1))
                    done(ins)

                def mg(n):
                    b = begin(f"mg{n}")
                    arrived(pe, "mg", n)
                    w = chunk("mg", n).rearrange("p (k n) -> p k n", k=KD)
                    for t in range(2):
                        for k in range(KD):
                            ins = pe.matmul(b[:, t * S:(t + 1) * S], w[:, k, t * P:(t + 1) * P], hT[:, k, :],
                                            start=(k == 0), stop=(k == KD - 1))
                    done(ins)

                def turn_cols(name, tiles):
                    b = begin(name)
                    for t, tile in enumerate(tiles):
                        for m in range(M):
                            ins = pe.transpose(b[:, t * S + m * P:t * S + m * P + P], tile(m), ident[:, :])
                    done(ins)

                pe.wait_ge(cond_ready, 1)
                ada(0)
                ada(1)
                adt(0)
                adt(1)
                pe.wait_ge(xn_ready, 2)
                for n in range(4):
                    turn_x(f"xT{n}", n, xs)
                drained(pe, "xT3")
                for n in range(len(WINC)):
                    win(n)
                mg(0)
                pe.wait_ge(kvn_ready, 2)
                b = begin("kvT")
                for m in range(M):
                    ins = pe.transpose(b[:, m * P:(m + 1) * P], kvn[:, m, :], ident[:, :])
                done(ins)
                mg(1)
                drained(pe, "kvT")
                pe.wait_ge(kv_w_in, 16)
                for n in range(4):
                    m, half = n // 2, n % 2
                    b = begin(f"kvp{n}")
                    done(pe.matmul(b[:, :], kvnT[:, m * P:(m + 1) * P], w_kv[:, half * 512:half * 512 + 512], start=True, stop=True))
                pe.wait_ge(roped, 1)
                turn_cols("iqT", [lambda m, t=t: xp[:, m, IQ + t * P:IQ + (t + 1) * P] for t in range(2)])
                turn_cols("ikT", [lambda m: kdup[:, m, 4, :]])
                b = begin("cmpx")
                for n, col in enumerate((KC, VC)):
                    for gi in range(GROUPS):
                        for par in range(2):
                            for m in range(M):
                                at = (n * GROUPS + gi) * P + m * HD
                                ins = pe.matmul(b[par * HD:(par + 1) * HD, at:at + HD], xp[:, m, col + gi * HD:col + (gi + 1) * HD],
                                                ident[:, par:P:2], start=True, stop=True)
                done(ins)
                for n in range(2):
                    turn_cols(f"qbT{n}", [lambda m, t=t: xp[:, m, QB + t * P:QB + (t + 1) * P] for t in (2 * n, 2 * n + 1)])
                turn_cols("ksT", [lambda m, gi=gi: kdup[:, m, gi, :] for gi in range(2)])
                turn_cols("kwT", [lambda m, gi=gi: kdup[:, m, 2 + gi, :] for gi in range(2)])
                mg(2)
                drained(pe, "ikT")
                for m in range(M):
                    nk = P * (m + 1)
                    banks = [begin(f"il{4 * m + r}") for r in range(4)]
                    for t in range(2):
                        for r in range(4):
                            rr = slice(r * IDX_DIM, (r + 1) * IDX_DIM)
                            ins = pe.matmul(banks[r][:, t * nk:(t + 1) * nk], iqT[rr, t, m * P:(m + 1) * P], ikT[rr, 0:nk],
                                            start=True, stop=True, tile_position=(r * IDX_DIM, 0))
                            if t == 1:
                                done(ins)
                pe.wait_ge(flat_ready, 1)
                b = begin("cmp1")
                for j in range(CMP_TILES):
                    for n, kind in enumerate(("cmp1k", "cmp1v")):
                        if j % KD == 0:
                            arrived(pe, kind, j // KD)
                        w = chunk(kind, j // KD).rearrange("p (k n) -> p k n", k=KD)
                        ins = pe.matmul(b[n * HD:n * HD + GROUPS * NCMP, 0:CMP_HIDDEN], flat[:, n, j, :], w[:, j % KD, :],
                                        start=(j == 0), stop=(j == CMP_TILES - 1), tile_position=(0, n * HD))
                done(ins)
                mg(3)
                b = begin("cmpT")
                drained(pe, "cmp1")
                for t in range(2):
                    ins = pe.transpose(b[:, t * 96:(t + 1) * 96], hid[0:96, t * P:(t + 1) * P], ident[0:96, 0:96])
                done(ins)
                b = begin("cmp2")
                drained(pe, "cmpT")
                pe.wait_ge(cmp_w_in, 32)
                for par in range(2):
                    for t in range(2):
                        pe.matmul(b[par * HD:(par + 1) * HD, 0:GROUPS * NCMP], w2[:, 0, t, :], hidT[:, t, 0:GROUPS * NCMP], start=(t == 0), stop=(t == 1))
                for gi in range(GROUPS):
                    for t in range(2):
                        ins = pe.matmul(b[0:NCMP, 64 + gi * HD:64 + (gi + 1) * HD], hidT[:, t, HD + gi * NCMP:HD + (gi + 1) * NCMP],
                                        w2[:, 1, t, :], start=(t == 0), stop=(t == 1))
                done(ins)
                drained(pe, "cmp2")
                for par in range(2):
                    b = begin(f"sc{par}")
                    r = slice(par * HD, (par + 1) * HD)
                    for m in range(M):
                        for i in range(PAIRS):
                            g = (2 * i + par) // (HEADS // GROUPS)
                            at = (m * PAIRS + i) * NCMP
                            ins = pe.matmul(b[:, at:at + NCMP], qbT[r, i, m * P:(m + 1) * P], kcT[r, g * NCMP:(g + 1) * NCMP], start=True, stop=True,
                                            tile_position=(par * HD, 0))
                    done(ins)

                def scores(u):
                    kind, m = UNITS[u]
                    nk = P * (m + 1)
                    per = PAIRS // (m + 1)
                    for blk in range(m + 1):
                        banks = [begin(f"S{kind}{m}_{2 * blk + par}") for par in range(2)]
                        for j in range(per):
                            for par in range(2):
                                i = blk * per + j
                                g = (2 * i + par) // (HEADS // GROUPS)
                                r = slice(par * HD, (par + 1) * HD)
                                q = (qaT if kind == "dsa" else qbT)[r, i, m * P:(m + 1) * P]
                                k = kaT[r, i, 0:nk] if kind == "dsa" else (ksT if kind == "sel" else kwT)[r, g, 0:nk]
                                ins = pe.matmul(banks[par][:, j * nk:(j + 1) * nk], q, k, start=True, stop=True, tile_position=(par * HD, 0))
                                if j == per - 1:
                                    done(ins)

                def turns(u):
                    kind, m = UNITS[u]
                    pe.wait_ge(unit_probs, u + 1)
                    for n in range(2 * (m + 1)):
                        b = begin(f"T{kind}{m}_{n}")
                        for j in range(4):
                            at = 4 * n + j
                            hs, kb = at // (m + 1), at % (m + 1)
                            ins = pe.transpose(b[:, j * P:(j + 1) * P], probs[u % 2][:, hs, kb * P:(kb + 1) * P], ident[:, :])
                        done(ins)

                def last_turn(u):
                    return f"T{UNITS[u][0]}{UNITS[u][1]}_{2 * UNITS[u][1] + 1}"

                def pv_b(m):
                    drained(pe, last_turn(2 * m + 1))
                    drained(pe, "pcT3")
                    b = begin(f"PVb{m}")
                    for i in range(PAIRS):
                        terms = []
                        for par in range(2):
                            hs, g = par * PAIRS + i, (2 * i + par) // (HEADS // GROUPS)
                            terms.append([(vcs[0:NCMP, g, :], pcT[0:NCMP, m * HEADS + hs, :])]
                                         + [(xp[:, kb, col + g * HD:col + (g + 1) * HD], pT[buf][:, hs * (m + 1) + kb, :])
                                            for buf, col in ((0, VS), (1, VW)) for kb in range(m + 1)])
                        for n in range(len(terms[0])):
                            for par in range(2):
                                v, p = terms[par][n]
                                ins = pe.matmul(b[par * HD:(par + 1) * HD, i * P:(i + 1) * P], v, p, start=(n == 0),
                                                stop=(n == len(terms[0]) - 1))
                    done(ins)

                def pv_a(m):
                    drained(pe, last_turn(4 + m))
                    b = begin(f"PVa{m}")
                    for i in range(PAIRS):
                        for kb in range(m + 1):
                            for par in range(2):
                                hs, h = par * PAIRS + i, 2 * i + par
                                v = kvx[:, kb, HEADS * HD + h * HD:HEADS * HD + (h + 1) * HD]
                                ins = pe.matmul(b[par * HD:(par + 1) * HD, i * P:(i + 1) * P], v, pT[m][:, hs * (m + 1) + kb, :],
                                                start=(kb == 0), stop=(kb == m))
                    done(ins)

                drained(pe, "kwT")
                scores(0)
                scores(1)
                mg(4)
                pe.wait_ge(cmp_probs, 1)
                for n in range(4):
                    b = begin(f"pcT{n}")
                    for j in range(4):
                        at = 4 * n + j
                        ins = pe.transpose(b[0:NCMP, j * P:(j + 1) * P], smc[:, at // HEADS, at % HEADS, :], ident[:, :])
                    done(ins)
                pe.wait_ge(roped, 2)
                for n in range(2):
                    turn_cols(f"qaT{n}", [lambda m, t=t: xp[:, m, QA + t * P:QA + (t + 1) * P] for t in (2 * n, 2 * n + 1)])
                for n in range(2):
                    turn_cols(f"kaT{n}", [lambda m, t=t: kvx[:, m, t * P:(t + 1) * P] for t in (2 * n, 2 * n + 1)])
                turns(0)
                scores(2)
                mg(5)
                turns(1)
                scores(3)
                mg(6)
                pv_b(0)
                turns(2)
                drained(pe, "kaT1")
                scores(4)
                mg(7)
                turns(3)
                pv_b(1)
                scores(5)
                ada(2)
                turns(4)
                adt(2)
                pv_a(0)
                ada(3)
                turns(5)
                adt(3)
                pv_a(1)
                ada(4)
                pe.wait_ge(diag_ready, 1)
                for n in range(2):
                    b = begin(f"gb{n}")
                    done(pe.matmul(b[:, :], ones[:, :], diag[:, n * 512:n * 512 + 512], start=True, stop=True))
                adt(4)
                ada(5)
                drained(pe, "PVa1")
                for t in range(KD):
                    if t == 1:
                        adt(5)
                    b = begin(f"up{t}")
                    for n, (kind, o) in enumerate((("upa", oaT), ("upb", obT))):
                        if t % 4 == 0:
                            arrived(pe, kind, t // 4)
                        w = chunk(kind, t // 4).rearrange("p (k n) -> p k n", k=PAIRS)
                        for i in range(PAIRS):
                            ins = pe.matmul(b[:, n * S:(n + 1) * S], w[:, i, (t % 4) * P:(t % 4) * P + P], o[:, i, :],
                                            start=(i == 0), stop=(i == PAIRS - 1))
                    done(ins)
                pe.wait_ge(gates_ready, KD)
                for n in range(4):
                    b = begin(f"out{n}")
                    arrived(pe, "out", n)
                    w = chunk("out", n).rearrange("p (k n) -> p k n", k=KD)
                    for m in range(M):
                        for k in range(KD):
                            ins = pe.matmul(b[:, m * CH:(m + 1) * CH], mT[:, k, m * P:(m + 1) * P], w[:, k, :],
                                            start=(k == 0), stop=(k == KD - 1))
                    done(ins)
                pe.wait_ge(diag_ready, 2)
                for n in range(2):
                    b = begin(f"gb{n + 2}")
                    done(pe.matmul(b[:, :], ones[:, :], diag2[:, n * 512:n * 512 + 512], start=True, stop=True))
                pe.wait_ge(x1n_ready, 1)
                for n in range(4):
                    turn_x(f"x1T{n}", n, x1n)
                drained(pe, "x1T3")
                pe.wait_ge(router_in, 64)
                b = begin("rt")
                for m in range(M):
                    for k in range(KD):
                        ins = pe.matmul(b[:, m * 36:(m + 1) * 36], h2T[:, k, m * P:(m + 1) * P], wr[:, k, :],
                                        start=(k == 0), stop=(k == KD - 1))
                done(ins)
                pe.wait_ge(sel_ready, 1)
                b = begin("pos")
                E = EXPERTS
                pe.matmul(b[:, 0:E], tri[:, :], sel[:, 0, 0:E], start=True, stop=True)
                pe.matmul(b[:, E:2 * E], tri[:, :], sel[:, 1, 0:E], start=True, stop=False)
                pe.matmul(b[:, E:2 * E], ones[:, :], sel[:, 0, 0:E], start=False, stop=True)
                pe.matmul(b[:, 2 * E:3 * E], ones[:, :], sel[:, 0, 0:E], start=True, stop=False)
                done(pe.matmul(b[:, 2 * E:3 * E], ones[:, :], sel[:, 1, 0:E], start=False, stop=True))

                def gather(count, buf, first=False):
                    pe.wait_ge(pick_ready, count + 1)
                    if not first:
                        pe.wait_ge(xgT_act, count)
                        pe.wait_ge(xgT_dve, count)
                    for half in range(2):
                        for k in range(4):
                            kk = 4 * half + k
                            for n, (src, m) in enumerate(((s, m) for s in (x1hi, x1lo) for m in range(M))):
                                ins = pe.matmul(bank[half][:, k * P:(k + 1) * P], src[:, m, kk * P:(kk + 1) * P],
                                                pick[buf][:, m, :], start=(n == 0), stop=(n == 3))
                        ins.then_inc(xg_done, 1)

                def gate_up(its, b):
                    for j in range(2):
                        for q in range(2):
                            pe.wait_ge(mlanded[PIECES * (2 * b + j) + q], 16 * (its + 1))
                    for k in range(KD):
                        for j in range(2):
                            ins = pe.matmul(bank[2 + b][j * SLOTS:(j + 1) * SLOTS, :], xgT[b][:, k, j * SLOTS:(j + 1) * SLOTS],
                                            gate_up_weights(2 * b + j, k), start=(k == 0), stop=(k == KD - 1))
                    ins.then_inc(gu_done, 1)

                def down(its, b):
                    for j in range(2):
                        pe.wait_ge(mlanded[PIECES * (2 * b + j) + 2], 16 * (its + 1))
                    for n in range(2):
                        for t in range(2):
                            for j in range(2):
                                w = mslot(PIECES * (2 * b + j) + 2).rearrange("p (k n) -> p k n", k=2)
                                ins = pe.matmul(bank[4 + n][j * SLOTS:(j + 1) * SLOTS, :], aT[:, t, j * SLOTS:(j + 1) * SLOTS],
                                                w[:, t, n * 512:n * 512 + 512], start=(t == 0), stop=(t == 1))
                    ins.then_inc(down_done, 1)

                def scatter(s, b):
                    pe.wait_ge(ylo_ready, s + 1)
                    for n in range(4):
                        m, half = n // 2, n % 2
                        pe.wait_ge(sc_drained, 4 * s + 3 + n)
                        for q, y in enumerate((yhi, ylo)):
                            ins = pe.matmul(bank[6 + n % 2][:, :], putT[b][:, m * P:(m + 1) * P],
                                            y[:, half * 512:half * 512 + 512], start=(q == 0), stop=(q == 1))
                        ins.then_inc(sc_done, 1)

                def rounds(r, late=False):
                    gather(r * (EXPERTS // 2 + 1), 0, first=not late)
                    with pe.Fori(0, EXPERTS // 4) as it:
                        its = r * (EXPERTS // 4) + it
                        for b in range(2):
                            pair = r * (EXPERTS // 2) + it * 2 + b
                            pe.wait_ge(xgT_act, pair + r + 1)
                            pe.wait_ge(xgT_dve, pair + r + 1)
                            pe.wait_ge(put_ready, pair + 1)
                            gate_up(its, b)
                            pe.wait_ge(aT_ready, pair + 1)
                            pb = bank[3 - b]
                            for m in range(M):
                                pe.transpose(pb[:, m * P:(m + 1) * P], pick[b][:, m, :].bitcast(F32), ident[:, :])
                            for m in range(M):
                                ins = pe.matmul(pb[:, M * P:M * P + 1], pickw[b][:, m, :], ones[:, 0:1], start=(m == 0), stop=(m == M - 1))
                            ins.then_inc(put_done, 1)
                            scatter(pair + r, 1 - b)
                            pe.wait_ge(a_ready, pair + 1)
                            for t in range(2):
                                ins = pe.transpose(bank[2 + b][:, t * P:(t + 1) * P], act_rows[:, t * P:(t + 1) * P], ident[:, :])
                            ins.then_inc(turned, 1)
                            gather(pair + r + 1, 1 - b)
                            pe.wait_ge(aT_ready, pair + 2)
                            down(its, b)
                    scatter((r + 1) * (EXPERTS // 2) + r, 1)

                drained(pe, "pos")
                pe.wait_ge(hi_ready, 1)
                pe.wait_ge(lo_ready, 1)
                pe.wait_ge(most_ready, 1)
                count = pe.value_load(mosti[0:1, 0:1], min_val=0, max_val=S)
                rounds(0)
                with pe.Fori(1, ROUNDS) as r:
                    with pe.If(count > r * SLOTS):
                        rounds(r, late=True)


def overlap(src):
    v = src[:, 0:CMP_TILES].unsqueeze(2).to_broadcast([P, CMP_TILES, NCMP]).copy()
    ap = [list(d) for d in v.ap]
    ap[-1][0] = CMP_STRIDE // 2
    return bass.AP(tensor=v.tensor, offset=v.offset, ap=ap)


_INS = ["x", "c", "positions", "w_ada", "b_ada", "g_norm1", "w_in", "g_kv_latent", "w_kv_up", "pe_cmp_k", "pe_cmp_v",
        "w_cmp1_k", "w_cmp2_k", "w_cmp1_v", "w_cmp2_v", "w_up_a", "w_up_b", "w_out", "g_norm2", "w_router_group",
        "b_router_group", "w_router_expert", "b_router_expert", "w_expert_gate", "w_expert_up", "w_expert_down", "g_final"]
_STRIP = {"w_ada", "w_in", "w_cmp1_k", "w_cmp1_v", "w_up_a", "w_up_b", "w_out", "w_expert_gate", "w_expert_up", "w_expert_down"}


def kernel(**inputs):
    import concourse.bacc as bacc
    from concourse.bass_utils import run_bass_kernel_spmd

    nc = bacc.Bacc("TRN2", target_bir_lowering=False, num_devices=1)
    arrays, args = {}, {}
    for name in _INS:
        v = np.ascontiguousarray(inputs[name])
        arrays[f"in_{name}_dram"] = v
        ap = nc.dram_tensor(f"in_{name}_dram", v.shape, mybir.dt.from_np(v.dtype), kind="ExternalInput").ap()
        args[name] = ap[0] if name in _STRIP else ap
    out = nc.dram_tensor("out_0_dram", (1, S, D), F32, kind="ExternalOutput").ap()
    layer_kernel(nc, **args, out=out)
    r = run_bass_kernel_spmd(nc, [arrays], core_ids=[0])
    return r.results[0]["out_0_dram"]
```

```python
from contextlib import ExitStack

import numpy as np

import concourse.bass as bass
from concourse import mybir

F32 = mybir.dt.float32
F32R = mybir.dt.float32r
I32 = mybir.dt.int32
ALU = mybir.AluOpType
ACT = mybir.ActivationFunctionType
AX = mybir.AxisListType.X

P = 128
D = 1024
S = 256
KD = D // P
M = S // P
HD = 64
HEADS = 8
PAIRS = HEADS // 2
ROT = HD // 4
RANK = 128
IDX_HEADS, IDX_DIM = 8, 32
IDX_ROT = IDX_DIM // 4
TOPK = S // 4
GROUPS = 2
CMP_LEN, CMP_STRIDE, CMP_HIDDEN = 32, 16, 256
NCMP = S // CMP_STRIDE - CMP_LEN // CMP_STRIDE + 1
CMP_TILES = CMP_LEN * HD // P
EXPERTS, EXPERT_GROUPS = 32, 4
PER_GROUP = EXPERTS // EXPERT_GROUPS
FF = 256
THETA = 500000.0
EPS = 1e-6
NEG = -1e30
TINY = 1e-30
SCALE = HD ** -0.5

QA = 0
KV = QA + HEADS * HD
IQ = KV + RANK
IW = IQ + IDX_HEADS * IDX_DIM
IK = IW + IDX_HEADS
QB = IK + IDX_DIM
KC = QB + HEADS * HD
VC, KS, VS, KW, VW = (KC + n * GROUPS * HD for n in range(1, 6))
BR = VW + GROUPS * HD
MG = BR + 3 * HEADS
WIN_COLS = MG + 2 * D

CH = 256
WIN_FIRST = MG % CH
WINC = [(max(c - CH, 0), c) for c in range(WIN_FIRST, MG + 1, CH)]
RING = 7
HI_SLOTS = 2
SLOTS = 64
ROUNDS = S // SLOTS
MRING = 16
PIECES = 3
QUADS = EXPERTS // 4

R_C, R_BADA, R_G1, R_G2, R_GKV, R_PEK, R_PEV, R_END = 0, 8, 56, 64, 72, 73, 89, 105

UNITS = [("sel", 0), ("win", 0), ("sel", 1), ("win", 1), ("dsa", 0), ("dsa", 1)]


def product_order():
    act, dve = "act", "dve"

    def score(kind, m):
        return [(f"S{kind}{m}_{n}", dve) for n in range(2 * (m + 1))]

    def turn(kind, m):
        return [(f"T{kind}{m}_{n}", act) for n in range(2 * (m + 1))]

    def mg(n):
        return [(f"mg{n}", act)]

    o = [("rows", dve), ("ada0", dve)] + [(f"xT{n}", act if n == 1 else "late") for n in range(4)]
    o += [("ada1", dve), ("adt0", dve), ("adt1", dve)]
    o += [(f"win{n}", act) for n in range(len(WINC))]
    o += mg(0) + [("kvT", dve)] + mg(1) + [(f"kvp{n}", act) for n in range(4)]
    o += [("iqT", act), ("ikT", act), ("cmpx", act), ("qbT0", act), ("qbT1", act), ("ksT", act), ("kwT", act)]
    o += mg(2) + [(f"il{n}", act) for n in range(8)]
    o += [("cmp1", dve)] + mg(3) + [("cmpT", dve), ("cmp2", dve)]
    o += score("sel", 0) + score("win", 0) + [("sc0", dve), ("sc1", dve)] + mg(4)
    o += [(f"pcT{n}", act) for n in range(4)]
    o += [("qaT0", act), ("qaT1", act)] + mg(5) + [("ada2", dve), ("kaT0", act), ("kaT1", act), ("adt2", dve)]
    o += turn("sel", 0) + score("sel", 1) + turn("win", 0) + score("win", 1) + mg(6) + mg(7) + [("ada3", dve)]
    o += [("adt3", dve), ("PVb0", act)] + turn("sel", 1) + score("dsa", 0) + [("ada4", dve)] + turn("win", 1)
    o += [("PVb1", act), ("adt4", dve)] + score("dsa", 1) + [("ada5", dve)] + turn("dsa", 0) + [("adt5", dve), ("PVa0", dve)]
    o += turn("dsa", 1) + [("PVa1", dve), ("gb0", act), ("gb1", act)]
    o += [("up0", dve), ("up1", dve), ("rsh", dve)] + [(f"up{n}", dve) for n in range(2, KD)]
    o += [("out0", dve), ("gb2", act), ("out1", dve), ("gb3", act), ("x1T0", act), ("out2", dve), ("x1T1", act)]
    o += [("out3", dve), ("x1T2", act), ("x1T3", act), ("rt0", dve), ("rt1", dve), ("pos", dve)]
    return o


HT_ORDER = [1, 0, 2, 3]
ORDER = product_order()
INDEX = {name: n for n, (name, _) in enumerate(ORDER)}


def chunk_order():
    o = []
    for name, _ in ORDER:
        if name[:3] == "ada":
            o += [(name, "ada", 4 * int(name[3:]) + j) for j in range(4)]
        elif name[:3] == "win":
            o.append((name, "win", int(name[3:])))
        elif name[:2] == "mg":
            o.append((name, "mg", int(name[2:])))
        elif name == "cmp1":
            o += [(name, kind, j) for j in range(2) for kind in ("cmp1k", "cmp1v")]
        elif name in ("up0", "up4"):
            n = int(name[2:])
            o += [(f"up{n + 3}", "upa", n // 4), (f"up{n + 3}", "upb", n // 4)]
        elif name[:3] == "out":
            o.append((name, "out", int(name[3:])))
    return o


CHUNKS = chunk_order()
CHUNK_AT = {(kind, n): at for at, (_, kind, n) in enumerate(CHUNKS)}

SPLITS = [(kind, n) for _, kind, n in CHUNKS if kind in ("win", "mg", "upa", "upb", "out")]


def hi_buffer(kind, n):
    if kind == "win":
        return n % 3
    if kind == "mg":
        return n % 2
    return {("upa", 0): 0, ("upb", 0): 1, ("upa", 1): 3, ("upb", 1): 4, ("out", 0): 0, ("out", 1): 1,
            ("out", 2): 5, ("out", 3): 6}[kind, n]


def by_pool(kind, n):
    return kind != "upa" and (kind, n) != ("win", 0)


def layer_kernel(nc, x, c, positions, w_ada, b_ada, g_norm1, w_in, g_kv_latent, w_kv_up, pe_cmp_k,
                 pe_cmp_v, w_cmp1_k, w_cmp2_k, w_cmp1_v, w_cmp2_v, w_up_a, w_up_b, w_out, g_norm2,
                 w_router_group, b_router_group, w_router_expert, b_router_expert, w_expert_gate,
                 w_expert_up, w_expert_down, g_final, out):
    base = (nc.sbuf_base + 63) // 64 * 64
    top = nc.sbuf_usable_end

    class Map:

        def __init__(self, at):
            self.at = at

        def __call__(self, name, shape, dt=F32):
            size = int(np.prod(shape[1:])) * 4
            t = place(name, shape, dt, self.at)
            self.at += (size + 31) // 32 * 32
            assert self.at <= top, (name, self.at, top)
            return t

    def place(name, shape, dt, at):
        return nc.alloc_sbuf_tensor_at(name, shape, dt, offset=at)

    keep = Map(base)
    ring_at = keep.at
    ring = keep("ring", [P, RING + HI_SLOTS, KD * CH])
    ident = keep("ident", [P, P])
    ones = keep("ones", [P, P])
    tri = keep("tri", [P, P])
    iota_slot = keep("iota_slot", [P, SLOTS])
    iota8 = keep("iota8", [P, 8])
    cols = keep("cols", [P, R_END])
    modT = keep("modT", [P, 48])
    A1 = keep("A1", [P, KD])
    A2 = keep("A2", [P, KD])
    condT = keep("condT", [P, KD])
    condB = keep("condB", [P, KD, 32])
    adaR = [keep(f"adaR{n}", [P, CH]) for n in range(2)]
    tiny = keep("tiny", [P, 64])
    wr = keep("wr", [P, KD, 36])
    brow = keep("brow", [P, 36])
    x1_at = keep.at
    x1 = keep("x1", [P, M, D])

    a = Map(keep.at)
    hT = place("hT", [P, KD, S], F32, x1_at)
    xs = a("xs", [P, M, D])
    kvx_at = a.at - 8192
    kvx = place("kvx", [P, M, D], F32, kvx_at)
    xp = a("xp", [P, M, MG])
    gT = a("gT", [P, 2 * KD, S])
    qkT_at = a.at
    qaT = a("qaT", [P, PAIRS, S])
    kaT = a("kaT", [P, PAIRS, S])
    qbT = a("qbT", [P, PAIRS, S])
    ksT = a("ksT", [P, GROUPS, S])
    kwT = a("kwT", [P, GROUPS, S])
    iqT = a("iqT", [P, 2, S])
    ikT = a("ikT", [P, S])
    probs_at = [a.at, a.at + 8192]
    probs = [a("probs0", [P, HEADS, S]), a("probs1", [P, HEADS, S])]
    pT_at = [a.at, a.at + 8192]
    pT = [a("pT0", [P, 2 * HEADS, P]), a("pT1", [P, 2 * HEADS, P])]
    oT_at = a.at
    oalo = a("oalo", [P, PAIRS, S], F32R)
    obT = a("obT", [P, PAIRS, S])
    wsh_at = a.at
    cbias = a("cbias", [P, M, S])
    abias = a("abias", [P, M, S])
    pcT = a("pcT", [P, M * HEADS, P])
    smc = a("smc", [P, M, HEADS, NCMP])
    kcT = a("kcT", [P, GROUPS * NCMP])
    vcs = a("vcs", [P, GROUPS, HD])
    w2 = a("w2", [P, 2, 2, HD])
    cbc = a("cbc", [P, M, NCMP])
    cmk = a("cmk", [P, M, NCMP])
    trig = a("trig", [P, 12, M * 8])
    c16 = a("c16", [P, 2, M, ROT])
    c8 = a("c8", [P, 2, M, IDX_ROT])
    posi = a("posi", [P, M], I32)
    gates = a("gates", [P, M, 3 * HEADS])
    stats = a("stats", [P, 12, HEADS])
    w_kv = place("w_kv", [P, 2 * HEADS * HD], F32, probs_at[1])
    junk = place("junk", [P, D], F32, probs_at[0])
    rows = place("rows", [P, P], F32, pT_at[0] + 4096)
    relu = [place(f"relu{m}", [P, HEADS, S], F32, probs_at[m]) for m in range(M)]
    cx = place("cx", [P, 2, GROUPS, P], F32, pT_at[0])
    flat = place("flat", [P, 2, CMP_TILES, GROUPS * NCMP], F32, pT_at[0] + 4096)
    kdup = place("kdup", [P, M, 5, P], F32, pT_at[1])
    hid = place("hid", [P, CMP_HIDDEN], F32, pT_at[1])
    hth = place("hth", [P, CMP_HIDDEN], F32, pT_at[1] + 1024)
    hidT = place("hidT", [P, 2, 96], F32, pT_at[1] + 2048)
    ropeA = a("ropeA", [P, M, 10, ROT])
    ropeB = a("ropeB", [P, M, 10, ROT])
    kvn = place("kvn", [P, M, RANK], F32, pT_at[1] + 7168)
    kvnT = place("kvnT", [P, S], F32, probs_at[0] + 4096)
    xr = place("xr", [P, M, D], F32, probs_at[0])
    mT = place("mT", [P, KD, S], F32, probs_at[1])
    gt1bc = place("gt1bc", [P, D], F32, pT_at[0])
    diag = place("diag", [P, D], F32, pT_at[0] + 4096)
    wsh = place("wsh", [P, KD, 36], F32, wsh_at)
    wshs = place("wshs", [P, 36], F32, wsh_at + 1152)
    x1sq = place("x1sq", [P, M, CH], F32, pT_at[0] + 6144)
    tmp_up = place("tmp_up", [P, 2, S], F32, pT_at[0] + 4096)
    ring_lo = place("ring_lo", [P, RING, KD * CH], F32R, ring_at)
    hThi = place("hThi", [P, KD, S], F32R, oT_at)
    hTlo = place("hTlo", [P, KD, S], F32R, x1_at)
    oahi = place("oahi", [P, PAIRS, S], F32R, qkT_at)
    obhi = place("obhi", [P, PAIRS, S], F32R, qkT_at + 8192)
    oblo = place("oblo", [P, PAIRS, S], F32R, oT_at + 4096)
    mThi = place("mThi", [P, KD, S], F32R, pT_at[1])
    mTlo = place("mTlo", [P, KD, S], F32R, probs_at[1])
    whi_at = [ring_at + 8192 * RING, ring_at + 8192 * (RING + 1), pT_at[0], kvx_at, kvx_at + 8192, qkT_at, qkT_at + 8192]
    whi = [place(f"whi{n}", [P, KD * CH], F32R, at) for n, at in enumerate(whi_at)]

    e = Map(keep.at)
    extra = e("extra", [P, 3, KD * CH])
    x1T_at = e.at
    x1T = e("x1T", [P, KD, S])
    gt2bc = e("gt2bc", [P, D])
    x1n_at = e.at
    x1n = e("x1n", [P, M, D])
    e.at += 8192
    fifth = place("fifth", [P, 2, KD * CH], F32, x1n_at)
    x1hi = e("x1hi", [P, M, D], F32R)
    x1lo = e("x1lo", [P, M, D], F32R)
    gfbc = e("gfbc", [P, D])
    xgT = [e(f"xgT{n}", [P, KD, 4 * SLOTS]) for n in range(2)]
    pick = [e(f"pick{n}", [P, M, 4 * SLOTS], F32R) for n in range(2)]
    pickw = [e(f"pickw{n}", [P, M, 4 * SLOTS]) for n in range(2)]
    putT = [e(f"putT{n}", [P, M * P], F32R) for n in range(2)]
    yw = [e(f"yw{n}", [P, 1]) for n in range(2)]
    thg = e("thg", [P, FF])
    sig = e("sig", [P, FF])
    act_rows = e("act_rows", [P, FF])
    aT = e("aT", [P, 2, 2 * SLOTS])
    yhi = e("yhi", [P, D], F32R)
    y_at = e.at
    ylo = e("ylo", [P, D], F32R)
    y = place("y", [P, D], F32, y_at)
    route = e("route", [P, M, 36])
    r4 = e("r4", [P, 6, M, EXPERT_GROUPS])
    r8 = e("r8", [P, 12, M, PER_GROUP])
    r32 = e("r32", [P, M, EXPERT_GROUPS, PER_GROUP])
    r1 = e("r1", [P, 20, M])
    NCOL = EXPERTS + 4
    comb = e("comb", [P, M, NCOL])
    sel = e("sel", [P, M, NCOL])
    slot = e("slot", [P, M, NCOL])
    most = e("most", [P, 1])
    mosti = e("mosti", [P, 1], I32)
    diag2 = place("diag2", [P, D], F32, e.at)
    more = [place("more0", [P, KD * CH], F32, x1T_at), e("more1", [P, KD * CH])]

    with ExitStack() as ctx:
        bank = [ctx.enter_context(nc.psum_tensor(f"bank{n}", [P, 512], F32)) for n in range(8)]

        def sem(name):
            return ctx.enter_context(nc.semaphore(name))

        x_in = sem("x_in")
        rows_in = sem("rows_in")
        more_rows_in = sem("more_rows_in")
        pos_in = sem("pos_in")
        kv_w_in = sem("kv_w_in")
        cmp_w_in = sem("cmp_w_in")
        router_in = sem("router_in")
        x_again = sem("x_again")
        mod1_ready = sem("mod1_ready")
        first_hi = sem("first_hi")
        first_lo = sem("first_lo")
        h_hi = sem("h_hi")
        h_lo = sem("h_lo")
        whi_ready = sem("whi_ready")
        wlo_pool = sem("wlo_pool")
        wlo_dve = sem("wlo_dve")
        o_hi = sem("o_hi")
        ob_lo = sem("ob_lo")
        mT_hi = sem("mT_hi")
        mT_lo = sem("mT_lo")
        mT_sum = sem("mT_sum")
        gf_in = sem("gf_in")
        landed = [sem(f"landed{n}") for n in range(RING)]
        consts = sem("consts")
        product_done = sem("product_done")
        act_drained = sem("act_drained")
        dve_drained = sem("dve_drained")
        late_drained = sem("late_drained")
        act_step = sem("act_step")
        dve_step = sem("dve_step")
        tanh_c = sem("tanh_c")
        cond_ready = sem("cond_ready")
        squares = sem("squares")
        recip_ms = sem("recip_ms")
        rms_ready = sem("rms_ready")
        xn_ready = sem("xn_ready")
        angles = sem("angles")
        trig_ready = sem("trig_ready")
        tanh_br = sem("tanh_br")
        kvn_ready = sem("kvn_ready")
        roped = sem("roped")
        flat_ready = sem("flat_ready")
        tanh_hid = sem("tanh_hid")
        cmp_shift = sem("cmp_shift")
        cmp_exp = sem("cmp_exp")
        cmp_probs = sem("cmp_probs")
        unit_max = sem("unit_max")
        unit_exp = sem("unit_exp")
        unit_probs = sem("unit_probs")
        diag_ready = sem("diag_ready")
        x1n_ready = sem("x1n_ready")
        hi_ready = sem("hi_ready")
        lo_ready = sem("lo_ready")
        shift_ready = sem("shift_ready")
        y_ready = sem("y_ready")
        rt_shift = sem("rt_shift")
        rt_exp = sem("rt_exp")
        sel_ready = sem("sel_ready")
        most_ready = sem("most_ready")
        mlanded = [sem(f"mlanded{n}") for n in range(MRING)]
        pick_ready = sem("pick_ready")
        pickw_ready = sem("pickw_ready")
        xg_done = sem("xg_done")
        xgT_act = sem("xgT_act")
        xgT_dve = sem("xgT_dve")
        gu_done = sem("gu_done")
        tanh_g = sem("tanh_g")
        a_ready = sem("a_ready")
        turned = sem("turned")
        aT_ready = sem("aT_ready")
        put_done = sem("put_done")
        put_ready = sem("put_ready")
        down_half = sem("down_half")
        down_done = sem("down_done")
        yhi_ready = sem("yhi_ready")
        ylo_ready = sem("ylo_ready")
        sc_done = sem("sc_done")
        sc_drained = sem("sc_drained")
        silu_ready = sem("silu_ready")
        slots_moved = sem("slots_moved")
        result = sem("result")
        scaled = sem("scaled")
        half_done = sem("half_done")
        stored = sem("stored")

        ALL_CONSTS = 8 + 5

        def drains_until(name, engine):
            return sum(1 for _, who in ORDER[:INDEX[name] + 1] if who == engine)

        def made(eng, name):
            eng.wait_ge(product_done, INDEX[name] + 1)

        def drained(eng, name):
            who = ORDER[INDEX[name]][1]
            eng.wait_ge({"act": act_drained, "dve": dve_drained, "late": late_drained}[who], drains_until(name, who))

        def bank_of(name):
            return bank[INDEX[name] % 8]

        class Steps:

            def __init__(self, eng, s):
                self.eng, self.s, self.n = eng, s, 0

            def do(self, ins):
                ins.then_inc(self.s, 1)
                self.n += 1

            def settle(self):
                self.eng.wait_ge(self.s, self.n)

        def chunk(kind, n):
            return ring[:, CHUNK_AT[kind, n] % RING, :]

        def arrived(eng, kind, n):
            at = CHUNK_AT[kind, n]
            eng.wait_ge(landed[at % RING], 16 * (at // RING + 1))

        def split_part(kind, n):
            return whi[hi_buffer(kind, n)], ring_lo[:, CHUNK_AT[kind, n] % RING, :]

        def split_ready(eng, kind, n):
            mine = [c for c in SPLITS[:SPLITS.index((kind, n)) + 1] if by_pool(*c) == by_pool(kind, n)]
            eng.wait_ge(wlo_pool if by_pool(kind, n) else wlo_dve, len(mine))

        def user(kind, n):
            return CHUNKS[CHUNK_AT[kind, n]][0]

        def low_part(eng, kind, n):
            eng.wait_ge(whi_ready, SPLITS.index((kind, n)) + 1)
            hi, lo = split_part(kind, n)
            wd = WINC[n][1] - WINC[n][0] if kind == "win" else CH
            w = slice(0, KD * wd)
            eng.tensor_tensor(lo[:, w], chunk(kind, n)[:, w], hi[:, w].bitcast(F32), ALU.subtract).then_inc(
                wlo_pool if by_pool(kind, n) else wlo_dve, 1)

        def chunk_source(kind, n):
            if kind == "ada":
                return w_ada[:, n * CH:(n + 1) * CH].rearrange("(k p) n -> p k n", p=P)
            if kind == "win":
                lo, hi = WINC[n]
                return w_in[:, lo:hi].rearrange("(k p) n -> p k n", p=P)
            if kind == "mg":
                return w_in[:, MG + n * CH:MG + (n + 1) * CH].rearrange("(k p) n -> p k n", p=P)
            if kind in ("cmp1k", "cmp1v"):
                w = w_cmp1_k if kind == "cmp1k" else w_cmp1_v
                return w[n * D:(n + 1) * D, :].rearrange("(k p) n -> p k n", p=P)
            if kind in ("upa", "upb"):
                w = w_up_a if kind == "upa" else w_up_b
                return w[:, n * 512:(n + 1) * 512].rearrange("(k p) n -> p k n", p=P)
            return w_out[:, n * CH:(n + 1) * CH].rearrange("(k p) n -> p k n", p=P)

        def head_slot(h):
            return (h % 2) * PAIRS + h // 2

        E = RING + HI_SLOTS
        assert len(CHUNKS) % RING == 4
        MSLOTS = [5, 6, 4, E, E + 1, E + 2, 0, 1, 2, RING, RING + 1, 3]
        MFIRST = [2, 0, 1, 3, 4, 5, 13, 6, 7, 8, 10, 9, 11, 12, 14, 15]

        def slot_number(b, j, q):
            if b == 2 and q == 2:
                return 12 + j
            if b == 2 and j == 0:
                return 14 + q
            return PIECES * (2 * (b % 2) + j) + q

        def landings(b, j, q, eights):
            times = [c for c in range(4) if slot_number(c, j, q) == slot_number(b, j, q)]
            return eights * len(times) + times.index(b) + 1

        def mslot(n):
            if n >= 14:
                return fifth[:, n - 14, :]
            if n >= 12:
                return more[n - 12][:, :]
            at = MSLOTS[n]
            return ring[:, at, :] if at < E else extra[:, at - E, :]

        def gate_up_weights(b, j, k):
            n = slot_number(b, j, 0)
            if n >= 14:
                t, at = fifth, 0
            else:
                at = MSLOTS[n]
                t, at = (ring, at) if at < E else (extra, at - E)
            return t[:, at:at + 2, k * CH:(k + 1) * CH]

        def zero_rows(eng):
            eng.memset(yhi[:, :].bitcast(F32), 0.0)
            eng.memset(ylo[:, :].bitcast(F32), 0.0).then_inc(ylo_ready, 2)

        with nc.Block() as block:

            @block.sync
            def _(sp):
                for lo, src in ((R_G1, g_norm1.rearrange("a (k p) -> (a k) p", p=P)),
                                (R_G2, g_norm2.rearrange("a (k p) -> (a k) p", p=P))):
                    sp.dma_start(rows[lo:lo + src.shape[0], :], src).then_inc(rows_in, 16)
                sp.dma_start(xs[:, :, :], x[0].rearrange("(m p) d -> p m d", p=P)).then_inc(x_in, 16)
                for at, (_, kind, n) in enumerate(CHUNKS):
                    if kind == "out" and n == 0:
                        made(sp, "Tdsa0_1")
                        sp.dma_start(xr[:, :, :], x[0].rearrange("(m p) d -> p m d", p=P)).then_inc(x_again, 16)
                    if (kind, n) == ("win", 2):
                        sp.dma_start(w_kv[:, :], w_kv_up[0]).then_inc(kv_w_in, 16)
                        for j, w in enumerate((w_cmp2_k, w_cmp2_v)):
                            sp.dma_start(w2[:, j, :, :], w[0].rearrange("(t p) d -> p t d", p=P)).then_inc(cmp_w_in, 16)
                        sp.dma_start(wr[:, :, 0:EXPERT_GROUPS], w_router_group[0].rearrange("(k p) n -> p k n", p=P)).then_inc(router_in, 16)
                        sp.dma_start(wr[:, :, EXPERT_GROUPS:], w_router_expert[0].rearrange("(k p) n -> p k n", p=P)).then_inc(router_in, 16)
                        sp.dma_start(brow[:, 0:EXPERT_GROUPS], b_router_group[0].partition_broadcast(P)).then_inc(router_in, 16)
                        sp.dma_start(brow[:, EXPERT_GROUPS:], b_router_expert[0].partition_broadcast(P)).then_inc(router_in, 16)
                    if at >= RING:
                        made(sp, CHUNKS[at - RING][0])
                    src = chunk_source(kind, n)
                    dst = chunk(kind, n)[:, 0:src.shape[1] * src.shape[2]]
                    sp.dma_start(dst.rearrange("p (k n) -> p k n", k=src.shape[1]), src).then_inc(landed[at % RING], 16)

                def piece(i, q, n):
                    if q < 2:
                        w = w_expert_gate if q == 0 else w_expert_up
                        src = w[bass.ds(i, 1)].rearrange("o (k p) n -> p (o k) n", p=P)
                        dst = mslot(n).rearrange("p (k n) -> p k n", k=KD)
                    else:
                        src = w_expert_down[bass.ds(i, 1)].rearrange("o (k p) n -> p (o k) n", p=P)
                        dst = mslot(n).rearrange("p (k n) -> p k n", k=2)
                    sp.dma_start(dst, src).then_inc(mlanded[n], 16)

                def gate_and_up(first, b, experts=(0, 1)):
                    for j in experts:
                        for q in range(2):
                            piece(first + j, q, slot_number(b, j, q))

                def downs(first, b):
                    for j in range(2):
                        piece(first + j, 2, slot_number(b, j, 2))

                def first_free(n):
                    if n == 12:
                        made(sp, "rt1")
                        return
                    if n == 13:
                        made(sp, "gb3")
                        return
                    if n >= 14:
                        sp.wait_ge(lo_ready, 1)
                        return
                    at = MSLOTS[n]
                    if at < RING:
                        made(sp, CHUNKS[max(c for c in range(len(CHUNKS)) if c % RING == at)][0])
                    elif at < E:
                        made(sp, [user(*c) for c in SPLITS if hi_buffer(*c) == at - RING][-1])
                    else:
                        sp.wait_ge(mT_lo, KD)

                for n in MFIRST:
                    first_free(n)
                    if n < 12:
                        piece(n // PIECES, n % PIECES, n)
                    elif n < 14:
                        piece(4 + n - 12, 2, n)
                    else:
                        piece(4, n - 14, n)

                def stream(r):
                    base = r * (EXPERTS // 2)
                    with sp.Fori(0, EXPERTS // 8 - 1) as it:
                        at, pair = it * 8, base + it * 4
                        sp.wait_ge(gu_done, pair + 1)
                        gate_and_up(at + 4, 2, experts=(1,))
                        sp.wait_ge(down_done, pair + 1)
                        downs(at + 8, 0)
                        sp.wait_ge(gu_done, pair + 2)
                        gate_and_up(at + 6, 3)
                        sp.wait_ge(down_done, pair + 2)
                        downs(at + 6, 3)
                        sp.wait_ge(gu_done, pair + 3)
                        gate_and_up(at + 8, 0)
                        gate_and_up(at + 12, 2, experts=(0,))
                        sp.wait_ge(gu_done, pair + 4)
                        gate_and_up(at + 10, 1)
                        sp.wait_ge(down_done, pair + 4)
                        downs(at + 10, 1)
                        downs(at + 12, 2)
                    at, pair = EXPERTS - 8, base + EXPERTS // 2 - 4
                    sp.wait_ge(gu_done, pair + 1)
                    gate_and_up(at + 4, 2, experts=(1,))
                    sp.wait_ge(gu_done, pair + 2)
                    gate_and_up(at + 6, 3)
                    sp.wait_ge(down_done, pair + 2)
                    downs(at + 6, 3)

                stream(0)
                sp.wait_ge(most_ready, 1)
                count = sp.value_load(mosti[0:1, 0:1], min_val=0, max_val=S)
                with sp.Fori(1, ROUNDS) as r:
                    with sp.If(count > r * SLOTS):
                        sp.wait_ge(down_done, r * (EXPERTS // 2))
                        for b in range(2):
                            gate_and_up(2 * b, b)
                            downs(2 * b, b)
                        gate_and_up(4, 2, experts=(0,))
                        downs(4, 2)
                        stream(r)

            @block.gpsimd
            def _(g):
                for lo, src in ((R_PEK, pe_cmp_k[0].rearrange("(j e) d -> j (e d)", e=2)),
                                (R_PEV, pe_cmp_v[0].rearrange("(j e) d -> j (e d)", e=2))):
                    g.dma_start(rows[lo:lo + src.shape[0], :], src).then_inc(more_rows_in, 16)
                g.memset(ident[:, :], 0.0).then_inc(consts, 1)
                g.memset(ones[:, :], 1.0).then_inc(consts, 1)
                g.memset(tri[:, :], 1.0).then_inc(consts, 1)
                g.memset(cbias[:, :, :], 0.0).then_inc(consts, 1)
                g.memset(cbc[:, :, :], 0.0).then_inc(consts, 1)
                g.memset(cmk[:, :, :], 1.0).then_inc(consts, 1)
                g.iota(iota_slot[:, :], [[1, SLOTS]], base=0, channel_multiplier=0,
                       allow_small_or_imprecise_dtypes=True).then_inc(consts, 1)
                g.iota(iota8[:, :], [[1, 8]], base=0, channel_multiplier=0,
                       allow_small_or_imprecise_dtypes=True).then_inc(consts, 1)
                g.wait_ge(consts, 8)
                g.affine_select(out=ident[:, :], in_=ident[:, :], compare_op=ALU.not_equal, fill=1.0, base=0,
                                pattern=[[-1, P]], channel_multiplier=1).then_inc(consts, 1)
                g.affine_select(out=tri[:, :], in_=tri[:, :], compare_op=ALU.is_gt, fill=0.0, base=0,
                                pattern=[[1, P]], channel_multiplier=-1).then_inc(consts, 1)
                g.affine_select(out=cbias[:, :, :], in_=cbias[:, :, :], compare_op=ALU.is_ge, fill=NEG, base=0,
                                pattern=[[P, M], [-1, S]], channel_multiplier=1).then_inc(consts, 1)
                for t, fill in ((cbc, NEG), (cmk, 0.0)):
                    g.affine_select(out=t[:, :, :], in_=t[:, :, :], compare_op=ALU.is_ge, fill=fill,
                                    base=-(CMP_LEN - 1), pattern=[[P, M], [-CMP_STRIDE, NCMP]],
                                    channel_multiplier=1).then_inc(consts, 1)
                for kind, n in SPLITS:
                    if by_pool(kind, n):
                        low_part(g, kind, n)
                    if kind == "upb" and n == 0:
                        g.wait_ge(o_hi, 1)
                        g.tensor_tensor(oblo[:, :, :], obT[:, :, :], obhi[:, :, :].bitcast(F32), ALU.subtract).then_inc(ob_lo, 1)
                g.wait_ge(x1n_ready, 1)
                g.wait_ge(hi_ready, 1)
                g.tensor_tensor(x1lo[:, :, :], x1n[:, :, :], x1hi[:, :, :].bitcast(F32), ALU.subtract).then_inc(lo_ready, 1)
                zero_rows(g)

            @block.scalar
            def _(act):
                step = Steps(act, act_step)
                for lo, src in ((R_C, c.rearrange("a (k p) -> (a k) p", p=P)),
                                (R_BADA, b_ada.rearrange("a (k p) -> (a k) p", p=P)),
                                (R_GKV, g_kv_latent)):
                    act.dma_start(rows[lo:lo + src.shape[0], :], src).then_inc(rows_in, 16)
                act.dma_start(posi[:, :], positions[0].rearrange("(m p) -> p m", p=P), allow_slow_non_contiguous=True).then_inc(pos_in, 16)

                def root(n, t):
                    act.wait_ge(recip_ms, n)
                    act.activation(t, t, ACT.Sqrt).then_inc(rms_ready, 1)

                drained(act, "rows")
                act.activation(condT[:, :], cols[:, R_C:R_C + KD], ACT.Tanh, scale=0.5).then_inc(tanh_c, 1)
                act.wait_ge(x_in, 16)
                for m in range(M):
                    if m:
                        step.settle()
                    ins = act.activation(junk[:, :], xs[:, m, :], ACT.Square, accum_out=tiny[:, m:m + 1])
                    if m == M - 1:
                        ins.then_inc(squares, 1)
                    else:
                        step.do(ins)
                root(1, tiny[:, 0:M])
                act.wait_ge(angles, 1)
                act.activation(trig[:, 10:12, :], trig[:, 8:10, :], ACT.Sin).then_inc(trig_ready, 1)

                def high_part(kind, n, halves=False):
                    at = SPLITS.index((kind, n))
                    before = [c for c in SPLITS[:at] if hi_buffer(*c) == hi_buffer(kind, n)]
                    if before:
                        made(act, user(*before[-1]))
                    arrived(act, kind, n)
                    wd = WINC[n][1] - WINC[n][0] if kind == "win" else CH
                    w = slice(0, KD * wd)
                    if halves:
                        half, w = slice(0, KD * wd // 2), slice(KD * wd // 2, KD * wd)
                        act.activation(split_part(kind, n)[0][:, half], chunk(kind, n)[:, half], ACT.Copy).then_inc(first_hi, 1)
                    act.activation(split_part(kind, n)[0][:, w], chunk(kind, n)[:, w], ACT.Copy).then_inc(whi_ready, 1)

                act.wait_ge(mod1_ready, 1)
                for n in HT_ORDER:
                    name = f"xT{n}"
                    if n == 3:
                        high_part("win", 0, halves=True)
                    if n == 1:
                        made(act, name)
                        for kk in range(2):
                            k = 2 * n + kk
                            ins = act.activation(hT[:, k, :], bank_of(name)[:, kk * S:kk * S + S], ACT.Identity,
                                                 scale=A1[:, k:k + 1], bias=modT[:, k:k + 1])
                        ins.then_inc(act_drained, 1)
                    drained(act, name)
                    act.activation(hThi[:, 2 * n:2 * n + 2, :], hT[:, 2 * n:2 * n + 2, :], ACT.Copy).then_inc(h_hi, 1)
                for n in (1, 2):
                    high_part("win", n)

                def copy_out(name, dst, src):
                    made(act, name)
                    act.activation(dst, src, ACT.Copy).then_inc(act_drained, 1)

                def win(n):
                    lo, hi = WINC[n]
                    w = hi - lo
                    copy_out(f"win{n}", xp[:, :, lo:hi], bank_of(f"win{n}")[:, 0:M * w].rearrange("p (m n) -> p m n", m=M))

                def mg(n):
                    made(act, f"mg{n}")
                    act.activation(gT[:, 2 * n:2 * n + 2, :], bank_of(f"mg{n}")[:, :].rearrange("p (t n) -> p t n", t=2),
                                   ACT.Tanh, scale=0.5).then_inc(act_drained, 1)
                    if n + 2 < KD:
                        high_part("mg", n + 2)

                for n in range(3):
                    win(n)
                    high_part("win", n + 3)
                drained(act, "win2")
                for m in range(M):
                    if m:
                        step.settle()
                    ins = act.activation(junk[:, 0:RANK], xp[:, m, KV:KV + RANK], ACT.Square, accum_out=tiny[:, 2 + m:3 + m])
                    if m == M - 1:
                        ins.then_inc(squares, 1)
                    else:
                        step.do(ins)
                for n in range(3, len(WINC)):
                    win(n)
                    if n + 3 < len(WINC):
                        high_part("win", n + 3)
                    elif n < len(WINC) - 1:
                        high_part("mg", n + 3 - len(WINC))
                root(2, tiny[:, 2:2 + M])
                drained(act, f"win{len(WINC) - 1}")
                act.activation(gates[:, :, :], xp[:, :, BR:BR + 3 * HEADS], ACT.Tanh, scale=0.5).then_inc(tanh_br, 1)
                mg(0)
                mg(1)
                for n in range(4):
                    m, half = n // 2, n % 2
                    copy_out(f"kvp{n}", kvx[:, m, half * 512:half * 512 + 512], bank_of(f"kvp{n}")[:, :])
                copy_out("iqT", iqT[:, :, :], bank_of("iqT")[:, :].rearrange("p (t n) -> p t n", t=2))
                copy_out("ikT", ikT[:, :], bank_of("ikT")[:, 0:S])
                copy_out("cmpx", cx[:, :, :, :], bank_of("cmpx")[:, :].rearrange("p (a g n) -> p a g n", a=2, g=2))
                for n in range(2):
                    copy_out(f"qbT{n}", qbT[:, 2 * n:2 * n + 2, :], bank_of(f"qbT{n}")[:, :].rearrange("p (t n) -> p t n", t=2))
                copy_out("ksT", ksT[:, :, :], bank_of("ksT")[:, :].rearrange("p (t n) -> p t n", t=2))
                copy_out("kwT", kwT[:, :, :], bank_of("kwT")[:, :].rearrange("p (t n) -> p t n", t=2))
                mg(2)
                for n in range(8):
                    m, r = n // 4, n % 4
                    nk = P * (m + 1)
                    made(act, f"il{n}")
                    act.activation(relu[m][:, r:HEADS:4, 0:nk], bank_of(f"il{n}")[:, 0:2 * nk].rearrange("p (t n) -> p t n", t=2),
                                   ACT.Relu).then_inc(act_drained, 1)
                made(act, "cmp1")
                for lo in (0, HD):
                    act.activation(hth[lo:lo + GROUPS * NCMP, :], bank_of("cmp1")[lo:lo + GROUPS * NCMP, 0:CMP_HIDDEN],
                                   ACT.Tanh, scale=0.5).then_inc(tanh_hid, 1)
                mg(3)

                def exps(u):
                    kind, m = UNITS[u]
                    nk = P * (m + 1)
                    act.wait_ge(unit_max, u + 1)
                    p = probs[u % 2]
                    so = 4 * (u % 2)
                    for h in range(HEADS):
                        ins = act.activation(p[:, h, 0:nk], p[:, h, 0:nk], ACT.Exp, bias=stats[:, so + 1, h:h + 1],
                                             accum_out=stats[:, so + 2, h:h + 1])
                    ins.then_inc(unit_exp, 1)

                def turns(u):
                    kind, m = UNITS[u]
                    for n in range(2 * (m + 1)):
                        name = f"T{kind}{m}_{n}"
                        copy_out(name, pT[u % 2][:, 4 * n:4 * n + 4, :], bank_of(name)[:, :].rearrange("p (t n) -> p t n", t=4))

                def pv(name, dst, m):
                    copy_out(name, dst[:, :, m * P:m * P + P], bank_of(name)[:, :].rearrange("p (t n) -> p t n", t=PAIRS))

                exps(0)
                exps(1)
                act.wait_ge(cmp_shift, 1)
                act.activation(smc[:, :, :, :], smc[:, :, :, :], ACT.Exp, scale=SCALE).then_inc(cmp_exp, 1)
                mg(4)
                for n in range(4):
                    name = f"pcT{n}"
                    made(act, name)
                    act.activation(pcT[0:NCMP, 4 * n:4 * n + 4, :], bank_of(name)[0:NCMP, :].rearrange("p (t n) -> p t n", t=4),
                                   ACT.Copy).then_inc(act_drained, 1)
                for t, name in ((qaT, "qaT"), (kaT, "kaT")):
                    if name == "kaT":
                        mg(5)
                    for n in range(2):
                        copy_out(f"{name}{n}", t[:, 2 * n:2 * n + 2, :], bank_of(f"{name}{n}")[:, :].rearrange("p (t n) -> p t n", t=2))
                turns(0)
                turns(1)
                exps(2)
                exps(3)
                mg(6)
                mg(7)
                pv("PVb0", obT, 0)
                turns(2)
                exps(4)
                turns(3)
                pv("PVb1", obT, 1)
                high_part("upa", 0)
                high_part("upb", 0)
                exps(5)
                turns(4)
                made(act, "Sdsa1_3")
                drained(act, "PVb1")
                act.activation(obhi[:, :, :], obT[:, :, :], ACT.Copy).then_inc(o_hi, 1)

                def pv_a_high(m):
                    name = f"PVa{m}"
                    made(act, name)
                    act.activation(oahi[:, :, m * P:(m + 1) * P], bank_of(name)[:, :].rearrange("p (t n) -> p t n", t=PAIRS), ACT.Copy).then_inc(o_hi, 1)

                pv_a_high(0)
                turns(5)
                pv_a_high(1)
                for kind in ("upa", "upb"):
                    high_part(kind, 1)
                for n in range(2):
                    copy_out(f"gb{n}", gt1bc[:, n * 512:n * 512 + 512], bank_of(f"gb{n}")[:, :])

                def x1_squares(n):
                    drained(act, f"out{n}")
                    for m in range(M):
                        step.settle()
                        ins = act.activation(x1sq[:, m, :], x1[:, m, n * CH:(n + 1) * CH], ACT.Square,
                                             accum_out=tiny[:, 8 + 4 * m + n:9 + 4 * m + n])
                        if n == 3 and m == M - 1:
                            ins.then_inc(squares, 1)
                        else:
                            step.do(ins)

                def x1_turned(n):
                    copy_out(f"x1T{n}", x1T[:, 2 * n:2 * n + 2, :], bank_of(f"x1T{n}")[:, :].rearrange("p (t n) -> p t n", t=2))

                for t in range(KD):
                    act.wait_ge(mT_sum, t + 1)
                    act.activation(mThi[:, t, :], mT[:, t, :], ACT.Copy).then_inc(mT_hi, 1)
                    if t == 4:
                        high_part("out", 0)
                        high_part("out", 1)
                made(act, "up7")
                high_part("out", 2)
                high_part("out", 3)
                copy_out("gb2", gt2bc[:, 0:512], bank_of("gb2")[:, :])
                x1_squares(0)
                copy_out("gb3", gt2bc[:, 512:], bank_of("gb3")[:, :])
                x1_squares(1)
                x1_turned(0)
                x1_squares(2)
                x1_turned(1)
                step.settle()
                step.do(act.activation(tiny[:, 16:17], ident[:, 0:1], ACT.Sqrt))
                x1_squares(3)
                x1_turned(2)
                root(3, tiny[:, 4:4 + M])
                x1_turned(3)
                act.dma_start(gfbc[:, :], g_final.partition_broadcast(P)).then_inc(gf_in, 16)
                act.wait_ge(x1n_ready, 1)
                act.activation(x1hi[:, :, :], x1n[:, :, :], ACT.Copy).then_inc(hi_ready, 1)
                act.wait_ge(rt_shift, 1)
                act.activation(r4[:, 1, :, :], r4[:, 0, :, :], ACT.Exp).then_inc(rt_exp, 1)
                act.wait_ge(rt_shift, 2)
                act.activation(r1[:, 6, :], r1[:, 5, :], ACT.Exp).then_inc(rt_exp, 1)

                def xg_out(g, buf, pb):
                    act.wait_ge(xg_done, 4 * g + 2 * pb + 1)
                    for j in range(2):
                        k = 4 * pb + j
                        ins = act.activation(xgT[buf][:, k, :], bank[0][:, j * 256:(j + 1) * 256], ACT.Identity,
                                             scale=A2[:, k:k + 1], bias=modT[:, 24 + k:25 + k])
                    ins.then_inc(xgT_act, 1)

                def rounds(r, late=False):
                    if late:
                        act.wait_ge(gu_done, r * (EXPERTS // 2))
                    for pb in range(2):
                        xg_out(r * (QUADS + 1), 0, pb)
                    with act.Fori(0, QUADS // 2) as it:
                        for b in range(4):
                            pair = r * (EXPERTS // 2) + it * 4 + b
                            q, pb = b // 2, b % 2
                            act.wait_ge(gu_done, pair + 1)
                            act.wait_ge(aT_ready, pair + 1)
                            act.activation(thg[:, :], bank[2 + pb][:, 0:FF], ACT.Tanh, scale=0.5).then_inc(tanh_g, 1)
                            xg_out(r * (QUADS + 1) + it * 2 + q + 1, 1 - q, pb)
                            for n in range(2):
                                s = slice(n * 512, n * 512 + 512)
                                act.wait_ge(y_ready, 2 * pair + n + 1)
                                act.activation(yhi[:, s], y[:, s], ACT.Copy).then_inc(yhi_ready, 1)

                act.wait_ge(most_ready, 1)
                count = act.value_load(mosti[0:1, 0:1], min_val=0, max_val=S)
                rounds(0)
                with act.If(count > SLOTS):
                    with act.Fori(1, ROUNDS) as r:
                        with act.If(count > r * SLOTS):
                            rounds(r, late=True)

                step.do(act.activation(tiny[:, 17:18], ident[:, 0:1], ACT.Sqrt))
                act.wait_ge(result, 1)
                for m, squared in enumerate((yhi, ylo)):
                    act.activation(squared[:, :], x1[:, m, :], ACT.Square, accum_out=tiny[:, 6 + m:7 + m]).then_inc(squares, 1)
                root(4, tiny[:, 6:6 + M])
                act.wait_ge(scaled, 2)
                act.wait_ge(rms_ready, 4)
                act.activation(x1n[:, 1, :], x1n[:, 1, :], ACT.Copy, scale=tiny[:, 7:8]).then_inc(half_done, 1)
                for m in range(M):
                    if m:
                        act.wait_ge(half_done, 1)
                    else:
                        act.wait_ge(result, 2)
                    act.dma_start(out[0, m * P:(m + 1) * P, :], x1n[:, m, :]).then_inc(stored, 16)
                act.wait_ge(stored, 16 * M)

            @block.vector
            def _(dve):
                step = Steps(dve, dve_step)
                do, settle = step.do, step.settle

                def drain_done(ins):
                    ins.then_inc(dve_drained, 1)

                def mean_square(n, t, width):
                    dve.wait_ge(squares, n)
                    do(dve.tensor_scalar(t, t, 1.0 / width, EPS, ALU.mult, ALU.add))
                    settle()
                    dve.reciprocal(t, t).then_inc(recip_ms, 1)

                made(dve, "rows")
                drain_done(dve.tensor_copy(cols[:, :], bank_of("rows")[:, 0:R_END]))
                mean_square(1, tiny[:, 0:M], D)
                dve.wait_ge(tanh_c, 1)
                do(dve.scalar_tensor_tensor(condT[:, :], condT[:, :], 1.0, cols[:, R_C:R_C + KD], ALU.add, ALU.mult))
                settle()
                dve.tensor_scalar(condB[:, :, :], condT[:, :].unsqueeze(2).to_broadcast([P, KD, 32]), 0.5, None, ALU.mult).then_inc(cond_ready, 1)
                dve.wait_ge(rms_ready, 1)
                for m in range(M):
                    dve.tensor_scalar(xs[:, m, :], xs[:, m, :], tiny[:, m:m + 1], None, ALU.mult).then_inc(xn_ready, 1)

                freq = (THETA ** (-np.arange(8, dtype=np.float32) / 8)).astype(np.float32)
                for n in range(8):
                    do(dve.memset(trig[:, 0, n:M * 8:8], float(freq[n])))
                dve.wait_ge(pos_in, 16)
                do(dve.tensor_copy(stats[:, 0, 0:M], posi[:, :]))
                settle()
                for m in range(M):
                    do(dve.tensor_scalar(trig[:, 1, m * 8:m * 8 + 8], trig[:, 0, m * 8:m * 8 + 8], stats[:, 0, m:m + 1], None, ALU.mult))
                settle()
                magic = 1.5 * 2.0 ** 23
                do(dve.tensor_scalar(trig[:, 2, :], trig[:, 1, :], float(1 / (2 * np.pi)), magic, ALU.mult, ALU.add))
                settle()
                do(dve.tensor_scalar(trig[:, 3, :], trig[:, 2, :], -magic, None, ALU.add))
                settle()
                two_pi = 2 * np.pi
                part1 = 6.28125
                part2 = float(np.float32(np.round((two_pi - part1) * 2 ** 22) / 2 ** 22))
                part3 = float(two_pi - part1 - part2)
                for n, part in enumerate((part1, part2, part3)):
                    do(dve.scalar_tensor_tensor(trig[:, 4 + n, :], trig[:, 3, :], -part, trig[:, 1 if n == 0 else 3 + n, :], ALU.mult, ALU.add))
                    settle()
                lim = float(np.nextafter(np.float32(np.pi), np.float32(0)))
                do(dve.tensor_scalar(trig[:, 8, :], trig[:, 6, :], lim, -lim, ALU.min, ALU.max))
                settle()
                do(dve.scalar_tensor_tensor(trig[:, 7, :], trig[:, 8, :], -1.0, trig[:, 8, :], ALU.mult, ALU.max))
                settle()
                dve.tensor_scalar(trig[:, 9, :], trig[:, 7, :], -1.0, float(np.float32(np.pi / 2)), ALU.mult, ALU.add).then_inc(angles, 1)
                dve.wait_ge(trig_ready, 1)
                for n, row in enumerate((11, 10)):
                    src = trig[:, row, :].rearrange("p (m f) -> p m f", m=M)
                    for half in range(2):
                        do(dve.tensor_copy(c16[:, n, :, half * 8:half * 8 + 8], src))
                        do(dve.tensor_copy(c8[:, n, :, half * 4:half * 4 + 4], src[:, :, 0:8:2]))
                settle()

                def ada(n):
                    made(dve, f"ada{n}")
                    drain_done(dve.tensor_copy(adaR[n % 2][:, :], bank_of(f"ada{n}")[:, 0:CH]))

                def adt(n):
                    made(dve, f"adt{n}")
                    drain_done(dve.tensor_tensor(modT[:, 8 * n:8 * n + 8].rearrange("p (q c) -> p c q", c=2),
                                                 bank_of(f"adt{n}")[:, 0:2 * P].rearrange("p (c q) -> p c q", c=2)[:, :, 0:P:32],
                                                 cols[:, R_BADA + 8 * n:R_BADA + 8 * n + 8].rearrange("p (q c) -> p c q", c=2), ALU.add))

                def hT_low(n):
                    dve.wait_ge(h_hi, 1 + HT_ORDER.index(n))
                    s = slice(2 * n, 2 * n + 2)
                    dve.tensor_tensor(hTlo[:, s, :], hT[:, s, :], hThi[:, s, :].bitcast(F32), ALU.subtract).then_inc(h_lo, 1)

                ada(0)
                ada(1)
                adt(0)
                adt(1)
                drained(dve, "adt1")
                do(dve.scalar_tensor_tensor(A1[:, :], modT[:, 8:16], 1.0, cols[:, R_G1:R_G1 + KD], ALU.add, ALU.mult))
                settle()
                dve.memset(tiny[:, 60:61], 0.0).then_inc(mod1_ready, 1)
                for n in (0, 2, 3):
                    name = f"xT{n}"
                    made(dve, name)
                    for kk in range(2):
                        k = 2 * n + kk
                        ins = dve.tensor_scalar(hT[:, k, :], bank_of(name)[:, kk * S:kk * S + S], A1[:, k:k + 1],
                                                modT[:, k:k + 1], ALU.mult, ALU.add)
                    ins.then_inc(late_drained, 1)
                hi, lo = split_part("win", 0)
                mid, end = KD * WIN_FIRST // 2, KD * WIN_FIRST
                hT_low(0)
                hT_low(1)
                dve.wait_ge(first_hi, 1)
                dve.tensor_tensor(lo[:, 0:mid], chunk("win", 0)[:, 0:mid], hi[:, 0:mid].bitcast(F32), ALU.subtract).then_inc(first_lo, 1)
                hT_low(2)
                dve.wait_ge(whi_ready, 1)
                dve.tensor_tensor(lo[:, mid:end], chunk("win", 0)[:, mid:end], hi[:, mid:end].bitcast(F32), ALU.subtract).then_inc(wlo_dve, 1)
                hT_low(3)

                def rotate(xv, heads, table, rot, final=None):
                    half = rot // 2
                    av, bv = ropeA[:, :, 0:heads, 0:rot], ropeB[:, :, 0:heads, 0:rot]
                    cosv = table[:, 0].unsqueeze(2).to_broadcast([P, M, heads, rot])
                    sinv = table[:, 1].unsqueeze(2).to_broadcast([P, M, heads, rot])
                    do(dve.tensor_tensor(av, xv[:, :, :, 0:rot], cosv, ALU.mult))
                    do(dve.tensor_tensor(bv, xv[:, :, :, 0:rot], sinv, ALU.mult))
                    settle()
                    do(dve.tensor_tensor(xv[:, :, :, 0:half], av[:, :, :, 0:half], bv[:, :, :, half:rot], ALU.subtract))
                    ins = dve.tensor_tensor(xv[:, :, :, half:rot], av[:, :, :, half:rot], bv[:, :, :, 0:half], ALU.add)
                    do(ins)
                    settle()

                def heads_of(col, heads, width):
                    return xp[:, :, col:col + heads * width].rearrange("p m (h w) -> p m h w", w=width)

                mean_square(2, tiny[:, 2:2 + M], RANK)
                drained(dve, "win3")
                rotate(heads_of(IQ, IDX_HEADS, IDX_DIM), IDX_HEADS, c8, IDX_ROT)
                rotate(heads_of(IK, 1, IDX_DIM), 1, c8, IDX_ROT)
                for n in range(4):
                    do(dve.tensor_copy(kdup[:, :, 4, n * IDX_DIM:(n + 1) * IDX_DIM], xp[:, :, IK:IK + IDX_DIM]))
                settle()
                dve.wait_ge(rms_ready, 2)
                for m in range(M):
                    dve.tensor_scalar(kvn[:, m, :], xp[:, m, KV:KV + RANK], tiny[:, 2 + m:3 + m], None, ALU.mult).then_inc(kvn_ready, 1)
                drained(dve, f"win{len(WINC) - 1}")
                rotate(heads_of(QB, HEADS + GROUPS, HD), HEADS + GROUPS, c16, ROT)
                for n, col in enumerate((KS, KW)):
                    rotate(heads_of(col, GROUPS, HD), GROUPS, c16, ROT)
                    for twice in range(2):
                        do(dve.tensor_copy(kdup[:, :, 2 * n:2 * n + 2, twice * HD:(twice + 1) * HD], heads_of(col, GROUPS, HD)))
                settle()
                dve.memset(tiny[:, 61:62], 0.0).then_inc(roped, 1)
                made(dve, "kvT")
                drain_done(dve.tensor_scalar(kvnT[:, :], bank_of("kvT")[:, 0:S], cols[:, R_GKV:R_GKV + 1], None, ALU.mult))
                rotate(heads_of(QA, HEADS, HD), HEADS, c16, ROT)
                dve.wait_ge(tanh_br, 1)
                do(dve.tensor_scalar(gates[:, :, :], gates[:, :, :], 0.5, 0.5, ALU.mult, ALU.add))
                settle()

                drained(dve, "cmpx")
                for n in range(2):
                    pe = cols[:, (R_PEK, R_PEV)[n]:(R_PEK, R_PEV)[n] + CMP_TILES]
                    for gi in range(GROUPS):
                        src = cx[:, n, gi, :]
                        win_ap = overlap(src)
                        ins = dve.tensor_tensor(flat[:, n, :, gi * NCMP:(gi + 1) * NCMP], win_ap,
                                                pe.unsqueeze(2).to_broadcast([P, CMP_TILES, NCMP]), ALU.add)
                        do(ins)
                settle()
                dve.memset(tiny[:, 62:63], 0.0).then_inc(flat_ready, 1)
                drained(dve, "kvp3")
                rotate(kvx[:, :, 0:HEADS * HD].rearrange("p m (h w) -> p m h w", w=HD), HEADS, c16, ROT)
                dve.memset(tiny[:, 61:62], 0.0).then_inc(roped, 1)

                def index_scores():
                    for m in range(M):
                        nk = P * (m + 1)
                        drained(dve, f"il{4 * m + 3}")
                        for h in range(IDX_HEADS):
                            prev = cbias[:, m, 0:nk] if h == 0 else abias[:, m, 0:nk]
                            do(dve.scalar_tensor_tensor(abias[:, m, 0:nk], relu[m][:, h, 0:nk], xp[:, m, IW + h:IW + h + 1],
                                                        prev, ALU.mult, ALU.add))
                            settle()

                def select(m):
                    nk = P * (m + 1)
                    for n in range(TOPK // 8):
                        do(dve.max(stats[:, 11, :], abias[:, m, 0:nk]))
                        settle()
                        do(dve.match_replace(abias[:, m, 0:nk], stats[:, 11, :], abias[:, m, 0:nk], -3e38))
                        settle()
                    do(dve.tensor_scalar(abias[:, m, 0:nk], abias[:, m, 0:nk], -2e38, NEG, ALU.is_gt, ALU.mult))
                    settle()
                    do(dve.tensor_tensor(abias[:, m, 0:nk], abias[:, m, 0:nk], cbias[:, m, 0:nk], ALU.min))
                    settle()

                def scores(u):
                    kind, m = UNITS[u]
                    nk = P * (m + 1)
                    per = PAIRS // (m + 1)
                    p, so = probs[u % 2], 4 * (u % 2)
                    mask = (abias if kind == "dsa" else cbias)[:, m, 0:nk]
                    if u >= 2:
                        made(dve, f"T{UNITS[u - 2][0]}{UNITS[u - 2][1]}_{2 * UNITS[u - 2][1] + 1}")
                    for n in range(2 * (m + 1)):
                        name = f"S{kind}{m}_{n}"
                        made(dve, name)
                        for j in range(per):
                            hs = (n % 2) * PAIRS + (n // 2) * per + j
                            ins = dve.tensor_tensor_reduce(p[:, hs, 0:nk], bank_of(name)[:, j * nk:(j + 1) * nk], mask,
                                                           SCALE, -3e38, ALU.add, ALU.max, stats[:, so, hs:hs + 1])
                        drain_done(ins)
                    drained(dve, f"S{kind}{m}_{2 * m + 1}")
                    dve.tensor_scalar(stats[:, so + 1, :], stats[:, so, :], -1.0, None, ALU.mult).then_inc(unit_max, 1)

                def normalise(u):
                    kind, m = UNITS[u]
                    nk = P * (m + 1)
                    p, so = probs[u % 2], 4 * (u % 2)
                    dve.wait_ge(unit_exp, u + 1)
                    do(dve.reciprocal(stats[:, so + 3, :], stats[:, so + 2, :]))
                    settle()
                    if kind != "dsa":
                        branch = 1 if kind == "sel" else 2
                        for par in range(2):
                            s = stats[:, so + 3, par * PAIRS:(par + 1) * PAIRS]
                            do(dve.tensor_tensor(s, s, gates[:, m, 3 * par + branch:3 * HEADS:6], ALU.mult))
                        settle()
                    dve.tensor_tensor(p[:, :, 0:nk], p[:, :, 0:nk], stats[:, so + 3, :].unsqueeze(2).to_broadcast([P, HEADS, nk]),
                                      ALU.mult).then_inc(unit_probs, 1)

                def pv_a_low(m):
                    dve.wait_ge(o_hi, 2 + m)
                    drain_done(dve.tensor_tensor(oalo[:, :, m * P:(m + 1) * P], bank_of(f"PVa{m}")[:, :].rearrange("p (t n) -> p t n", t=PAIRS),
                                                 oahi[:, :, m * P:(m + 1) * P].bitcast(F32), ALU.subtract))

                index_scores()
                made(dve, "kwT")
                do(dve.memset(hid[:, :], 0.0))
                settle()
                dve.wait_ge(tanh_hid, 2)
                for lo in (0, HD):
                    r = slice(lo, lo + GROUPS * NCMP)
                    ins = dve.scalar_tensor_tensor(hid[r, :], hth[r, :], 1.0, bank_of("cmp1")[r, 0:CMP_HIDDEN], ALU.add, ALU.mult)
                drain_done(ins)
                made(dve, "cmpT")
                drain_done(dve.tensor_copy(hidT[:, :, :], bank_of("cmpT")[:, 0:2 * 96].rearrange("p (t n) -> p t n", t=2)))
                made(dve, "cmp2")
                do(dve.tensor_scalar(kcT[:, :], bank_of("cmp2")[:, 0:GROUPS * NCMP], 0.5, None, ALU.mult))
                drain_done(dve.tensor_scalar(vcs[0:NCMP, :, :], bank_of("cmp2")[0:NCMP, 64:64 + GROUPS * HD].rearrange("p (g d) -> p g d", g=GROUPS),
                                             0.5, None, ALU.mult))
                scores(0)
                scores(1)
                for par in range(2):
                    made(dve, f"sc{par}")
                    drain_done(dve.tensor_tensor(smc[:, :, par * PAIRS:(par + 1) * PAIRS, :],
                                                 bank_of(f"sc{par}")[:, 0:M * PAIRS * NCMP].rearrange("p (m i c) -> p m i c", m=M, i=PAIRS),
                                                 cbc[:, :, :].unsqueeze(2).to_broadcast([P, M, PAIRS, NCMP]), ALU.add))
                drained(dve, "sc1")
                cmax = stats[:, 8:10, :]
                do(dve.tensor_reduce(cmax, smc[:, :, :, :], AX, ALU.max))
                settle()
                dve.tensor_tensor(smc[:, :, :, :], smc[:, :, :, :], cmax.unsqueeze(3).to_broadcast([P, M, HEADS, NCMP]),
                                  ALU.subtract).then_inc(cmp_shift, 1)
                dve.wait_ge(cmp_exp, 1)
                do(dve.tensor_tensor(smc[:, :, :, :], smc[:, :, :, :], cmk[:, :, :].unsqueeze(2).to_broadcast([P, M, HEADS, NCMP]), ALU.mult))
                settle()
                do(dve.tensor_reduce(cmax, smc[:, :, :, :], AX, ALU.add))
                settle()
                do(dve.tensor_scalar_max(cmax, cmax, TINY))
                settle()
                do(dve.reciprocal(cmax, cmax))
                settle()
                for par in range(2):
                    do(dve.tensor_tensor(cmax[:, :, par * PAIRS:(par + 1) * PAIRS], cmax[:, :, par * PAIRS:(par + 1) * PAIRS],
                                         gates[:, :, 3 * par:3 * HEADS:6], ALU.mult))
                settle()
                dve.tensor_tensor(smc[:, :, :, :], smc[:, :, :, :], cmax.unsqueeze(3).to_broadcast([P, M, HEADS, NCMP]),
                                  ALU.mult).then_inc(cmp_probs, 1)

                normalise(0)
                normalise(1)
                ada(2)
                adt(2)
                scores(2)
                select(0)
                scores(3)
                normalise(2)
                ada(3)
                select(1)
                adt(3)
                scores(4)
                normalise(3)
                ada(4)
                adt(4)
                scores(5)
                normalise(4)
                low_part(dve, "upa", 0)
                ada(5)
                adt(5)
                normalise(5)
                pv_a_low(0)
                made(dve, "PVa0")
                drained(dve, "adt2")
                for k in range(KD):
                    ins = dve.tensor_scalar(diag[:, k * P:(k + 1) * P], ident[:, :], modT[:, 16 + k:17 + k], 0.5, ALU.mult, ALU.mult)
                ins.then_inc(diag_ready, 1)
                drained(dve, "adt5")
                do(dve.scalar_tensor_tensor(A2[:, :], modT[:, 32:40], 1.0, cols[:, R_G2:R_G2 + KD], ALU.add, ALU.mult))
                dve.wait_ge(router_in, 64)
                do(dve.tensor_tensor(wsh[:, :, :], wr[:, :, :], modT[:, 24:32].unsqueeze(2).to_broadcast([P, KD, 36]), ALU.mult))
                settle()
                do(dve.tensor_tensor(wr[:, :, :], wr[:, :, :], A2[:, :].unsqueeze(2).to_broadcast([P, KD, 36]), ALU.mult))
                settle()
                dve.tensor_reduce(wshs[:, :], wsh[:, :, :].rearrange("p k n -> p n k"), AX, ALU.add).then_inc(shift_ready, 1)
                pv_a_low(1)
                low_part(dve, "upa", 1)

                def merged_low(t):
                    dve.wait_ge(mT_hi, t + 1)
                    dve.tensor_tensor(mTlo[:, t, :], mT[:, t, :], mThi[:, t, :].bitcast(F32), ALU.subtract).then_inc(mT_lo, 1)

                drained(dve, "mg7")
                for t in range(KD):
                    if t == 2:
                        made(dve, "rsh")
                        drain_done(dve.tensor_tensor(brow[:, :], brow[:, :], bank_of("rsh")[:, 0:36], ALU.add))
                    name = f"up{t}"
                    made(dve, name)
                    b = bank_of(name)
                    do(dve.scalar_tensor_tensor(mT[:, t, :], gT[:, t, :], 1.0, b[:, 0:S], ALU.add, ALU.mult))
                    drain_done(dve.scalar_tensor_tensor(tmp_up[:, t % 2, :], gT[:, KD + t, :], 1.0, b[:, S:2 * S], ALU.add, ALU.mult))
                    drained(dve, name)
                    settle()
                    dve.tensor_tensor(mT[:, t, :], mT[:, t, :], tmp_up[:, t % 2, :], ALU.add).then_inc(mT_sum, 1)
                    if t > 0:
                        merged_low(t - 1)
                merged_low(KD - 1)
                drained(dve, "adt5")
                dve.wait_ge(mT_lo, KD)
                for k in range(KD):
                    ins = dve.tensor_scalar(diag2[:, k * P:(k + 1) * P], ident[:, :], modT[:, 40 + k:41 + k], None, ALU.mult)
                ins.then_inc(diag_ready, 1)
                drained(dve, "gb1")
                dve.wait_ge(x_again, 16)
                for n in range(4):
                    name = f"out{n}"
                    made(dve, name)
                    xv = x1[:, :, n * CH:(n + 1) * CH]
                    do(dve.tensor_tensor(xv, bank_of(name)[:, :].rearrange("p (m n) -> p m n", m=M),
                                         gt1bc[:, n * CH:(n + 1) * CH].unsqueeze(1).to_broadcast([P, M, CH]), ALU.mult))
                    settle()
                    drain_done(dve.tensor_tensor(xv, xv, xr[:, :, n * CH:(n + 1) * CH], ALU.add))
                dve.wait_ge(squares, 3)
                do(dve.tensor_reduce(tiny[:, 4:4 + M], tiny[:, 8:16].rearrange("p (m n) -> p m n", m=M), AX, ALU.add))
                settle()
                mean_square(3, tiny[:, 4:4 + M], D)
                dve.wait_ge(rms_ready, 3)
                drained(dve, "out3")
                do(dve.tensor_scalar(x1n[:, 0, :], x1[:, 0, :], tiny[:, 4:5], None, ALU.mult))
                dve.tensor_scalar(x1n[:, 1, :], x1[:, 1, :], tiny[:, 5:6], None, ALU.mult).then_inc(x1n_ready, 1)

                drained(dve, "rsh")
                for m in range(M):
                    made(dve, f"rt{m}")
                    drain_done(dve.scalar_tensor_tensor(route[:, m, :], bank_of(f"rt{m}")[:, 0:36], tiny[:, 4 + m:5 + m], brow[:, :],
                                                        ALU.mult, ALU.add))
                drained(dve, "rt1")

                def bc(v, n):
                    return v.unsqueeze(2).to_broadcast([P, M, n])

                def first_greatest(values, greatest, cand, n):
                    do(dve.tensor_reduce(greatest, values, AX, ALU.max))
                    settle()
                    do(dve.tensor_tensor(cand, values, bc(greatest, n), ALU.is_ge))
                    settle()
                    do(dve.scalar_tensor_tensor(cand, cand, -1000.0, iota8[:, 0:n].unsqueeze(1).to_broadcast([P, M, n]), ALU.mult, ALU.add))
                    settle()
                    do(dve.tensor_reduce(r1[:, 10, :], cand, AX, ALU.min))
                    settle()
                    do(dve.tensor_tensor(cand, cand, bc(r1[:, 10, :], n), ALU.is_equal))
                    settle()

                lg = route[:, :, 0:EXPERT_GROUPS]
                oh4 = r4[:, 2]
                first_greatest(lg, r1[:, 0, :], oh4, EXPERT_GROUPS)
                dve.tensor_tensor(r4[:, 0], lg, bc(r1[:, 0, :], EXPERT_GROUPS), ALU.subtract).then_inc(rt_shift, 1)
                do(dve.tensor_tensor(r32[:, :, :, :], route[:, :, EXPERT_GROUPS:].rearrange("p m (g n) -> p m g n", g=EXPERT_GROUPS),
                                     oh4.unsqueeze(3).to_broadcast([P, M, EXPERT_GROUPS, PER_GROUP]), ALU.mult))
                settle()
                le = r8[:, 0]
                do(dve.tensor_reduce(le, r32[:, :, :, :].rearrange("p m g n -> p m n g"), AX, ALU.add))
                settle()
                first_greatest(le, r1[:, 1, :], r8[:, 1], PER_GROUP)
                do(dve.scalar_tensor_tensor(r8[:, 2], r8[:, 1], -3e38, le, ALU.mult, ALU.add))
                settle()
                first_greatest(r8[:, 2], r1[:, 2, :], r8[:, 3], PER_GROUP)
                dve.tensor_tensor(r1[:, 5, :], r1[:, 2, :], r1[:, 1, :], ALU.subtract).then_inc(rt_shift, 1)
                dve.wait_ge(rt_exp, 2)
                do(dve.tensor_reduce(r1[:, 3, :], r4[:, 1], AX, ALU.add))
                do(dve.tensor_scalar(r1[:, 7, :], r1[:, 6, :], 1.0, 2.0, ALU.add, ALU.mult))
                settle()
                do(dve.tensor_tensor(r1[:, 8, :], r1[:, 3, :], r1[:, 7, :], ALU.mult))
                settle()
                do(dve.reciprocal(r1[:, 8, :], r1[:, 8, :]))
                settle()
                do(dve.tensor_tensor(r1[:, 9, :], r1[:, 8, :], r1[:, 6, :], ALU.mult))
                settle()
                do(dve.tensor_tensor(r8[:, 4], r8[:, 1], bc(r1[:, 8, :], PER_GROUP), ALU.mult))
                do(dve.tensor_tensor(r8[:, 5], r8[:, 3], bc(r1[:, 9, :], PER_GROUP), ALU.mult))
                do(dve.tensor_tensor(r8[:, 6], r8[:, 1], r8[:, 3], ALU.add))
                settle()
                do(dve.tensor_tensor(r8[:, 4], r8[:, 4], r8[:, 5], ALU.add))
                do(dve.memset(comb[:, :, EXPERTS:], 0.0))
                do(dve.memset(slot[:, :, EXPERTS:], -1.0))
                settle()
                four = oh4.unsqueeze(3).to_broadcast([P, M, EXPERT_GROUPS, PER_GROUP])
                do(dve.tensor_tensor(comb[:, :, 0:EXPERTS].rearrange("p m (g n) -> p m g n", g=EXPERT_GROUPS), four,
                                     r8[:, 4].unsqueeze(2).to_broadcast([P, M, EXPERT_GROUPS, PER_GROUP]), ALU.mult))
                dve.tensor_tensor(sel[:, :, 0:EXPERTS].rearrange("p m (g n) -> p m g n", g=EXPERT_GROUPS), four,
                                  r8[:, 6].unsqueeze(2).to_broadcast([P, M, EXPERT_GROUPS, PER_GROUP]), ALU.mult).then_inc(sel_ready, 1)
                made(dve, "pos")
                dve.wait_ge(sel_ready, 1)
                do(dve.tensor_reduce(most[:, :], bank_of("pos")[:, 2 * EXPERTS:3 * EXPERTS], AX, ALU.max))
                settle()
                drain_done(dve.scalar_tensor_tensor(slot[:, :, 0:EXPERTS], bank_of("pos")[:, 0:2 * EXPERTS].rearrange("p (m n) -> p m n", m=M),
                                                    1.0, sel[:, :, 0:EXPERTS], ALU.add, ALU.mult))
                dve.tensor_copy(mosti[:, :], most[:, :]).then_inc(most_ready, 1)
                drained(dve, "pos")
                do(dve.tensor_scalar_add(slot[:, :, 0:EXPERTS], slot[:, :, 0:EXPERTS], -1.0))
                settle()

                def picks(first, buf, picked):
                    def of_experts(t):
                        return t[:, :, bass.ds(first, 4)].unsqueeze(3).to_broadcast([P, M, 4, SLOTS])

                    def columns(t):
                        return t[:, :, :].rearrange("p m (j s) -> p m j s", j=4)

                    slots = iota_slot[:, :].unsqueeze(1).unsqueeze(1).to_broadcast([P, M, 4, SLOTS])
                    dve.tensor_tensor(columns(pick[buf]), slots, of_experts(slot), ALU.is_equal).then_inc(pick_ready, 1)
                    dve.wait_ge(pick_ready, picked + 1)
                    dve.tensor_tensor(columns(pickw[buf]), columns(pick[buf]).bitcast(F32), of_experts(comb), ALU.mult).then_inc(pickw_ready, 1)

                def xg_out(g, buf, pb):
                    dve.wait_ge(xg_done, 4 * g + 2 * pb + 2)
                    for j in range(2):
                        k = 4 * pb + 2 + j
                        ins = dve.tensor_scalar(xgT[buf][:, k, :], bank[1][:, j * 256:(j + 1) * 256], A2[:, k:k + 1],
                                                modT[:, 24 + k:25 + k], ALU.mult, ALU.add)
                    ins.then_inc(xgT_dve, 1)

                def scatter_out(s):
                    for n in range(4):
                        dve.wait_ge(sc_done, 4 * s + n + 1)
                        av = x1[:, n // 2, (n % 2) * 512:(n % 2) * 512 + 512]
                        dve.tensor_tensor(av, bank[6 + n % 2][:, :], av, ALU.add).then_inc(sc_drained, 1)

                def rounds(r, late=False):
                    if late:
                        dve.wait_ge(pick_ready, r * (QUADS + 1))
                        dve.tensor_scalar_add(slot[:, :, :], slot[:, :, :], float(-SLOTS)).then_inc(slots_moved, 1)
                        dve.wait_ge(slots_moved, r)
                        dve.wait_ge(xg_done, 4 * r * (QUADS + 1))
                        dve.wait_ge(put_done, r * (EXPERTS // 2))
                        zero_rows(dve)
                        picks(0, 0, r * (QUADS + 1))
                    for pb in range(2):
                        xg_out(r * (QUADS + 1), 0, pb)
                    with dve.Fori(0, QUADS // 2) as it:
                        for b in range(4):
                            pair = r * (EXPERTS // 2) + it * 4 + b
                            q, pb = b // 2, b % 2
                            if pb == 0:
                                picks(it * 8 + 4 * q + 4, 1 - q, r * (QUADS + 1) + it * 2 + q + 1)
                            dve.wait_ge(tanh_g, pair + 1)
                            dve.scalar_tensor_tensor(sig[:, :], thg[:, :], 1.0, bank[2 + pb][:, 0:FF], ALU.add, ALU.mult).then_inc(silu_ready, 1)
                            dve.wait_ge(silu_ready, pair + 1)
                            dve.tensor_tensor(act_rows[:, :], bank[2 + pb][:, FF:2 * FF], sig[:, :], ALU.mult).then_inc(a_ready, 1)
                            dve.wait_ge(put_done, pair + 1)
                            other = bank[3 - pb]
                            dve.tensor_copy(putT[pb][:, :], other[:, 0:M * P])
                            dve.tensor_copy(yw[pb][:, :], other[:, M * P:M * P + 1]).then_inc(put_ready, 1)
                            dve.wait_ge(sc_drained, 4 * (pair + r) + 4)
                            scatter_out(pair + r)
                            dve.wait_ge(turned, pair + 1)
                            dve.tensor_copy(aT[:, :, :], bank[2 + pb][:, 0:FF].rearrange("p (t n) -> p t n", t=2)).then_inc(aT_ready, 1)
                            xg_out(r * (QUADS + 1) + it * 2 + q + 1, 1 - q, pb)
                            dve.wait_ge(put_ready, pair + 2)
                            dve.wait_ge(sc_drained, 4 * (pair + r) + 8)
                            for n in range(2):
                                s = slice(n * 512, n * 512 + 512)
                                dve.wait_ge((down_half, down_done)[n], pair + 1)
                                dve.scalar_tensor_tensor(y[:, s], bank[4 + n][:, :], yw[pb][:, 0:1], gt2bc[:, s],
                                                         ALU.mult, ALU.mult).then_inc(y_ready, 1)
                            for n in range(2):
                                s = slice(n * 512, n * 512 + 512)
                                dve.wait_ge(yhi_ready, 2 * pair + n + 1)
                                dve.tensor_tensor(ylo[:, s], y[:, s], yhi[:, s].bitcast(F32), ALU.subtract).then_inc(ylo_ready, 1)
                    last = (r + 1) * (EXPERTS // 2) + r
                    dve.wait_ge(sc_drained, 4 * last + 4)
                    scatter_out(last)

                picks(0, 0, 0)
                dve.memset(aT[:, :, :], 0.0).then_inc(aT_ready, 1)
                dve.memset(yw[1][:, :], 0.0).then_inc(put_ready, 1)
                dve.memset(putT[1][:, :].bitcast(F32), 0.0).then_inc(sc_drained, 4)
                dve.wait_ge(sc_drained, 4)
                dve.wait_ge(aT_ready, 1)
                dve.wait_ge(put_ready, 1)
                dve.wait_ge(most_ready, 1)
                count = dve.value_load(mosti[0:1, 0:1], min_val=0, max_val=S)
                rounds(0)
                with dve.If(count > SLOTS):
                    with dve.Fori(1, ROUNDS) as r:
                        with dve.If(count > r * SLOTS):
                            rounds(r, late=True)

                dve.drain()
                dve.memset(tiny[:, 60:61], 0.0).then_inc(result, 1)
                dve.wait_ge(gf_in, 16)
                for m in range(M):
                    dve.tensor_tensor(x1n[:, m, :], x1[:, m, :], gfbc[:, :], ALU.mult).then_inc(scaled, 1)
                mean_square(5, tiny[:, 6:6 + M], D)
                dve.wait_ge(rms_ready, 4)
                dve.wait_ge(scaled, 1)
                dve.tensor_scalar(x1n[:, 0, :], x1n[:, 0, :], tiny[:, 6:7], None, ALU.mult).then_inc(result, 1)

            @block.tensor
            def _(pe):
                def begin(name):
                    n = INDEX[name]
                    if n >= 8:
                        drained(pe, ORDER[n - 8][0])
                    return bank_of(name)

                def done(ins):
                    ins.then_inc(product_done, 1)

                pe.wait_ge(rows_in, 16 * 5)
                pe.wait_ge(more_rows_in, 16 * 2)
                pe.wait_ge(consts, ALL_CONSTS)
                b = begin("rows")
                done(pe.transpose(b[:, 0:R_END], rows[0:R_END, :], ident[0:R_END, 0:R_END]))

                def ada(n, apart=False):
                    b = begin(f"ada{n}")
                    steps = [(q, k) for q in range(4) for k in range(KD)] if apart else [(q, k) for k in range(KD) for q in range(4)]
                    for q, k in steps:
                        if k == 0:
                            arrived(pe, "ada", 4 * n + q)
                        w = chunk("ada", 4 * n + q).rearrange("p (k n) -> p k n", k=KD)
                        ins = pe.matmul(b[32 * q:32 * q + 32, 0:CH], condB[:, k, :], w[:, k, :], start=(k == 0),
                                        stop=(k == KD - 1), tile_position=(0, 32 * q))
                    done(ins)

                def adt(n):
                    b = begin(f"adt{n}")
                    drained(pe, f"ada{n}")
                    for t in range(2):
                        ins = pe.transpose(b[:, t * P:(t + 1) * P], adaR[n % 2][:, t * P:(t + 1) * P], ident[:, :])
                    done(ins)

                def turn_x(name, n, src):
                    b = begin(name)
                    for kk in range(2):
                        for m in range(M):
                            k = 2 * n + kk
                            ins = pe.transpose(b[:, kk * S + m * P:kk * S + m * P + P], src[:, m, k * P:(k + 1) * P], ident[:, :])
                    done(ins)

                CROSS = ((0, 0), (0, 1), (1, 0))

                def cross(dst, stationary, moving, wait=None):
                    for k in range(KD):
                        if wait:
                            wait(k)
                        for j, (u, v) in enumerate(CROSS):
                            ins = pe.matmul(dst, stationary(k)[u], moving(k)[v], start=(k == 0 and j == 0),
                                            stop=(k == KD - 1 and j == 2))
                    return ins

                def win(n):
                    lo, hi = WINC[n]
                    wd = hi - lo
                    b = begin(f"win{n}")
                    if n > 0:
                        split_ready(pe, "win", n)
                    w = [v[:, 0:KD * wd].rearrange("p (k n) -> p k n", k=KD) for v in split_part("win", n)]
                    for m in range(M):
                        def tile_ready(k):
                            pe.wait_ge(h_lo, k // 2 + 1)
                            if k == 0:
                                pe.wait_ge(first_lo, 1)
                            elif k == KD // 2:
                                split_ready(pe, "win", 0)

                        ins = cross(b[:, m * wd:(m + 1) * wd], lambda k: [v[:, k, m * P:(m + 1) * P] for v in (hThi, hTlo)],
                                    lambda k: [v[:, k, :] for v in w], tile_ready if n + m == 0 else None)
                    done(ins)

                def mg(n):
                    b = begin(f"mg{n}")
                    split_ready(pe, "mg", n)
                    w = [v.rearrange("p (k n) -> p k n", k=KD) for v in split_part("mg", n)]
                    for t in range(2):
                        ins = cross(b[:, t * S:(t + 1) * S], lambda k: [v[:, k, t * P:(t + 1) * P] for v in w],
                                    lambda k: [v[:, k, :] for v in (hThi, hTlo)])
                    done(ins)

                def turn_cols(name, tiles):
                    b = begin(name)
                    for t, tile in enumerate(tiles):
                        for m in range(M):
                            ins = pe.transpose(b[:, t * S + m * P:t * S + m * P + P], tile(m), ident[:, :])
                    done(ins)

                pe.wait_ge(cond_ready, 1)
                ada(0, apart=True)
                pe.wait_ge(xn_ready, 2)
                for n in range(4):
                    turn_x(f"xT{n}", n, xs)
                ada(1, apart=True)
                adt(0)
                adt(1)
                for n in range(len(WINC)):
                    win(n)
                mg(0)
                pe.wait_ge(kvn_ready, 2)
                b = begin("kvT")
                for m in range(M):
                    ins = pe.transpose(b[:, m * P:(m + 1) * P], kvn[:, m, :], ident[:, :])
                done(ins)
                mg(1)
                drained(pe, "kvT")
                pe.wait_ge(kv_w_in, 16)
                for n in range(4):
                    m, half = n // 2, n % 2
                    b = begin(f"kvp{n}")
                    done(pe.matmul(b[:, :], kvnT[:, m * P:(m + 1) * P], w_kv[:, half * 512:half * 512 + 512], start=True, stop=True))
                pe.wait_ge(roped, 1)
                turn_cols("iqT", [lambda m, t=t: xp[:, m, IQ + t * P:IQ + (t + 1) * P] for t in range(2)])
                turn_cols("ikT", [lambda m: kdup[:, m, 4, :]])
                b = begin("cmpx")
                for n, col in enumerate((KC, VC)):
                    for gi in range(GROUPS):
                        for par in range(2):
                            for m in range(M):
                                at = (n * GROUPS + gi) * P + m * HD
                                ins = pe.matmul(b[par * HD:(par + 1) * HD, at:at + HD], xp[:, m, col + gi * HD:col + (gi + 1) * HD],
                                                ident[:, par:P:2], start=True, stop=True)
                done(ins)
                for n in range(2):
                    turn_cols(f"qbT{n}", [lambda m, t=t: xp[:, m, QB + t * P:QB + (t + 1) * P] for t in (2 * n, 2 * n + 1)])
                turn_cols("ksT", [lambda m, gi=gi: kdup[:, m, gi, :] for gi in range(2)])
                turn_cols("kwT", [lambda m, gi=gi: kdup[:, m, 2 + gi, :] for gi in range(2)])
                mg(2)
                drained(pe, "ikT")
                for m in range(M):
                    nk = P * (m + 1)
                    banks = [begin(f"il{4 * m + r}") for r in range(4)]
                    for t in range(2):
                        for r in range(4):
                            rr = slice(r * IDX_DIM, (r + 1) * IDX_DIM)
                            ins = pe.matmul(banks[r][:, t * nk:(t + 1) * nk], iqT[rr, t, m * P:(m + 1) * P], ikT[rr, 0:nk],
                                            start=True, stop=True, tile_position=(r * IDX_DIM, 0))
                            if t == 1:
                                done(ins)
                pe.wait_ge(flat_ready, 1)
                b = begin("cmp1")
                for j in range(CMP_TILES):
                    for n, kind in enumerate(("cmp1k", "cmp1v")):
                        if j % KD == 0:
                            arrived(pe, kind, j // KD)
                        w = chunk(kind, j // KD).rearrange("p (k n) -> p k n", k=KD)
                        ins = pe.matmul(b[n * HD:n * HD + GROUPS * NCMP, 0:CMP_HIDDEN], flat[:, n, j, :], w[:, j % KD, :],
                                        start=(j == 0), stop=(j == CMP_TILES - 1), tile_position=(0, n * HD))
                done(ins)
                mg(3)
                b = begin("cmpT")
                drained(pe, "cmp1")
                for t in range(2):
                    ins = pe.transpose(b[:, t * 96:(t + 1) * 96], hid[0:96, t * P:(t + 1) * P], ident[0:96, 0:96])
                done(ins)
                b = begin("cmp2")
                drained(pe, "cmpT")
                pe.wait_ge(cmp_w_in, 32)
                for par in range(2):
                    for t in range(2):
                        pe.matmul(b[par * HD:(par + 1) * HD, 0:GROUPS * NCMP], w2[:, 0, t, :], hidT[:, t, 0:GROUPS * NCMP], start=(t == 0), stop=(t == 1))
                for gi in range(GROUPS):
                    for t in range(2):
                        ins = pe.matmul(b[0:NCMP, 64 + gi * HD:64 + (gi + 1) * HD], hidT[:, t, HD + gi * NCMP:HD + (gi + 1) * NCMP],
                                        w2[:, 1, t, :], start=(t == 0), stop=(t == 1))
                done(ins)

                def scores(u):
                    kind, m = UNITS[u]
                    nk = P * (m + 1)
                    per = PAIRS // (m + 1)
                    for blk in range(m + 1):
                        banks = [begin(f"S{kind}{m}_{2 * blk + par}") for par in range(2)]
                        for j in range(per):
                            for par in range(2):
                                i = blk * per + j
                                g = (2 * i + par) // (HEADS // GROUPS)
                                r = slice(par * HD, (par + 1) * HD)
                                q = (qaT if kind == "dsa" else qbT)[r, i, m * P:(m + 1) * P]
                                k = kaT[r, i, 0:nk] if kind == "dsa" else (ksT if kind == "sel" else kwT)[r, g, 0:nk]
                                ins = pe.matmul(banks[par][:, j * nk:(j + 1) * nk], q, k, start=True, stop=True, tile_position=(par * HD, 0))
                                if j == per - 1:
                                    done(ins)

                def turns(u):
                    kind, m = UNITS[u]
                    pe.wait_ge(unit_probs, u + 1)
                    for n in range(2 * (m + 1)):
                        b = begin(f"T{kind}{m}_{n}")
                        for j in range(4):
                            at = 4 * n + j
                            hs, kb = at // (m + 1), at % (m + 1)
                            ins = pe.transpose(b[:, j * P:(j + 1) * P], probs[u % 2][:, hs, kb * P:(kb + 1) * P], ident[:, :])
                        done(ins)

                def last_turn(u):
                    return f"T{UNITS[u][0]}{UNITS[u][1]}_{2 * UNITS[u][1] + 1}"

                def pv_b(m):
                    drained(pe, last_turn(2 * m + 1))
                    drained(pe, "pcT3")
                    b = begin(f"PVb{m}")
                    for i in range(PAIRS):
                        terms = []
                        for par in range(2):
                            hs, g = par * PAIRS + i, (2 * i + par) // (HEADS // GROUPS)
                            terms.append([(vcs[0:NCMP, g, :], pcT[0:NCMP, m * HEADS + hs, :])]
                                         + [(xp[:, kb, col + g * HD:col + (g + 1) * HD], pT[buf][:, hs * (m + 1) + kb, :])
                                            for buf, col in ((0, VS), (1, VW)) for kb in range(m + 1)])
                        for n in range(len(terms[0])):
                            for par in range(2):
                                v, p = terms[par][n]
                                ins = pe.matmul(b[par * HD:(par + 1) * HD, i * P:(i + 1) * P], v, p, start=(n == 0),
                                                stop=(n == len(terms[0]) - 1))
                    done(ins)

                def pv_a(m):
                    drained(pe, last_turn(4 + m))
                    b = begin(f"PVa{m}")
                    for i in range(PAIRS):
                        for kb in range(m + 1):
                            for par in range(2):
                                hs, h = par * PAIRS + i, 2 * i + par
                                v = kvx[:, kb, HEADS * HD + h * HD:HEADS * HD + (h + 1) * HD]
                                ins = pe.matmul(b[par * HD:(par + 1) * HD, i * P:(i + 1) * P], v, pT[m][:, hs * (m + 1) + kb, :],
                                                start=(kb == 0), stop=(kb == m))
                    done(ins)

                drained(pe, "kwT")
                scores(0)
                scores(1)
                drained(pe, "cmp2")
                for par in range(2):
                    b = begin(f"sc{par}")
                    r = slice(par * HD, (par + 1) * HD)
                    for m in range(M):
                        for i in range(PAIRS):
                            g = (2 * i + par) // (HEADS // GROUPS)
                            at = (m * PAIRS + i) * NCMP
                            ins = pe.matmul(b[:, at:at + NCMP], qbT[r, i, m * P:(m + 1) * P], kcT[r, g * NCMP:(g + 1) * NCMP], start=True, stop=True,
                                            tile_position=(par * HD, 0))
                    done(ins)
                mg(4)
                pe.wait_ge(cmp_probs, 1)
                for n in range(4):
                    b = begin(f"pcT{n}")
                    for j in range(4):
                        at = 4 * n + j
                        ins = pe.transpose(b[0:NCMP, j * P:(j + 1) * P], smc[:, at // HEADS, at % HEADS, :], ident[:, :])
                    done(ins)
                pe.wait_ge(roped, 2)
                for n in range(2):
                    turn_cols(f"qaT{n}", [lambda m, t=t: xp[:, m, QA + t * P:QA + (t + 1) * P] for t in (2 * n, 2 * n + 1)])
                mg(5)
                ada(2)
                for n in range(2):
                    turn_cols(f"kaT{n}", [lambda m, t=t: kvx[:, m, t * P:(t + 1) * P] for t in (2 * n, 2 * n + 1)])
                adt(2)
                turns(0)
                scores(2)
                turns(1)
                scores(3)
                mg(6)
                mg(7)
                ada(3)
                adt(3)
                pv_b(0)
                turns(2)
                drained(pe, "kaT1")
                scores(4)
                ada(4)
                turns(3)
                pv_b(1)
                adt(4)
                scores(5)
                ada(5)
                turns(4)
                adt(5)
                pv_a(0)
                turns(5)
                pv_a(1)
                pe.wait_ge(diag_ready, 1)
                for n in range(2):
                    b = begin(f"gb{n}")
                    done(pe.matmul(b[:, :], ones[:, :], diag[:, n * 512:n * 512 + 512], start=True, stop=True))
                drained(pe, "PVa1")
                pe.wait_ge(ob_lo, 1)
                for t in range(KD):
                    if t == 2:
                        pe.wait_ge(shift_ready, 1)
                        b = begin("rsh")
                        done(pe.matmul(b[:, 0:36], ones[:, :], wshs[:, :], start=True, stop=True))
                    b = begin(f"up{t}")
                    for n, (kind, o) in enumerate((("upa", (oahi, oalo)), ("upb", (obhi, oblo)))):
                        if t % 4 == 0:
                            split_ready(pe, kind, t // 4)
                        w = [v.rearrange("p (k n) -> p k n", k=PAIRS) for v in split_part(kind, t // 4)]
                        for i in range(PAIRS):
                            for j, (u, v) in enumerate(CROSS):
                                ins = pe.matmul(b[:, n * S:(n + 1) * S], w[u][:, i, (t % 4) * P:(t % 4) * P + P], o[v][:, i, :],
                                                start=(i == 0 and j == 0), stop=(i == PAIRS - 1 and j == 2))
                    done(ins)
                for n in range(4):
                    b = begin(f"out{n}")
                    split_ready(pe, "out", n)
                    w = [v.rearrange("p (k n) -> p k n", k=KD) for v in split_part("out", n)]
                    for m in range(M):
                        ins = cross(b[:, m * CH:(m + 1) * CH], lambda k: [v[:, k, m * P:(m + 1) * P] for v in (mThi, mTlo)],
                                    lambda k: [v[:, k, :] for v in w], (lambda k: pe.wait_ge(mT_lo, k + 1)) if n + m == 0 else None)
                    done(ins)
                    if n < 2:
                        pe.wait_ge(diag_ready, 2)
                        b = begin(f"gb{n + 2}")
                        done(pe.matmul(b[:, :], ones[:, :], diag2[:, n * 512:n * 512 + 512], start=True, stop=True))
                    if n > 0:
                        drained(pe, f"out{n - 1}")
                        turn_x(f"x1T{n - 1}", n - 1, x1)

                def router(m, ks):
                    for k in ks:
                        ins = pe.matmul(banks[m][:, 0:36], x1T[:, k, m * P:(m + 1) * P], wr[:, k, :], start=(k == 0), stop=(k == KD - 1))
                    return ins

                banks = [begin("rt0"), begin("rt1")]
                drained(pe, "x1T1")
                for m in range(M):
                    router(m, range(3))
                drained(pe, "out3")
                turn_x("x1T3", 3, x1)
                drained(pe, "x1T2")
                for m in range(M):
                    router(m, range(3, 6))
                drained(pe, "x1T3")
                for m in range(M):
                    done(router(m, range(6, KD)))
                def stay_warm(times):
                    for _ in range(times):
                        pe.matmul(bank[7][:, :], ident[:, :], gt2bc[:, 0:512], start=True, stop=True)

                drained(pe, "gb2")
                stay_warm(4)
                pe.wait_ge(sel_ready, 1)
                b = begin("pos")
                E = EXPERTS
                pe.matmul(b[:, 0:2 * E].rearrange("p (m n) -> p m n", m=M), tri[:, :], sel[:, :, 0:E], start=True, stop=False)
                pe.matmul(b[:, E:2 * E], ones[:, :], sel[:, 0, 0:E], start=False, stop=True)
                pe.matmul(b[:, 2 * E:3 * E], ones[:, :], sel[:, 0, 0:E], start=True, stop=False)
                done(pe.matmul(b[:, 2 * E:3 * E], ones[:, :], sel[:, 1, 0:E], start=False, stop=True))

                def gather(g, buf, step, first=False):
                    half = step % 2
                    pe.wait_ge(pick_ready, g + 1)
                    if not (first and step < 2):
                        pe.wait_ge((xgT_act, xgT_dve)[half], 2 * g + step // 2)
                    for j in range(2):
                        k = 2 * step + j
                        for n, (src, m) in enumerate(((s, m) for s in (x1hi, x1lo) for m in range(M))):
                            ins = pe.matmul(bank[half][:, j * 256:(j + 1) * 256], src[:, m, k * P:(k + 1) * P],
                                            pick[buf][:, m, :], start=(n == 0), stop=(n == 3))
                    ins.then_inc(xg_done, 1)

                def gate_up(its, q, b, g):
                    for j in range(2):
                        for piece in range(2):
                            pe.wait_ge(mlanded[slot_number(b, j, piece)], 16 * landings(b, j, piece, its))
                    for k in range(KD):
                        if b % 2 == 0 and k % 2 == 0:
                            pe.wait_ge((xgT_act, xgT_dve)[k // 2 % 2], 2 * g + 1 + k // 4)
                        for j in range(2):
                            ins = pe.matmul(bank[2 + b % 2][j * SLOTS:(j + 1) * SLOTS, :],
                                            xgT[q][:, k, (2 * (b % 2) + j) * SLOTS:(2 * (b % 2) + j + 1) * SLOTS],
                                            gate_up_weights(b, j, k), start=(k == 0), stop=(k == KD - 1))
                    ins.then_inc(gu_done, 1)

                def down(its, b):
                    for j in range(2):
                        pe.wait_ge(mlanded[slot_number(b, j, 2)], 16 * landings(b, j, 2, its))
                    for n in range(2):
                        for t in range(2):
                            for j in range(2):
                                w = mslot(slot_number(b, j, 2)).rearrange("p (k n) -> p k n", k=2)
                                ins = pe.matmul(bank[4 + n][j * SLOTS:(j + 1) * SLOTS, :], aT[:, t, j * SLOTS:(j + 1) * SLOTS],
                                                w[:, t, n * 512:n * 512 + 512], start=(t == 0), stop=(t == 1))
                        ins.then_inc((down_half, down_done)[n], 1)

                def scatter(s, b, m):
                    for half in range(2):
                        n = 2 * m + half
                        if m == 0:
                            pe.wait_ge(ylo_ready, 2 * s + half + 1)
                        pe.wait_ge(sc_drained, 4 * s + 3 + n)
                        for q, y in enumerate((yhi, ylo)):
                            ins = pe.matmul(bank[6 + n % 2][:, :], putT[b][:, m * P:(m + 1) * P],
                                            y[:, half * 512:half * 512 + 512], start=(q == 0), stop=(q == 1))
                        ins.then_inc(sc_done, 1)

                def rounds(r, late=False):
                    for step in range(4):
                        gather(r * (QUADS + 1), 0, step, first=not late)
                    with pe.Fori(0, QUADS // 2) as it:
                        for b in range(4):
                            q, pb = b // 2, b % 2
                            pair = r * (EXPERTS // 2) + it * 4 + b
                            g = r * (QUADS + 1) + it * 2 + q
                            its = r * (QUADS // 2) + it
                            pe.wait_ge(put_ready, pair + 1)
                            gate_up(its, q, b, g)
                            pe.wait_ge(aT_ready, pair + 1)
                            other = bank[3 - pb]
                            half = slice(pb * P, (pb + 1) * P)
                            for m in range(M):
                                pe.transpose(other[:, m * P:(m + 1) * P], pick[q][:, m, half].bitcast(F32), ident[:, :])
                            if pb == 0:
                                pe.wait_ge(pickw_ready, g + 1)
                            for m in range(M):
                                ins = pe.matmul(other[:, M * P:M * P + 1], pickw[q][:, m, half], ones[:, 0:1], start=(m == 0), stop=(m == M - 1))
                            ins.then_inc(put_done, 1)
                            scatter(pair + r, 1 - pb, 0)
                            gather(g + 1, 1 - q, 2 * pb)
                            scatter(pair + r, 1 - pb, 1)
                            pe.wait_ge(a_ready, pair + 1)
                            for t in range(2):
                                ins = pe.transpose(bank[2 + pb][:, t * P:(t + 1) * P], act_rows[:, t * P:(t + 1) * P], ident[:, :])
                            ins.then_inc(turned, 1)
                            gather(g + 1, 1 - q, 2 * pb + 1)
                            pe.wait_ge(aT_ready, pair + 2)
                            down(its, b)
                    for m in range(M):
                        scatter((r + 1) * (EXPERTS // 2) + r, 1, m)

                stay_warm(2)
                drained(pe, "pos")
                pe.wait_ge(hi_ready, 1)
                pe.wait_ge(lo_ready, 1)
                pe.wait_ge(most_ready, 1)
                count = pe.value_load(mosti[0:1, 0:1], min_val=0, max_val=S)
                rounds(0)
                with pe.If(count > SLOTS):
                    with pe.Fori(1, ROUNDS) as r:
                        with pe.If(count > r * SLOTS):
                            rounds(r, late=True)


def overlap(src):
    v = src[:, 0:CMP_TILES].unsqueeze(2).to_broadcast([P, CMP_TILES, NCMP]).copy()
    ap = [list(d) for d in v.ap]
    ap[-1][0] = CMP_STRIDE // 2
    return bass.AP(tensor=v.tensor, offset=v.offset, ap=ap)


_INS = ["x", "c", "positions", "w_ada", "b_ada", "g_norm1", "w_in", "g_kv_latent", "w_kv_up", "pe_cmp_k", "pe_cmp_v",
        "w_cmp1_k", "w_cmp2_k", "w_cmp1_v", "w_cmp2_v", "w_up_a", "w_up_b", "w_out", "g_norm2", "w_router_group",
        "b_router_group", "w_router_expert", "b_router_expert", "w_expert_gate", "w_expert_up", "w_expert_down", "g_final"]
_STRIP = {"w_ada", "w_in", "w_cmp1_k", "w_cmp1_v", "w_up_a", "w_up_b", "w_out", "w_expert_gate", "w_expert_up", "w_expert_down"}


def kernel(**inputs):
    import concourse.bacc as bacc
    from concourse.bass_utils import run_bass_kernel_spmd

    nc = bacc.Bacc("TRN2", target_bir_lowering=False, num_devices=1)
    arrays, args = {}, {}
    for name in _INS:
        v = np.ascontiguousarray(inputs[name])
        arrays[f"in_{name}_dram"] = v
        ap = nc.dram_tensor(f"in_{name}_dram", v.shape, mybir.dt.from_np(v.dtype), kind="ExternalInput").ap()
        args[name] = ap[0] if name in _STRIP else ap
    out = nc.dram_tensor("out_0_dram", (1, S, D), F32, kind="ExternalOutput").ap()
    layer_kernel(nc, **args, out=out)
    r = run_bass_kernel_spmd(nc, [arrays], core_ids=[0])
    return r.results[0]["out_0_dram"]
```
